# Optimizing a Trainium2 kernel written in Bass

```python
import math
import jax, jax.numpy as jnp
from jax import lax
import numpy as np

D_MODEL = 1024
BATCH = 1
SEQ = 256
DEPTH = 2

N_MIXERS = 2
N_HGRN_LAYERS = (DEPTH + 1) // 2
N_DSA_LAYERS = DEPTH // 2

HGRN_EXPAND = 128
HGRN_HEADS = D_MODEL // HGRN_EXPAND
HGRN_DK = HGRN_EXPAND
HGRN_DV = D_MODEL // HGRN_HEADS
HGRN_CHUNK = 32

ATT_HEADS = 16
ATT_HEAD_DIM = D_MODEL // ATT_HEADS
ATT_KV_HEADS = 2
ATT_GROUP = ATT_HEADS // ATT_KV_HEADS
IDX_HEADS = 8
IDX_HEAD_DIM = 64
TOPK_MAX = 256
Q_BLOCK = 128
DSA_SPLITS = (ATT_HEADS * ATT_HEAD_DIM, ATT_KV_HEADS * ATT_HEAD_DIM, ATT_KV_HEADS * ATT_HEAD_DIM,
              IDX_HEADS * IDX_HEAD_DIM, IDX_HEAD_DIM, IDX_HEADS)
DSA_IN_WIDTH = sum(DSA_SPLITS)

REL_BUCKETS = 32
REL_MAX_DIST = 128

D_FF = 2816
CONV_WIDTH = 3

EPS = 1e-6
NEG_BIG = -1e30
TINY = 1e-30


def rms_norm(x, gain):
    xf = x.astype(jnp.float32)
    y = xf * lax.rsqrt(jnp.mean(xf * xf, axis=-1, keepdims=True) + EPS)
    return (y * gain.astype(jnp.float32)).astype(x.dtype)

def hgrn2_mixer(x, w_in, w_out, gate_norm, lower_bound):
    B, L, _ = x.shape
    n_chunks = L // HGRN_CHUNK
    proj = x @ w_in
    q, f, i, g = jnp.split(proj, 4, axis=-1)
    f32 = f.astype(jnp.float32)
    lb = lower_bound.astype(jnp.float32)
    forget = lb + (1.0 - lb) * jax.nn.sigmoid(f32)
    log_f = jnp.log(jnp.maximum(forget, TINY))
    k = (1.0 - lb) * jax.nn.sigmoid(-f32)

    def to_chunks(t, d):
        t = t.astype(jnp.float32).reshape(B, n_chunks, HGRN_CHUNK, HGRN_HEADS, d)
        return t.transpose(1, 0, 3, 2, 4)

    qc, kc, ic, gc = to_chunks(q, HGRN_DK), to_chunks(k, HGRN_DK), to_chunks(i, HGRN_DV), to_chunks(log_f, HGRN_DK)
    causal = jnp.tril(jnp.ones((HGRN_CHUNK, HGRN_CHUNK), dtype=bool))[None, None, :, :, None]

    def step(S, inp):
        qb, kb, ib, gb = inp
        b = jnp.cumsum(gb, axis=2)
        diff = b[:, :, :, None, :] - b[:, :, None, :, :]
        decay = jnp.where(causal, jnp.exp(jnp.where(causal, diff, 0.0)), 0.0)
        scores = jnp.einsum('bhtd,bhsd,bhtsd->bhts', qb, kb, decay)
        o = jnp.einsum('bhts,bhsv->bhtv', scores, ib) + jnp.einsum('bhtd,bhdv->bhtv', qb * jnp.exp(b), S)
        b_last = b[:, :, -1:, :]
        S_new = jnp.exp(b_last[:, :, 0, :])[..., None] * S + jnp.einsum('bhsd,bhsv->bhdv', kb * jnp.exp(b_last - b), ib)
        return S_new, o

    S0 = jnp.zeros((B, HGRN_HEADS, HGRN_DK, HGRN_DV), jnp.float32)
    _, o = lax.scan(step, S0, (qc, kc, ic, gc))
    o = o.transpose(1, 0, 3, 2, 4).reshape(B, L, HGRN_HEADS, HGRN_DV)
    o = o * lax.rsqrt(jnp.mean(o * o, axis=-1, keepdims=True) + EPS) * gate_norm.astype(jnp.float32)
    o = o * jax.nn.silu(g.astype(jnp.float32)).reshape(B, L, HGRN_HEADS, HGRN_DV)
    return o.reshape(B, L, D_MODEL).astype(x.dtype) @ w_out

def t5_causal_bucket(rel):
    n = jnp.maximum(rel, 0)
    max_exact = REL_BUCKETS // 2
    nf = jnp.maximum(n, max_exact).astype(jnp.float32)
    large = max_exact + (jnp.log(nf / max_exact) / math.log(REL_MAX_DIST / max_exact)
                         * (REL_BUCKETS - max_exact)).astype(jnp.int32)
    large = jnp.minimum(large, REL_BUCKETS - 1)
    return jnp.where(n < max_exact, n, large)

def dsa_mixer(x, w_in, w_out, rel_bias):
    B, L, _ = x.shape
    top_k = min(TOPK_MAX, L // 4)
    n_blocks = L // Q_BLOCK
    proj = x @ w_in
    cuts = np.cumsum(DSA_SPLITS)[:-1].tolist()
    q, k, v, q_idx, k_idx, w_idx = jnp.split(proj, cuts, axis=-1)
    q = q.reshape(B, L, ATT_KV_HEADS, ATT_GROUP, ATT_HEAD_DIM)
    q_idx = q_idx.reshape(B, L, IDX_HEADS, IDX_HEAD_DIM)
    w_idx = w_idx * (IDX_HEADS ** -0.5 * IDX_HEAD_DIM ** -0.5)

    def blockify(t):
        return jnp.moveaxis(t.reshape(B, n_blocks, Q_BLOCK, *t.shape[2:]), 1, 0)

    key_pos = jnp.arange(L, dtype=jnp.int32)
    starts = jnp.arange(n_blocks, dtype=jnp.int32) * Q_BLOCK

    def one_block(args):
        qb, qib, wb, start = args
        q_pos = start + jnp.arange(Q_BLOCK, dtype=jnp.int32)
        dots = jnp.einsum('bthd,bsd->bths', qib, k_idx).astype(jnp.float32)
        scores = jnp.einsum('bths,bth->bts', jax.nn.relu(dots), wb.astype(jnp.float32))
        admissible = key_pos[None, :] <= q_pos[:, None]
        scores = jnp.where(admissible[None], scores, NEG_BIG)
        _, sel = lax.top_k(scores, top_k)
        k_sel = jax.vmap(lambda kk, ii: kk[ii])(k, sel).reshape(B, Q_BLOCK, top_k, ATT_KV_HEADS, ATT_HEAD_DIM)
        v_sel = jax.vmap(lambda vv, ii: vv[ii])(v, sel).reshape(B, Q_BLOCK, top_k, ATT_KV_HEADS, ATT_HEAD_DIM)
        logits = jnp.einsum('btkgd,btskd->btkgs', qb, k_sel).astype(jnp.float32) * (ATT_HEAD_DIM ** -0.5)
        rel = q_pos[None, :, None] - sel
        bias = rel_bias.astype(jnp.float32)[t5_causal_bucket(rel)]
        bias = bias.reshape(B, Q_BLOCK, top_k, ATT_KV_HEADS, ATT_GROUP).transpose(0, 1, 3, 4, 2)
        valid = (rel >= 0)[:, :, None, None, :]
        logits = jnp.where(valid, logits + bias, NEG_BIG)
        probs = jax.nn.softmax(logits, axis=-1)
        out = jnp.einsum('btkgs,btskd->btkgd', probs, v_sel.astype(jnp.float32))
        return out.reshape(B, Q_BLOCK, D_MODEL).astype(x.dtype)

    out = lax.map(one_block, (blockify(q), blockify(q_idx), blockify(w_idx), starts))
    out = jnp.moveaxis(out, 0, 1).reshape(B, L, D_MODEL)
    return out @ w_out

def conv_ffn(x, w_up, conv_w, conv_b, w_down):
    h = x @ w_up
    C = h.shape[-1]
    h = lax.conv_general_dilated(h, conv_w[:, None, :].astype(h.dtype), window_strides=(1,),
                                 padding=[(CONV_WIDTH - 1, 0)],
                                 dimension_numbers=('NWC', 'WIO', 'NWC'),
                                 feature_group_count=C) + conv_b
    gate, up = jnp.split(h, 2, axis=-1)
    return (jax.nn.silu(gate) * up) @ w_down

def first_inputs(seed: int = 0) -> dict:
    key = jax.random.key(seed)
    ks = jax.random.split(key, 16)
    D = D_MODEL

    def dense(k, shape, fan_in):
        return jax.random.normal(k, shape, jnp.float32) * fan_in ** -0.5

    return {
        "x": jax.random.normal(ks[0], (BATCH, SEQ, D), jnp.float32),
        "attn_norm": 1.0 + 0.05 * jax.random.normal(ks[1], (DEPTH, D), jnp.float32),
        "ffn_norm": 1.0 + 0.05 * jax.random.normal(ks[2], (DEPTH, D), jnp.float32),
        "hgrn_w_in": dense(ks[3], (N_HGRN_LAYERS, D, 4 * D), D),
        "hgrn_w_out": dense(ks[4], (N_HGRN_LAYERS, D, D), D),
        "hgrn_gate_norm": 1.0 + 0.05 * jax.random.normal(ks[5], (N_HGRN_LAYERS, HGRN_DV), jnp.float32),
        "hgrn_lower_bounds": 0.1 * jax.random.normal(ks[6], (N_HGRN_LAYERS, D), jnp.float32),
        "dsa_w_in": dense(ks[7], (N_DSA_LAYERS, D, DSA_IN_WIDTH), D),
        "dsa_w_out": dense(ks[8], (N_DSA_LAYERS, D, D), D),
        "rel_bias": 0.1 * jax.random.normal(ks[9], (REL_BUCKETS, ATT_HEADS), jnp.float32),
        "ffn_w_up": dense(ks[10], (DEPTH, D, 2 * D_FF), D),
        "ffn_conv_w": dense(ks[11], (DEPTH, CONV_WIDTH, 2 * D_FF), CONV_WIDTH),
        "ffn_conv_b": 0.01 * jax.random.normal(ks[12], (DEPTH, 2 * D_FF), jnp.float32),
        "ffn_w_down": dense(ks[13], (DEPTH, D_FF, D), D_FF),
        "final_norm": 1.0 + 0.05 * jax.random.normal(ks[14], (D,), jnp.float32),
    }

def first_block(x, attn_norm, ffn_norm, hgrn_w_in, hgrn_w_out, hgrn_gate_norm, hgrn_lower_bounds,
              dsa_w_in, dsa_w_out, rel_bias, ffn_w_up, ffn_conv_w, ffn_conv_b, ffn_w_down, final_norm):
    lb_soft = jax.nn.softmax(hgrn_lower_bounds.astype(jnp.float32), axis=0)
    lower_bounds = jnp.cumsum(lb_soft, axis=0) - lb_soft[0]
    h = x
    for layer in range(DEPTH):
        j = layer // N_MIXERS
        hn = rms_norm(h, attn_norm[layer])
        if layer % N_MIXERS == 0:
            mix = hgrn2_mixer(hn, hgrn_w_in[j], hgrn_w_out[j], hgrn_gate_norm[j], lower_bounds[j])
        else:
            mix = dsa_mixer(hn, dsa_w_in[j], dsa_w_out[j], rel_bias)
        h = h + mix
        h = h + conv_ffn(rms_norm(h, ffn_norm[layer]), ffn_w_up[layer], ffn_conv_w[layer],
                         ffn_conv_b[layer], ffn_w_down[layer])
    return rms_norm(h, final_norm)


N_EVEN = (DEPTH + 1) // 2
N_ODD = DEPTH // 2
N_NORMS = 6

D_FF_2 = ((8 * D_MODEL // 3 + 127) // 128) * 128
FFN_RES = 0.5

SB_HEADS = 8
SB_HEAD_DIM = 64
SB_WIDTH = SB_HEADS * SB_HEAD_DIM
SB_BLOCK = 128

CONV_CH = D_MODEL // 2
CONV_WIDTH_2 = 31

EVEN_IN = 3 * SB_WIDTH + 2 * CONV_CH
EVEN_OUT = SB_WIDTH + CONV_CH

GLA_HEADS = 4
GLA_KEY = D_MODEL // 2
GLA_VAL = D_MODEL
GLA_DK = GLA_KEY // GLA_HEADS
GLA_DV = GLA_VAL // GLA_HEADS
GATE_RANK = 16
GATE_TAU = 16.0
GLA_CHUNK = 64
ODD_IN = 2 * GLA_KEY + 2 * GLA_VAL + GATE_RANK

NORM_EPS = 1e-6


def rms_norm_2(x, g):
    xf = x.astype(jnp.float32)
    y = xf * lax.rsqrt(jnp.mean(xf * xf, axis=-1, keepdims=True) + NORM_EPS)
    return (y * g.astype(jnp.float32)).astype(x.dtype)

def layer_norm(x, g, b):
    xf = x.astype(jnp.float32)
    mu = jnp.mean(xf, axis=-1, keepdims=True)
    var = jnp.mean(jnp.square(xf - mu), axis=-1, keepdims=True)
    y = (xf - mu) * lax.rsqrt(var + NORM_EPS)
    return (y * g.astype(jnp.float32) + b.astype(jnp.float32)).astype(x.dtype)

def swiglu(x, w_in, w_out):
    a, b = jnp.split(x @ w_in, 2, axis=-1)
    return (jax.nn.silu(a) * b) @ w_out

def split_heads(t, n):
    B, S, W = t.shape
    return t.reshape(B, S, n, W // n).transpose(0, 2, 1, 3)

def merge_heads(t):
    B, H, S, d = t.shape
    return t.transpose(0, 2, 1, 3).reshape(B, S, H * d)

def stick_breaking_attention(q, k, v):
    B, H, S, Dh = q.shape
    scale = Dh ** -0.5
    outs = []
    for i in range(S // SB_BLOCK):
        t0, t1 = i * SB_BLOCK, (i + 1) * SB_BLOCK
        qb = q[:, :, t0:t1]
        kb = k[:, :, :t1]
        vb = v[:, :, :t1]
        z = jnp.einsum('bhqd,bhkd->bhqk', qb, kb).astype(jnp.float32) * scale
        mask = jnp.arange(t1)[None, :] < jnp.arange(t0, t1)[:, None]
        log_1m = jnp.where(mask, jax.nn.log_sigmoid(-z), 0.0)
        rest = lax.cumsum(log_1m, axis=3, reverse=True) - log_1m
        w = jnp.where(mask, jnp.exp(jax.nn.log_sigmoid(z) + rest), 0.0)
        outs.append(jnp.einsum('bhqk,bhkd->bhqd', w.astype(vb.dtype), vb))
    return jnp.concatenate(outs, axis=2)

def causal_depthwise_conv(x, w, b):
    K, C = w.shape
    xp = jnp.pad(x, ((0, 0), (K - 1, 0), (0, 0)))
    y = lax.conv_general_dilated(
        xp, w[:, None, :].astype(x.dtype), window_strides=(1,), padding='VALID',
        dimension_numbers=('NWC', 'WIO', 'NWC'), feature_group_count=C)
    return y + b.astype(x.dtype)

def even_mixer(h, w_in, w_out, dw_w, dw_b, ln_g, ln_b):
    proj = h @ w_in
    q, k, v, u, gate = jnp.split(
        proj, [SB_WIDTH, 2 * SB_WIDTH, 3 * SB_WIDTH, 3 * SB_WIDTH + CONV_CH], axis=-1)
    a_out = merge_heads(stick_breaking_attention(
        split_heads(q, SB_HEADS), split_heads(k, SB_HEADS), split_heads(v, SB_HEADS)))
    c = u * jax.nn.sigmoid(gate)
    c = causal_depthwise_conv(c, dw_w, dw_b)
    c = jax.nn.silu(layer_norm(c, ln_g, ln_b))
    return jnp.concatenate([a_out.astype(h.dtype), c], axis=-1) @ w_out

def gla_chunked(q, k, v, g):
    B, H, S, dk = q.shape
    dv = v.shape[-1]
    N = S // GLA_CHUNK

    def to_chunks(t):
        return t.reshape(B, H, N, GLA_CHUNK, t.shape[-1]).transpose(2, 0, 1, 3, 4)

    mask = jnp.tril(jnp.ones((GLA_CHUNK, GLA_CHUNK), dtype=bool))

    def step(state, inp):
        qc, kc, vc, gc = inp
        b = jnp.cumsum(gc, axis=2)
        inter = jnp.einsum('bhtk,bhkv->bhtv', qc * jnp.exp(b), state)
        diff = b[:, :, :, None, :] - b[:, :, None, :, :]
        decay = jnp.exp(jnp.where(mask[:, :, None], diff, -jnp.inf))
        scores = jnp.einsum('bhtk,bhsk,bhtsk->bhts', qc, kc, decay)
        out = inter + jnp.einsum('bhts,bhsv->bhtv', scores, vc)
        b_last = b[:, :, -1, :]
        state = jnp.exp(b_last)[..., None] * state + jnp.einsum(
            'bhsk,bhsv->bhkv', kc * jnp.exp(b_last[:, :, None, :] - b), vc)
        return state, out

    init = jnp.zeros((B, H, dk, dv), jnp.float32)
    _, o = lax.scan(step, init, (to_chunks(q), to_chunks(k), to_chunks(v), to_chunks(g)))
    return o.transpose(1, 2, 0, 3, 4).reshape(B, H, S, dv)

def odd_mixer(h, w_in, w_gate, b_gate, norm_g, w_out):
    proj = h @ w_in
    q, k, v, r, g_lr = jnp.split(
        proj, [GLA_KEY, 2 * GLA_KEY, 2 * GLA_KEY + GLA_VAL, 2 * GLA_KEY + 2 * GLA_VAL], axis=-1)
    g = jax.nn.log_sigmoid((g_lr @ w_gate + b_gate).astype(jnp.float32)) / GATE_TAU
    f32 = jnp.float32
    qh = split_heads(q, GLA_HEADS).astype(f32) * (GLA_DK ** -0.5)
    kh = split_heads(k, GLA_HEADS).astype(f32)
    vh = split_heads(v, GLA_HEADS).astype(f32)
    gh = split_heads(g, GLA_HEADS)
    o = gla_chunked(qh, kh, vh, gh)
    o = merge_heads(rms_norm_2(o, norm_g)).astype(h.dtype)
    return (o * jax.nn.silu(r)) @ w_out

def second_inputs(seed: int = 0) -> dict:
    key = jax.random.key(seed)
    ks = jax.random.split(key, 20)
    f32 = jnp.float32

    def w(k, shape, fan_in):
        return jax.random.normal(k, shape, f32) * (fan_in ** -0.5)

    return {
        "x": jax.random.normal(ks[0], (BATCH, SEQ, D_MODEL), f32),
        "norm_g": 1.0 + 0.05 * jax.random.normal(ks[1], (DEPTH, N_NORMS, D_MODEL), f32),
        "ffn1_w_in": w(ks[2], (DEPTH, D_MODEL, 2 * D_FF_2), D_MODEL),
        "ffn1_w_out": w(ks[3], (DEPTH, D_FF_2, D_MODEL), D_FF_2),
        "ffn2_w_in": w(ks[4], (DEPTH, D_MODEL, 2 * D_FF_2), D_MODEL),
        "ffn2_w_out": w(ks[5], (DEPTH, D_FF_2, D_MODEL), D_FF_2),
        "hyb_w_in": w(ks[6], (N_EVEN, D_MODEL, EVEN_IN), D_MODEL),
        "hyb_w_out": w(ks[7], (N_EVEN, EVEN_OUT, D_MODEL), EVEN_OUT),
        "conv_dw_w": w(ks[8], (N_EVEN, CONV_WIDTH_2, CONV_CH), CONV_WIDTH_2),
        "conv_dw_b": 0.02 * jax.random.normal(ks[9], (N_EVEN, CONV_CH), f32),
        "conv_ln_g": 1.0 + 0.05 * jax.random.normal(ks[10], (N_EVEN, CONV_CH), f32),
        "conv_ln_b": 0.02 * jax.random.normal(ks[11], (N_EVEN, CONV_CH), f32),
        "gla_w_in": w(ks[12], (N_ODD, D_MODEL, ODD_IN), D_MODEL),
        "gla_w_gate": w(ks[13], (N_ODD, GATE_RANK, GLA_KEY), GATE_RANK),
        "gla_b_gate": 0.02 * jax.random.normal(ks[14], (N_ODD, GLA_KEY), f32),
        "gla_norm_g": 1.0 + 0.05 * jax.random.normal(ks[15], (N_ODD, GLA_DV), f32),
        "gla_w_out": w(ks[16], (N_ODD, GLA_VAL, D_MODEL), GLA_VAL),
    }

def second_block(x, norm_g, ffn1_w_in, ffn1_w_out, ffn2_w_in, ffn2_w_out,
              hyb_w_in, hyb_w_out, conv_dw_w, conv_dw_b, conv_ln_g, conv_ln_b,
              gla_w_in, gla_w_gate, gla_b_gate, gla_norm_g, gla_w_out):
    h = x
    for l in range(DEPTH):
        g = norm_g[l]
        f = swiglu(rms_norm_2(h, g[0]), ffn1_w_in[l], ffn1_w_out[l])
        h = h + FFN_RES * rms_norm_2(f, g[1])
        hn = rms_norm_2(h, g[2])
        if l % 2 == 0:
            e = l // 2
            m = even_mixer(hn, hyb_w_in[e], hyb_w_out[e], conv_dw_w[e], conv_dw_b[e],
                           conv_ln_g[e], conv_ln_b[e])
        else:
            o = l // 2
            m = odd_mixer(hn, gla_w_in[o], gla_w_gate[o], gla_b_gate[o], gla_norm_g[o],
                          gla_w_out[o])
        h = h + rms_norm_2(m, g[3])
        f = swiglu(rms_norm_2(h, g[4]), ffn2_w_in[l], ffn2_w_out[l])
        h = h + FFN_RES * rms_norm_2(f, g[5])
    return h


def setup_inputs(seed=0):
    out = dict(first_inputs(seed))
    for name, value in second_inputs(seed + 1).items():
        if name != "x":
            out[name + "_2"] = value
    return out


def reference(
    x, attn_norm, ffn_norm, hgrn_w_in, hgrn_w_out, hgrn_gate_norm, hgrn_lower_bounds, dsa_w_in,
    dsa_w_out, rel_bias, ffn_w_up, ffn_conv_w, ffn_conv_b, ffn_w_down, final_norm, norm_g_2,
    ffn1_w_in_2, ffn1_w_out_2, ffn2_w_in_2, ffn2_w_out_2, hyb_w_in_2, hyb_w_out_2, conv_dw_w_2,
    conv_dw_b_2, conv_ln_g_2, conv_ln_b_2, gla_w_in_2, gla_w_gate_2, gla_b_gate_2, gla_norm_g_2,
    gla_w_out_2,
):
    x = first_block(
        x, attn_norm, ffn_norm, hgrn_w_in, hgrn_w_out, hgrn_gate_norm, hgrn_lower_bounds,
        dsa_w_in, dsa_w_out, rel_bias, ffn_w_up, ffn_conv_w, ffn_conv_b, ffn_w_down, final_norm,
    )
    return second_block(
        x, norm_g_2, ffn1_w_in_2, ffn1_w_out_2, ffn2_w_in_2, ffn2_w_out_2, hyb_w_in_2,
        hyb_w_out_2, conv_dw_w_2, conv_dw_b_2, conv_ln_g_2, conv_ln_b_2, gla_w_in_2,
        gla_w_gate_2, gla_b_gate_2, gla_norm_g_2, gla_w_out_2,
    )


_drawn_inputs = setup_inputs


def setup_inputs(seed=0):
    import zlib

    import numpy as np

    out = dict(_drawn_inputs(seed))
    spreads = {}
    factors = {'gla_b_gate_2': 8.0}
    for name, (base, spread) in spreads.items():
        noise = np.random.default_rng([zlib.crc32(name.encode()), seed]).standard_normal(out[name].shape)
        drawn = base * np.exp(spread * noise) if base else spread * noise
        out[name] = __import__('jax').numpy.asarray(drawn.astype(out[name].dtype))
    for name, factor in factors.items():
        out[name] = (out[name] * factor).astype(out[name].dtype)
    return out
```

```python
from contextlib import ExitStack
import math

import numpy as np
import concourse.bass as bass
from concourse import mybir

F32 = mybir.dt.float32
F32R = mybir.dt.float32r
BF16 = mybir.dt.bfloat16
U8 = mybir.dt.uint8
ALU = mybir.AluOpType
ACT = mybir.ActivationFunctionType
AX_X = mybir.AxisListType.X

P = 128
D = 1024
SEQ = 256
NTB = SEQ // P
NK = D // P
FF = 2816
SLAB = 256
NF = FF // SLAB
RING = 4
EPS = 1e-6
NEG_BIG = -1e30
TAKEN = -3e38
TINY = 1e-30
LN_EDGE = 2.0 ** -60

HG_HEADS = 8
GLA_HEADS = 4
ATT_HEADS = 16
IDX_HEADS = 8
TOP_K = 64
SB_HEADS = 8
CONV_TAPS = 31
GATE_RANK = 16
GLA_TAU = 16.0
BUCKETS = 32
MAX_DIST = 128
LEVELS = [64, 32, 16, 8, 4, 2, 1]
DISTS = 3 * P

IDENT, CAUSAL, STRICT, TRI, ONES, ONEHOT, ZEROS = 0, 128, 256, 384, 512, 640, 1024
CONST_COLS = ZEROS + 512


def shape_constants():
    c = np.zeros((P, CONST_COLS), np.float32)
    i = np.arange(P)
    row, col = i[:, None], i[None, :]
    c[:, IDENT:IDENT + P] = np.eye(P)
    c[:, CAUSAL:CAUSAL + P] = np.where(col > row, NEG_BIG, 0.0)
    c[:, STRICT:STRICT + P] = np.where(row >= col, NEG_BIG, 0.0)
    c[:, TRI:TRI + P] = np.where(row >= col, -1.0, 0.0)
    c[:, ONES:ONES + P] = -1.0
    dist = np.maximum(255 - np.arange(DISTS), 0)
    exact = BUCKETS // 2
    far = np.maximum(dist, exact).astype(np.float32)
    large = exact + (np.log(far / np.float32(exact)) / np.float32(math.log(MAX_DIST / exact))
                     * np.float32(BUCKETS - exact)).astype(np.int32)
    bucket = np.where(dist < exact, dist, np.minimum(large, BUCKETS - 1))
    c[bucket, ONEHOT + np.arange(DISTS)] = 1.0
    masks = np.zeros((P, len(LEVELS), P), np.float32)
    for n, m in enumerate(LEVELS):
        same = row // (2 * m) == col // (2 * m)
        masks[:, n] = same & (row // m % 2 == 0) & (col // m % 2 == 1)
    return c, masks


class Tally:

    def __init__(self):
        self.n = {}

    def __call__(self, sem, more=1):
        self.n[sem] = self.n.get(sem, 0) + more
        return self.n[sem]


class Uses:

    def __init__(self):
        self.uses = [0] * RING
        self.dmas = [0] * RING

    def take(self, slot, dmas=1):
        u = self.uses[slot]
        self.uses[slot] += 1
        self.dmas[slot] += 16 * dmas
        return u, self.dmas[slot]

    def skip(self, slot, n):
        self.uses[slot] += n
        self.dmas[slot] += 16 * n


def build(nc, A, out):
    with ExitStack() as ctx:
        def sb(name, shape, dt=F32):
            return ctx.enter_context(nc.sbuf_tensor(name, shape, dt))

        def sem(name):
            return ctx.enter_context(nc.semaphore(name))

        raw = [sb(f"raw{s}", [P, 2048]) for s in range(RING)]
        w_hi = [sb(f"w_hi{s}", [P, 2048], F32R) for s in range(RING)]
        w_lo = [sb(f"w_lo{s}", [P, 2048], F32R) for s in range(RING)]
        h = sb("h", [P, NTB, D])
        x_hi = sb("x_hi", [P, NK, SEQ], F32R)
        x_lo = sb("x_lo", [P, NK, SEQ], F32R)
        xn = sb("xn", [P, NTB, D])
        g_hi = sb("g_hi", [P, 2, SEQ], F32R)
        g_lo = sb("g_lo", [P, 2, SEQ], F32R)
        const = sb("const", [P, CONST_COLS])
        level_mask = sb("level_mask", [P, len(LEVELS), P], U8)
        cols = sb("cols", [P, 640])
        small = sb("small", [P, 160])
        arena = sb("arena", [P, 16384])
        ps = ctx.enter_context(nc.psum_tensor("ps", [P, 8, 512], F32))
        bias_dram = nc.dram_tensor("bias_rows", (ATT_HEADS, P, DISTS), F32, kind="Internal").ap()

        ident = const[:, IDENT:IDENT + P]
        zeros = const[:, ZEROS:ZEROS + 512]
        ssq = small[:, 0:2]
        ms = small[:, 2:4]
        std = small[:, 4:6]
        rstd = small[:, 6:8]
        head_ssq = small[:, 8:24]
        head_ms = small[:, 24:40]
        head_std = small[:, 40:56]
        head_rstd = small[:, 56:72]
        lb = small[:, 72:80]
        one_minus_lb = small[:, 80:88]
        lb_a = small[:, 88:96]
        lb_b = small[:, 96:104]
        top8 = small[:, 104:112]
        att_max = small[:, 112:116]
        att_neg = small[:, 116:120]
        att_sum = small[:, 120:124]
        att_inv = small[:, 124:128]
        ln_stats = small[:, 128:140]
        ln_mv = small[:, 140:144]
        ln_std = small[:, 144:146]
        ln_rstd = small[:, 146:148]

        def words(a, n):
            return arena[:, a:a + n]

        proj = words(0, 16 * 512).rearrange("p (s n) -> p s n", n=512)
        ff_c = words(0, 1024).rearrange("p (b g t) -> p b g t", b=2, g=2)
        ff_s = words(1024, 512).rearrange("p (b t) -> p b t", b=2)
        ff_g = words(1536, 512).rearrange("p (b t) -> p b t", b=2)
        gain_row = words(15360, 1024)
        bias_x = words(8192, 16 * 256).rearrange("p (h c) -> p h c", h=ATT_HEADS)

        row_of, row_src, n_rows = {}, [], 0
        for name, src in [
            ("attn_norm", A["attn_norm"].rearrange("l (c p) -> (l c) p", p=P)),
            ("ffn_norm", A["ffn_norm"].rearrange("l (c p) -> (l c) p", p=P)),
            ("hgrn_gate_norm", A["hgrn_gate_norm"]),
            ("hgrn_lower_bounds", A["hgrn_lower_bounds"].rearrange("l (c p) -> (l c) p", p=P)),
            ("norm_g_2", A["norm_g_2"].rearrange("l g (c p) -> (l g c) p", p=P)),
            ("ffn_conv_w", A["ffn_conv_w"].rearrange("l k (c p) -> (l k c) p", p=P)),
            ("ffn_conv_b", A["ffn_conv_b"].rearrange("l (c p) -> (l c) p", p=P)),
            ("conv_dw_w_2", A["conv_dw_w_2"].rearrange("l k (c p) -> (l k c) p", p=P)),
            ("conv_dw_b_2", A["conv_dw_b_2"].rearrange("l (c p) -> (l c) p", p=P)),
            ("conv_ln_g_2", A["conv_ln_g_2"].rearrange("l (c p) -> (l c) p", p=P)),
            ("conv_ln_b_2", A["conv_ln_b_2"].rearrange("l (c p) -> (l c) p", p=P)),
            ("gla_b_gate_2", A["gla_b_gate_2"].rearrange("l (c p) -> (l c) p", p=P)),
            ("gla_norm_g_2", A["gla_norm_g_2"].rearrange("l (c p) -> (l c) p", p=P)),
        ]:
            row_of[name] = n_rows
            done, n = 0, src.shape[0]
            while done < n:
                k = min(n - done, P - n_rows % P)
                row_src.append((n_rows % P, n_rows // P, k, src[done:done + k, :]))
                done += k
                n_rows += k
        n_row_tiles = -(-n_rows // P)
        rows = words(0, n_row_tiles * P).rearrange("p (t n) -> p t n", n=P)
        masks_in = words(1024, len(LEVELS) * P).rearrange("p (l n) -> p l n", n=P)
        rel_bias_sb = words(15360, ATT_HEADS)
        bias_vec = words(15488, DISTS)
        w_gate = words(14336, 512)

        def col(name, i=0):
            c = row_of[name] + i
            return cols[:, c:c + 1]

        raw_full = [sem(f"raw_full{s}") for s in range(RING)]
        hi_done = [sem(f"hi_done{s}") for s in range(RING)]
        slab_ready = [sem(f"slab_ready{s}") for s in range(RING)]
        slab_used = [sem(f"slab_used{s}") for s in range(RING)]
        seeded = sem("seeded")
        const_in = sem("const_in")
        rows_turned, cols_ready = sem("rows_turned"), sem("cols_ready")
        lb_step = sem("lb_step")
        bias_vec_done, bias_vec_copied, bias_out, bias_in = (
            sem("bias_vec_done"), sem("bias_vec_copied"), sem("bias_out"), sem("bias_in"))
        gain_in, gate_in = sem("gain_in"), sem("gate_in")
        h_ready = sem("h_ready")
        rms_sq, rms_ms, rms_std = sem("rms_sq"), sem("rms_ms"), sem("rms_std")
        xn_ready, turned, x_hi_done, x_ready = sem("xn_ready"), sem("turned"), sem("x_hi_done"), sem("x_ready")
        proj_free = sem("proj_free")
        up_half = sem("up_half")
        conv_in = [sem(f"conv_in{b}") for b in range(2)]
        tap_done = [sem(f"tap_done{b}") for b in range(2)]
        conv_done = [sem(f"conv_done{b}") for b in range(2)]
        silu_done = [sem(f"silu_done{b}") for b in range(2)]
        gt_done = [sem(f"gt_done{b}") for b in range(2)]
        gt_hi = [sem(f"gt_hi{b}") for b in range(2)]
        g_ready = sem("g_ready")
        dve_step = sem("dve_step")
        act_step = sem("act_step")
        la_gate, la_ln_in, la_ln, la_init = sem("la_gate"), sem("la_ln_in"), sem("la_ln"), sem("la_init")
        la_diff, la_exp, la_factors, la_scores = sem("la_diff"), sem("la_exp"), sem("la_factors"), sem("la_scores")
        la_masked, la_cross = sem("la_masked"), sem("la_cross")
        la_out, la_sq, la_ms, la_std, la_silu = sem("la_out"), sem("la_sq"), sem("la_ms"), sem("la_std"), sem("la_silu")
        la_q = sem("la_q")
        gate_mm, gate_x, gate_ln = sem("gate_mm"), sem("gate_x"), sem("gate_ln")
        ix_dots, ix_relu, ix_acc = sem("ix_dots"), sem("ix_relu"), sem("ix_acc")
        at_k, at_qk, at_max, at_exp, at_p, at_tr, at_pt, at_pv = (
            sem("at_k"), sem("at_qk"), sem("at_max"), sem("at_exp"), sem("at_p"), sem("at_tr"), sem("at_pt"), sem("at_pv"))
        at_bank = sem("at_bank")
        sb_k, sb_z, sb_ln, sb_sp, sb_rest, sb_w, sb_pv = (
            sem("sb_k"), sem("sb_z"), sem("sb_ln"), sem("sb_sp"), sem("sb_rest"), sem("sb_w"), sem("sb_pv"))
        cv_sig, cv_pad, cv_tap, cv_turn, cv_ms, cv_std, cv_norm, cv_back, cv_silu = (
            sem("cv_sig"), sem("cv_pad"), sem("cv_tap"), sem("cv_turn"), sem("cv_ms"), sem("cv_std"), sem("cv_norm"),
            sem("cv_back"), sem("cv_silu"))
        stored = sem("stored")

        block = ctx.enter_context(nc.Block())

        def col_slab(w, c0, n=SLAB):
            return w[:, bass.ds(c0, n)].rearrange("(c p) n -> p c n", p=P)

        def row_slab(w, r0):
            return w[bass.ds(r0, SLAB), :].rearrange("(c p) n -> p c n", p=P)

        def raw_cols(s, a=0, n=SLAB):
            return raw[s][:, :].rearrange("p (c n) -> p c n", c=NK)[:, :, a:a + n]

        def raw_rows(s):
            return raw[s][:, :].rearrange("p (c n) -> p c n", c=2)

        ffn_w = [(A["ffn_w_up"][l], A["ffn_w_down"][l]) for l in range(2)]
        ffn1_w = [(A["ffn1_w_in_2"][l], A["ffn1_w_out_2"][l]) for l in range(2)]
        ffn2_w = [(A["ffn2_w_in_2"][l], A["ffn2_w_out_2"][l]) for l in range(2)]
        FFNS = [ffn_w[0], ffn_w[1], ffn1_w[0], ffn2_w[0], ffn1_w[1], ffn2_w[1]]
        hgrn_in, hgrn_out = A["hgrn_w_in"][0], A["hgrn_w_out"][0]
        dsa_in, dsa_out = A["dsa_w_in"][0], A["dsa_w_out"][0]
        hyb_in, hyb_out = A["hyb_w_in_2"][0], A["hyb_w_out_2"][0]
        gla_in, gla_out = A["gla_w_in_2"][0], A["gla_w_out_2"][0]
        DSA_K, DSA_V, DSA_QI, DSA_KI, DSA_W = 1024, 1152, 1280, 1792, 1856

        def hgrn_views():
            return dict(
                q=words(0, 2048), f=words(2048, 2048), v=proj[:, 8:12, :], gate=words(6144, 2048),
                k=words(8192, 2048), b=words(10240, 2048), qt=words(12288, 2048), ln2=words(12288, 2048),
                kt=xn[:, :, :].rearrange("p b n -> p (b n)"), scores=words(14336, 2048),
                e=words(2048, 2048), cross=words(2048, 1024), sq=words(10240, 2048).rearrange("p (b n) -> p b n", b=2))

        def gla_views():
            return dict(
                q=words(0, 1024), k=words(1024, 1024), v=proj[:, 4:8, :], gate=words(4096, 2048),
                x=words(6656, 1024), f=words(6656, 1024), b=words(8704, 1024), e=words(9728, 1024),
                qt=words(10752, 1024), kt=words(11776, 1024), scores=words(12800, 1024), cross=words(13824, 512),
                sq=words(0, 2048).rearrange("p (b n) -> p b n", b=2), rank=proj[0:GATE_RANK, 12, 0:SEQ])

        def dsa_views():
            return dict(
                q=words(0, 2048).rearrange("p (c t) -> p c t", t=SEQ), k=words(2048, 512).rearrange("p (c t) -> p c t", t=SEQ),
                qi=words(2560, 1024).rearrange("p (c t) -> p c t", t=SEQ), ki=words(3584, SEQ),
                v=words(3584 + SEQ, SEQ).rearrange("p (b n) -> p b n", b=NTB), w=words(4096, 16),
                w_scaled=words(4112, 16), relu=words(4608, 512).rearrange("p (b s) -> p b s", b=2),
                score=words(5120, 512).rearrange("p (b s) -> p b s", b=2), rest=words(5632, SEQ),
                mask=words(6144, 512).rearrange("p (b s) -> p b s", b=2),
                a=words(6656, 1024).rearrange("p (b s) -> p b s", b=4), pt=words(7680, 512).rearrange("p (b s) -> p b s", b=2))

        def hyb_views():
            return dict(
                q=words(0, 1024).rearrange("p (c t) -> p c t", t=SEQ), k_all=words(1024, 1024),
                k=words(1024, 1024).rearrange("p (c t) -> p c t", t=SEQ),
                u=words(2048, 1024).rearrange("p (c t) -> p c t", t=SEQ), gate=words(3072, 1024),
                v=proj[:, 8:10, :], pad=words(5120, 4 * (SEQ + CONV_TAPS - 1)).rearrange("p (c t) -> p c t", c=4),
                co=words(6400, 1024).rearrange("p (c t) -> p c t", t=SEQ), cs=words(7424, 1024).rearrange("p (c t) -> p c t", t=SEQ),
                l=words(9216, 768).rearrange("p (b n) -> p b n", b=2),
                sp=words(9984, 768).rearrange("p (b n) -> p b n", b=2), w=words(10752, 768).rearrange("p (b n) -> p b n", b=2))

        def v_of(la, tb, hd, dv):
            c = hd * dv
            return la["v"][:, c // SLAB, tb * SLAB + c % SLAB:tb * SLAB + c % SLAB + dv]

        @block.sync
        def _(sp):
            ring = Uses()

            def load(slot, pieces):
                u, _ = ring.take(slot, len(pieces))
                sp.wait_ge(slab_ready[slot], u + 1)
                for dst, src in pieces:
                    sp.dma_start(dst, src).then_inc(raw_full[slot], 16)

            def load_four_columns(w, c0, n, stride=RING * SLAB):
                with sp.Fori(0, n) as i:
                    for s in range(RING):
                        sp.wait_ge(slab_ready[s], i + (ring.uses[s] + 1))
                        sp.dma_start(raw_cols(s), col_slab(w, i * stride + (c0 + s * SLAB))).then_inc(raw_full[s], 16)
                for s in range(RING):
                    ring.skip(s, n)

            def load_out(w):
                for s in range(RING):
                    load(s, [(raw_rows(s), row_slab(w, s * SLAB))])

            def load_ffn(f):
                up, down = FFNS[f]
                load(0, [(raw_cols(0), col_slab(up, 0))])
                load(1, [(raw_cols(1), col_slab(up, FF))])
                with sp.Fori(0, NF - 1) as i:
                    sp.wait_ge(slab_ready[0], i + (ring.uses[0] + 1))
                    sp.dma_start(raw_cols(0), col_slab(up, i * SLAB + SLAB)).then_inc(raw_full[0], 16)
                    sp.wait_ge(slab_ready[1], i + (ring.uses[1] + 1))
                    sp.dma_start(raw_cols(1), col_slab(up, i * SLAB + (FF + SLAB))).then_inc(raw_full[1], 16)
                    sp.wait_ge(slab_ready[2], i + (ring.uses[2] + 1))
                    sp.dma_start(raw_rows(2), row_slab(down, i * SLAB)).then_inc(raw_full[2], 16)
                for s in range(3):
                    ring.skip(s, NF - 1)
                load(2, [(raw_rows(2), row_slab(down, (NF - 1) * SLAB))])

            load_four_columns(hgrn_in, 0, 4)
            load_out(hgrn_out)
            load_ffn(0)
            for s in range(RING):
                load(s, [(raw_cols(s), col_slab(dsa_in, s * SLAB))])
            k0, k1 = (dsa_in[:, DSA_K + 64 * j:DSA_K + 64 * j + 64].rearrange("(c p) n -> p c n", p=P) for j in range(2))
            ki = dsa_in[:, DSA_KI:DSA_KI + 64].rearrange("(c p) n -> p c n", p=P)
            load(0, [(raw_cols(0, 64 * j, 64), k) for j, k in enumerate([k0, k0, k1, k1])])
            load(1, [(raw_cols(1), col_slab(dsa_in, DSA_QI))])
            load(2, [(raw_cols(2), col_slab(dsa_in, DSA_QI + SLAB))])
            load(3, [(raw_cols(3, 0, 64), ki), (raw_cols(3, 64, 64), ki), (raw_cols(3, P, P), col_slab(dsa_in, DSA_V, P))])
            load(0, [(raw_cols(0, 0, IDX_HEADS), col_slab(dsa_in, DSA_W, IDX_HEADS))])
            load_out(dsa_out)
            load_ffn(1)
            load_ffn(2)
            load_four_columns(hyb_in, 0, 2, stride=6 * SLAB)
            for s in range(2):
                load(s, [(raw_cols(s), col_slab(hyb_in, 4 * SLAB + s * SLAB))])
            load_out(hyb_out)
            load_ffn(3)
            load_ffn(4)
            load_four_columns(gla_in, 0, 3)
            load(0, [(raw_cols(0, 0, GATE_RANK), col_slab(gla_in, 12 * SLAB, GATE_RANK))])
            load_out(gla_out)
            load_ffn(5)
            sp.wait_ge(h_ready, 2 * 11)
            sp.dma_start(out[0].rearrange("(b p) d -> p b d", p=P), h[:, :, :]).then_inc(stored, 16)
            sp.wait_ge(stored, 16)

        @block.gpsimd
        def _(pool):
            ring = Uses()

            def low(slot, u):
                pool.wait_ge(hi_done[slot], u + 1)
                pool.tensor_tensor(w_lo[slot][:, :], raw[slot][:, :], w_hi[slot][:, :].bitcast(F32), ALU.subtract)\
                    .then_inc(slab_ready[slot], 1)

            def low_one(slot):
                u, _ = ring.take(slot)
                low(slot, u)

            def low_four(n):
                with pool.Fori(0, n) as i:
                    for s in range(RING):
                        low(s, i + ring.uses[s])
                for s in range(RING):
                    ring.skip(s, n)

            def low_ffn():
                low_one(0)
                low_one(1)
                with pool.Fori(0, NF - 1) as i:
                    for s in range(3):
                        low(s, i + ring.uses[s])
                for s in range(3):
                    ring.skip(s, NF - 1)
                low_one(2)

            low_four(5)
            low_ffn()
            low_four(2)
            low_one(0)
            low_four(1)
            low_ffn()
            low_ffn()
            low_four(2)
            low_one(0)
            low_one(1)
            low_four(1)
            low_ffn()
            low_ffn()
            low_four(3)
            low_one(0)
            low_four(1)
            low_ffn()

        @block.scalar
        def _(act):
            ring, want = Uses(), Tally()
            consts = 0

            def fetch(dst, src):
                nonlocal consts
                act.dma_start(dst, src).then_inc(const_in, 16)
                consts += 16

            def link(ins):
                ins.then_inc(act_step, 1)
                act.wait_ge(act_step, want(act_step))

            def high(slot, u, full):
                act.wait_ge(raw_full[slot], full)
                act.wait_ge(slab_used[slot], u + 1)
                act.activation(w_hi[slot][:, :], raw[slot][:, :], ACT.Copy).then_inc(hi_done[slot], 1)

            def high_one(slot, dmas=1):
                high(slot, *ring.take(slot, dmas))

            def high_four(n):
                with act.Fori(0, n) as i:
                    for s in range(RING):
                        high(s, i + ring.uses[s], i * 16 + (ring.dmas[s] + 16))
                for s in range(RING):
                    ring.skip(s, n)

            def rms(src):
                for tb in range(NTB):
                    act.activation(xn[:, tb, :], src(tb), ACT.Square, accum_out=ssq[:, tb:tb + 1]).then_inc(rms_sq, 1)
                act.wait_ge(rms_ms, want(rms_ms))
                act.activation(std, ms, ACT.Sqrt).then_inc(rms_std, 1)

            def split_turned(gains):
                for c in range(NK):
                    if c % 2 == 0:
                        act.wait_ge(turned, want(turned))
                    act.activation(x_hi[:, c, :], ps[:, 4 + c // 2, c % 2 * SEQ:c % 2 * SEQ + SEQ], ACT.Copy,
                                   scale=gains[c]).then_inc(x_hi_done, 1)

            def norm(name, i, updates):
                if updates:
                    act.wait_ge(h_ready, 2 * updates)
                rms(lambda tb: h[:, tb, :])
                split_turned([col(name, i * NK + c) for c in range(NK)])

            def rms_product(slot):
                act.wait_ge(slab_used[slot], ring.uses[slot] + 1)
                rms(lambda tb: ps[:, 2 * tb:2 * tb + 2, :].rearrange("p b n -> p (b n)"))

            def ffn(conv, f_conv, f):
                b0, b1, b2 = ring.uses[0], ring.uses[1], ring.uses[2]
                m0, m1, m2 = ring.dmas[0], ring.dmas[1], ring.dmas[2]
                q0 = f * NF

                def up_done(b, i):
                    if b == 0:
                        act.wait_ge(up_half, i + (q0 + 1))
                    else:
                        act.wait_ge(slab_used[1], i + (b1 - 1 + 2))

                def start_gate(b, i):
                    up_done(b, i)
                    bank = ps[:, 4 + b, :]
                    if conv:
                        for g in range(2):
                            c = i * 2 + (row_of["ffn_conv_w"] + f_conv * 132 + 88 + g * 22 + b)
                            cb = i * 2 + (row_of["ffn_conv_b"] + f_conv * 44 + g * 22 + b)
                            ins = act.activation(ff_c[:, b, g, :], bank[:, g * SEQ:g * SEQ + SEQ], ACT.Identity,
                                                 bias=cols[:, bass.ds(cb, 1)], scale=cols[:, bass.ds(c, 1)])
                        ins.then_inc(conv_in[b], 1)
                    else:
                        act.activation(ff_s[:, b, :], bank[:, 0:SEQ], ACT.Silu).then_inc(silu_done[b], 1)

                def conv_silu(b, i):
                    act.wait_ge(conv_done[b], i + (f_conv * NF + 1))
                    act.activation(ff_s[:, b, :], ff_c[:, b, 0, :], ACT.Silu).then_inc(silu_done[b], 1)

                def split(b, i):
                    act.wait_ge(gt_done[b], i + (q0 + 2))
                    if b == 0:
                        act.wait_ge(slab_used[2], i + (b2 + 1))
                    act.activation(g_hi[:, b, :], ff_g[:, b, :], ACT.Copy).then_inc(gt_hi[b], 1)

                def body(i, last):
                    if not last:
                        high(0, i + b0, i * 16 + (m0 + 16))
                    start_gate(0, i)
                    start_gate(1, i)
                    if conv:
                        conv_silu(0, i)
                    if not last:
                        high(1, i + b1, i * 16 + (m1 + 16))
                    if conv:
                        conv_silu(1, i)
                    if not last:
                        split(0, i)
                        split(1, i)
                        high(2, i + b2, i * 16 + (m2 + 16))
                    else:
                        high(2, i + b2, i * 16 + (m2 + 16))
                        split(0, i)
                        split(1, i)

                with act.Fori(0, NF - 1) as i:
                    body(i, False)
                body(NF - 1, True)
                ring.skip(0, NF - 1)
                ring.skip(1, NF - 1)
                ring.skip(2, NF)

            fetch(h[:, :, :], A["x"][0].rearrange("(b p) d -> p b d", p=P))
            fetch(const[:, :], A["shape_const"])
            fetch(masks_in, A["level_masks"])
            for p0, t, k, src in row_src:
                fetch(rows[p0:p0 + k, t, :], src)
            fetch(rel_bias_sb[0:BUCKETS, :], A["rel_bias"])
            high_one(0)
            act.wait_ge(const_in, consts)
            act.wait_ge(rows_turned, 1)
            act.activation(cols[:, 0:n_rows], ps[:, 0:2, :].rearrange("p b n -> p (b n)")[:, 0:n_rows], ACT.Copy).then_inc(cols_ready, 1)
            act.wait_ge(lb_step, 1)
            act.activation(lb_b, lb_a, ACT.Exp).then_inc(lb_step, 1)
            act.wait_ge(bias_vec_done, 1)
            link(act.activation(bias_vec[0:ATT_HEADS, :], ps[0:ATT_HEADS, 2, 0:DISTS], ACT.Copy))
            act.dma_start(bias_dram, bias_vec[0:ATT_HEADS, :].unsqueeze(1).broadcast_to([ATT_HEADS, P, DISTS]))\
                .then_inc(bias_out, 16)
            norm("attn_norm", 0, 0)
            for s in range(1, RING):
                high_one(s)

            def linear_attention(H):
                e, cross = la["e"], la["cross"]
                act.wait_ge(la_q, want(la_q))
                act.activation(la["qt"], la["q"], ACT.Copy)
                act.activation(la["kt"], la["k"], ACT.Copy).then_inc(la_init, 1)
                for m in LEVELS + [P]:
                    act.wait_ge(la_diff, want(la_diff))
                    act.activation(e, e, ACT.Exp).then_inc(la_exp, 1)
                act.wait_ge(la_scores, want(la_scores, 8 * (H // 2) + H // 4))
                act.activation(cross[:, 0:H * P], ps[:, 0:H // 4, :].rearrange("p b n -> p (b n)"), ACT.Copy)\
                    .then_inc(la_cross, 1)
                act.wait_ge(la_out, want(la_out))
                for tb in range(NTB):
                    act.activation(la["sq"][:, tb, :], ps[:, 4 + 2 * tb:6 + 2 * tb, :].rearrange("p b n -> p (b n)"),
                                   ACT.Square).then_inc(la_sq, 1)
                act.wait_ge(la_ms, want(la_ms))
                act.activation(head_std[:, 0:2 * H], head_ms[:, 0:2 * H], ACT.Sqrt).then_inc(la_std, 1)

            la = hgrn_views()
            high_four(4)
            act.wait_ge(proj_free, 4 + 8)
            act.activation(la["k"], la["f"], ACT.Sigmoid, scale=-1.0)
            act.activation(la["f"], la["f"], ACT.Sigmoid).then_inc(la_gate, 1)
            act.wait_ge(proj_free, 4 + 16)
            act.activation(la["gate"], la["gate"], ACT.Silu).then_inc(la_silu, 1)
            act.wait_ge(la_ln_in, 1)
            act.activation(la["f"], la["f"], ACT.Ln)
            act.activation(la["ln2"], la["ln2"], ACT.Ln, scale=1.0 / LN_EDGE).then_inc(la_ln, 1)
            linear_attention(HG_HEADS)
            split_turned([col("hgrn_gate_norm")] * NK)
            high_one(0)
            high_one(1)
            norm("ffn_norm", 0, 1)
            ffn(True, 0, 0)

            act.wait_ge(bias_out, 16)
            act.wait_ge(h_ready, 2 * 1)
            act.dma_start(bias_x[:, :, :], bass.AP(bias_dram.tensor, P - 1, [[DISTS - 1, P], [P * DISTS, ATT_HEADS], [1, SEQ]]))\
                .then_inc(bias_in, 16)
            high_one(0)
            high_one(1)
            norm("attn_norm", 1, 2)
            high_one(2)
            high_one(3)
            high_one(0, 4)
            high_one(1)
            high_one(2)
            high_one(3, 3)
            high_one(0)
            high_four(1)
            dsa = dsa_views()
            for tb in range(NTB):
                S = (tb + 1) * P
                for hd in range(IDX_HEADS):
                    n = tb * IDX_HEADS + hd
                    act.wait_ge(ix_dots, n + 1)
                    if n >= 2:
                        act.wait_ge(ix_acc, n - 1)
                    act.activation(dsa["relu"][:, n % 2, 0:S], ps[:, n % 4, 0:S], ACT.Relu).then_inc(ix_relu, 1)
            UNITS = NTB * ATT_HEADS

            def exps(n):
                S = (n // ATT_HEADS + 1) * P
                act.wait_ge(at_max, n + 1)
                act.activation(dsa["a"][:, n % 4, 0:S], dsa["a"][:, n % 4, 0:S], ACT.Exp, bias=att_neg[:, n % 4:n % 4 + 1],
                               accum_out=att_sum[:, n % 4:n % 4 + 1]).then_inc(at_exp, 1)

            def copy_turned(n):
                S = (n // ATT_HEADS + 1) * P
                act.wait_ge(at_tr, n + 1)
                if n >= 2:
                    act.wait_ge(at_pv, n - 1)
                act.activation(dsa["pt"][:, n % 2, 0:S], ps[:, 2 + n % 2, 0:S], ACT.Copy).then_inc(at_pt, 1)

            for n in range(UNITS + 2):
                if n < UNITS:
                    exps(n)
                if n >= 2:
                    copy_turned(n - 2)
            act.wait_ge(at_pv, UNITS)
            for b in range(4):
                act.activation(x_hi[:, 2 * b:2 * b + 2, :].rearrange("p c t -> p (c t)"), ps[:, 4 + b, :], ACT.Copy)\
                    .then_inc(x_hi_done, 1)
            high_one(0)
            high_one(1)
            norm("ffn_norm", 1, 3)
            ffn(True, 1, 1)

            def fetch_gain(src):
                act.dma_start(gain_row, src.unsqueeze(0).broadcast_to([P, D])).then_inc(gain_in, 16)

            def pre(l, g, updates):
                norm("norm_g_2", l * 6 + g, updates)

            high_one(0)
            high_one(1)
            fetch_gain(A["final_norm"])
            act.wait_ge(h_ready, 2 * 4)
            rms(lambda tb: h[:, tb, :])
            updates = 5
            for l in range(2):
                pre(l, 0, updates)
                act.wait_ge(h_ready, 2 * updates)
                fetch_gain(A["norm_g_2"][l, 1])
                ffn(False, 0, 2 + 2 * l)
                high_one(0)
                high_one(1)
                rms_product(2)
                updates += 1
                pre(l, 2, updates)
                high_one(2)
                high_one(3)
                act.wait_ge(h_ready, 2 * updates)
                fetch_gain(A["norm_g_2"][l, 3])
                if l == 0:
                    hyb = hyb_views()
                    high_four(1)
                    high_one(0)
                    high_one(1)
                    high_four(1)
                    base = 4 + 16 + 9
                    act.wait_ge(proj_free, base + 8)
                    act.activation(hyb["gate"], hyb["gate"], ACT.Sigmoid).then_inc(cv_sig, 1)

                    def stick_exp(hd):
                        act.wait_ge(sb_z, hd + 1)
                        if hd >= 2:
                            act.wait_ge(sb_sp, hd - 1)
                        link(act.activation(hyb["l"][:, hd % 2, :], ps[:, hd % 4, 0:3 * P], ACT.Abs))
                        link(act.activation(hyb["l"][:, hd % 2, :], hyb["l"][:, hd % 2, :], ACT.Exp, scale=-1.0))
                        act.activation(hyb["l"][:, hd % 2, :], hyb["l"][:, hd % 2, :], ACT.Ln, bias=1.0).then_inc(sb_ln, 1)

                    def stick_weights(hd):
                        act.wait_ge(sb_rest, hd + 1)
                        if hd >= 2:
                            act.wait_ge(sb_pv, hd - 1)
                        act.activation(hyb["w"][:, hd % 2, :], ps[:, hd % 4, 0:3 * P], ACT.Exp).then_inc(sb_w, 1)

                    for hd in range(SB_HEADS + 1):
                        if hd < SB_HEADS:
                            stick_exp(hd)
                        if hd >= 1:
                            stick_weights(hd - 1)
                    act.wait_ge(sb_pv, SB_HEADS)
                    for b in range(2):
                        act.activation(x_hi[:, 2 * b:2 * b + 2, :].rearrange("p c t -> p (c t)"), ps[:, 4 + b, :], ACT.Copy)\
                            .then_inc(x_hi_done, 1)
                    act.wait_ge(cv_ms, 1)
                    act.activation(ln_std, ln_mv.rearrange("p (b s) -> p b s", s=2)[:, :, 1], ACT.Sqrt).then_inc(cv_std, 1)
                    for c in range(4):
                        act.wait_ge(cv_back, c // 2 + 1)
                        act.activation(hyb["cs"][:, c, :], ps[:, 2 + c // 2, c % 2 * SEQ:c % 2 * SEQ + SEQ], ACT.Silu,
                                       bias=col("conv_ln_b_2", c), scale=col("conv_ln_g_2", c)).then_inc(cv_silu, 1)
                    for c in range(4):
                        act.wait_ge(cv_silu, c + 1)
                        act.activation(x_hi[:, 4 + c, :], hyb["cs"][:, c, :], ACT.Copy).then_inc(x_hi_done, 1)
                else:
                    la = gla_views()
                    act.dma_start(w_gate[0:GATE_RANK, :], A["gla_w_gate_2"][0]).then_inc(gate_in, 16)
                    high_four(2)
                    high_one(0)
                    high_four(1)
                    base = 4 + 16 + 9 + 10
                    act.wait_ge(proj_free, base + 13)
                    act.activation(la["gate"], la["gate"], ACT.Silu).then_inc(la_silu, 1)
                    for c in range(4):
                        act.wait_ge(gate_mm, 1)
                        ins = act.activation(la["x"][:, c * SEQ:c * SEQ + SEQ], ps[:, c // 2, c % 2 * SEQ:c % 2 * SEQ + SEQ],
                                             ACT.Identity, bias=col("gla_b_gate_2", c))
                    ins.then_inc(gate_x, 1)
                    act.wait_ge(gate_x, 1)
                    link(act.activation(la["e"], la["x"], ACT.Abs))
                    link(act.activation(la["e"], la["e"], ACT.Exp, scale=-1.0))
                    act.activation(la["e"], la["e"], ACT.Ln, bias=1.0).then_inc(gate_ln, 1)
                    linear_attention(GLA_HEADS)
                    split_turned([col("gla_norm_g_2", c % 2) for c in range(NK)])
                high_one(0)
                high_one(1)
                rms_product(3)
                updates += 1
                pre(l, 4, updates)
                act.wait_ge(h_ready, 2 * updates)
                fetch_gain(A["norm_g_2"][l, 5])
                ffn(False, 0, 3 + 2 * l)
                if l == 0:
                    high_one(0)
                    high_one(1)
                rms_product(2)
                updates += 1

        @block.vector
        def _(dve):
            used, want = [0] * RING, Tally()

            def link(ins):
                ins.then_inc(dve_step, 1)
                dve.wait_ge(dve_step, want(dve_step))

            def flat(bank, n=1):
                return ps[:, bank:bank + n, :].rearrange("p b n -> p (b n)")

            def copy_products(n, at, parts=None):
                for j in range(n):
                    s = j % RING
                    used[s] += 1
                    dve.wait_ge(slab_used[s], used[s] + 1)
                    dst, src = arena[:, at + j * 512:at + j * 512 + 512], ps[:, 4 + s, :]
                    if parts is not None:
                        dst, src = dst[0:parts[0], 0:parts[1]], src[0:parts[0], 0:parts[1]]
                    dve.tensor_copy(dst, src).then_inc(proj_free, 1)

            def copy_four(n, at):
                with dve.Fori(0, n) as i:
                    for s in range(RING):
                        dve.wait_ge(slab_used[s], i + (used[s] + 2))
                        dve.tensor_copy(arena[:, bass.ds(i * 2048 + (at + s * 512), 512)], ps[:, 4 + s, :]).then_inc(proj_free, 1)
                for s in range(RING):
                    used[s] += n

            def inverse_rms(width):
                dve.wait_ge(rms_sq, want(rms_sq, NTB))
                dve.tensor_scalar(ms, ssq, 1.0 / width, EPS, ALU.mult, ALU.add).then_inc(rms_ms, 1)
                dve.wait_ge(rms_std, want(rms_std))
                link(dve.reciprocal(rstd, std))

            def split_turned(gains):
                for c in range(NK):
                    if c % 2 == 0:
                        dve.wait_ge(x_hi_done, want(x_hi_done, 2))
                    dve.scalar_tensor_tensor(x_lo[:, c, :], ps[:, 4 + c // 2, c % 2 * SEQ:c % 2 * SEQ + SEQ], gains[c],
                                             x_hi[:, c, :].bitcast(F32), ALU.mult, ALU.subtract).then_inc(x_ready, 1)

            def norm(name, i):
                inverse_rms(D)
                for tb in range(NTB):
                    dve.tensor_scalar(xn[:, tb, :], h[:, tb, :], rstd[:, tb:tb + 1], None, ALU.mult).then_inc(xn_ready, 1)
                split_turned([col(name, i * NK + c) for c in range(NK)])

            def add_product(slot):
                dve.wait_ge(slab_used[slot], used[slot] + 1)
                for tb in range(NTB):
                    dve.tensor_tensor(h[:, tb, :], h[:, tb, :], flat(2 * tb, 2), ALU.add).then_inc(h_ready, 1)

            def add_normed_product(half):
                inverse_rms(D)
                if half:
                    link(dve.tensor_scalar(rstd, rstd, 0.5, None, ALU.mult))
                dve.wait_ge(gain_in, want(gain_in, 16))
                for tb in range(NTB):
                    dve.scalar_tensor_tensor(xn[:, tb, :], flat(2 * tb, 2), rstd[:, tb:tb + 1], gain_row, ALU.mult, ALU.mult)\
                        .then_inc(dve_step, 1)
                n = want(dve_step, NTB)
                for tb in range(NTB):
                    dve.wait_ge(dve_step, n - 1 + tb)
                    dve.tensor_tensor(h[:, tb, :], h[:, tb, :], xn[:, tb, :], ALU.add).then_inc(h_ready, 1)

            def out_used():
                for s in range(RING):
                    used[s] += 1

            def ffn(conv, f_conv, f):
                q0 = f * NF
                with dve.Fori(0, NF) as i:
                    if conv:
                        for b in range(2):
                            bank = ps[:, 4 + b, :]

                            def tap(g, k):
                                shift = 2 - k
                                c = i * 2 + (row_of["ffn_conv_w"] + f_conv * 132 + k * 44 + g * 22 + b)
                                dst = ff_c[:, b, g, shift:SEQ]
                                return dve.scalar_tensor_tensor(dst, bank[:, g * SEQ:g * SEQ + SEQ - shift],
                                                                cols[:, bass.ds(c, 1)], dst, ALU.mult, ALU.add)
                            dve.wait_ge(conv_in[b], i + (f_conv * NF + 1))
                            tap(0, 1).then_inc(tap_done[b], 1)
                            tap(1, 1).then_inc(tap_done[b], 1)
                            dve.wait_ge(tap_done[b], i * 2 + (f_conv * NF * 2 + 2))
                            tap(0, 0)
                            tap(1, 0).then_inc(conv_done[b], 1)
                    for b in range(2):
                        dve.wait_ge(silu_done[b], i + (q0 + 1))
                        if not conv and b == 0:
                            dve.wait_ge(g_ready, i * 2 + 2 * q0)
                        up = ff_c[:, b, 1, :] if conv else ps[:, 4 + b, SEQ:2 * SEQ]
                        dve.tensor_tensor(ff_g[:, b, :], ff_s[:, b, :], up, ALU.mult).then_inc(gt_done[b], 1)
                    for b in range(2):
                        dve.wait_ge(gt_hi[b], i + (q0 + 1))
                        dve.tensor_tensor(g_lo[:, b, :], ff_g[:, b, :], g_hi[:, b, :].bitcast(F32), ALU.subtract)\
                            .then_inc(g_ready, 1)
                for s in range(3):
                    used[s] += NF

            def linear_attention(la, H, dv, gains):
                q, k, qt, kt, b, e = la["q"], la["k"], la["qt"], la["kt"], la["b"], la["e"]
                scores = la["scores"]
                banks = H // 2

                def halves(t, m):
                    v = t.rearrange("p (n two m) -> p n two m", two=2, m=m)
                    return v[:, :, 0, :], v[:, :, 1, :]

                def differences(m):
                    b_lo, b_up = halves(b, m)
                    e_lo, e_up = halves(e, m)
                    r = b_lo[:, :, m - 1:m].broadcast_to([P, H * SEQ // (2 * m), m])
                    dve.tensor_tensor(e_up, b_up, r, ALU.subtract)
                    dve.tensor_tensor(e_lo, r, b_lo, ALU.subtract).then_inc(la_diff, 1)

                def by_head(t, bank):
                    return t[:, bank * 512:bank * 512 + 512].rearrange("p (n t) -> p n t", t=P)

                for hd in range(H):
                    a = hd * SEQ
                    ins = dve.tensor_tensor_scan(b[:, a:a + SEQ], la["f"][:, a:a + SEQ], zeros[:, 0:SEQ], 0.0, ALU.add, ALU.add)
                link(ins)
                levels = LEVELS + [P]
                differences(levels[0])
                for n in range(banks):
                    dve.wait_ge(la_scores, want(la_scores))
                    ins = dve.tensor_tensor(by_head(scores, n), by_head(flat(n), 0),
                                            ident.unsqueeze(1).broadcast_to([P, 4, P]), ALU.mult)
                ins.then_inc(la_masked, 1)
                dve.wait_ge(la_init, want(la_init))
                for n, m in enumerate(levels):
                    dve.wait_ge(la_exp, want(la_exp))
                    lo, up = 0, 1
                    dve.tensor_tensor(halves(qt, m)[up], halves(q, m)[up], halves(e, m)[up], ALU.mult)
                    dve.tensor_tensor(halves(kt, m)[lo], halves(k, m)[lo], halves(e, m)[lo], ALU.mult).then_inc(la_factors, 1)
                    if n + 1 < len(levels):
                        dve.wait_ge(la_factors, want(la_factors))
                        differences(levels[n + 1])
                        mask = level_mask[:, n, :].unsqueeze(1).broadcast_to([P, 4, P])
                        for bank in range(banks):
                            dve.wait_ge(la_scores, want(la_scores))
                            ins = dve.copy_predicated(by_head(scores, bank), mask, by_head(flat(bank), 0))
                        ins.then_inc(la_masked, 1)
                want(la_factors)
                want(la_scores, H // 4)
                per = H
                for tb in range(NTB):
                    dve.wait_ge(la_sq, want(la_sq))
                    ins = dve.tensor_reduce(head_ssq[:, tb * per:tb * per + per],
                                            la["sq"][:, tb, :].rearrange("p (h d) -> p h d", d=dv), AX_X, ALU.add)
                link(ins)
                dve.tensor_scalar(head_ms[:, 0:2 * per], head_ssq[:, 0:2 * per], 1.0 / dv, EPS, ALU.mult, ALU.add).then_inc(la_ms, 1)
                dve.wait_ge(la_std, want(la_std))
                link(dve.reciprocal(head_rstd[:, 0:2 * per], head_std[:, 0:2 * per]))
                dve.wait_ge(la_silu, want(la_silu))
                gate = la["gate"].rearrange("p (s n) -> p s n", n=512)
                for tb in range(NTB):
                    for hd in range(H):
                        c = hd * dv
                        ins = dve.scalar_tensor_tensor(
                            xn[:, tb, c:c + dv], ps[:, 4 + 2 * tb + c // 512, c % 512:c % 512 + dv],
                            head_rstd[:, tb * per + hd:tb * per + hd + 1],
                            gate[:, c // SLAB, tb * SLAB + c % SLAB:tb * SLAB + c % SLAB + dv], ALU.mult, ALU.mult)
                    ins.then_inc(xn_ready, 1)
                split_turned(gains)

            def low_of_banks(n):
                for b in range(n):
                    dve.wait_ge(x_hi_done, want(x_hi_done))
                    dve.tensor_tensor(x_lo[:, 2 * b:2 * b + 2, :].rearrange("p c t -> p (c t)"), ps[:, 4 + b, :],
                                      x_hi[:, 2 * b:2 * b + 2, :].bitcast(F32).rearrange("p c t -> p (c t)"), ALU.subtract)\
                        .then_inc(x_ready, 1)

            for s in range(RING):
                dve.sem_inc(slab_ready[s], 1)
                dve.sem_inc(slab_used[s], 1)
            for b in range(2):
                dve.sem_inc(gt_done[b], 1)
            dve.sem_inc(proj_free, RING)
            dve.wait_ge(cols_ready, 1)
            link(dve.tensor_copy(level_mask[:, :, :], masks_in))
            lb_col = cols[:, row_of["hgrn_lower_bounds"]:row_of["hgrn_lower_bounds"] + NK]
            dve.tensor_tensor(lb_a, lb_col, lb_col, ALU.subtract).then_inc(lb_step, 1)
            dve.wait_ge(lb_step, 2)
            link(dve.reciprocal(lb_a, lb_b))
            link(dve.tensor_tensor(lb_b, lb_b, lb_a, ALU.mult))
            link(dve.tensor_tensor(lb, lb_b, lb_b, ALU.subtract))
            link(dve.tensor_scalar(one_minus_lb, lb, -1.0, 1.0, ALU.mult, ALU.add))

            norm("attn_norm", 0)
            copy_four(4, 0)
            la = hgrn_views()
            dve.wait_ge(la_gate, 1)
            for hd in range(HG_HEADS):
                f, k = (la[n][:, hd * SEQ:hd * SEQ + SEQ] for n in "fk")
                dve.tensor_scalar(f, f, one_minus_lb[:, hd:hd + 1], lb[:, hd:hd + 1], ALU.mult, ALU.add)
                ins = dve.tensor_scalar(k, k, one_minus_lb[:, hd:hd + 1], None, ALU.mult)
            link(ins)
            dve.tensor_scalar(la["ln2"], la["f"], TINY, LN_EDGE, ALU.max, ALU.min)
            dve.tensor_scalar(la["f"], la["f"], LN_EDGE, None, ALU.max).then_inc(la_ln_in, 1)
            dve.wait_ge(la_ln, 1)
            dve.tensor_tensor(la["f"], la["f"], la["ln2"], ALU.add).then_inc(la_q, 1)
            dve.wait_ge(la_q, 1)
            dve.wait_ge(bias_out, 16)
            linear_attention(la, HG_HEADS, P, [col("hgrn_gate_norm")] * NK)
            out_used()
            add_product(3)
            norm("ffn_norm", 0)
            ffn(True, 0, 0)
            add_product(2)

            norm("attn_norm", 1)
            dsa = dsa_views()
            copy_products(8, 0)
            copy_products(1, 4096, (P, 2 * IDX_HEADS))
            dve.wait_ge(proj_free, 4 + 16 + 9)
            dve.tensor_scalar(words(2048, 512), words(2048, 512), 64 ** -0.5, None, ALU.mult).then_inc(at_k, 1)
            link(dve.tensor_scalar(dsa["w_scaled"], dsa["w"], IDX_HEADS ** -0.5 * 64 ** -0.5, None, ALU.mult))
            for tb in range(NTB):
                S = (tb + 1) * P
                score = dsa["score"][:, tb, 0:S]
                diag = dsa["score"][:, tb, S - P:S]
                for hd in range(IDX_HEADS):
                    n = tb * IDX_HEADS + hd
                    w = dsa["w_scaled"][:, tb * IDX_HEADS + hd:tb * IDX_HEADS + hd + 1]
                    dve.wait_ge(ix_relu, n + 1)
                    r = dsa["relu"][:, n % 2, 0:S]
                    if hd == 0:
                        dve.tensor_scalar(score, r, w, None, ALU.mult).then_inc(ix_acc, 1)
                    else:
                        dve.wait_ge(ix_acc, n)
                        dve.scalar_tensor_tensor(score, r, w, score, ALU.mult, ALU.add).then_inc(ix_acc, 1)
                dve.wait_ge(ix_acc, n + 1)
                link(dve.tensor_tensor(diag, diag, const[:, CAUSAL:CAUSAL + P], ALU.add))
                rest, src = dsa["rest"][:, 0:S], score
                for _ in range(TOP_K // 8):
                    link(dve.max(top8, src))
                    link(dve.match_replace(rest, top8, src, TAKEN))
                    src = rest
                mask = dsa["mask"][:, tb, 0:S]
                link(dve.tensor_scalar(mask, rest, TAKEN, NEG_BIG, ALU.is_gt, ALU.mult))
                diag = dsa["mask"][:, tb, S - P:S]
                link(dve.tensor_tensor(diag, diag, const[:, CAUSAL:CAUSAL + P], ALU.add))
            UNITS = NTB * ATT_HEADS

            def logits(n):
                S = (n // ATT_HEADS + 1) * P
                slot = n % 4
                dve.wait_ge(at_qk, n + 1)
                if n >= 4:
                    dve.wait_ge(at_tr, n - 3)
                link(dve.tensor_tensor_reduce(dsa["a"][:, slot, 0:S], ps[:, n % 2, 0:S], dsa["mask"][:, n // ATT_HEADS, 0:S],
                                              1.0, -3.0e38, ALU.add, ALU.max, att_max[:, slot:slot + 1]))
                dve.tensor_scalar(att_neg[:, slot:slot + 1], att_max[:, slot:slot + 1], -1.0, None, ALU.mult).then_inc(at_max, 1)

            def normalise(n):
                S = (n // ATT_HEADS + 1) * P
                slot = n % 4
                dve.wait_ge(at_exp, n + 1)
                link(dve.reciprocal(att_inv[:, slot:slot + 1], att_sum[:, slot:slot + 1]))
                a = dsa["a"][:, slot, 0:S]
                dve.tensor_scalar(a, a, att_inv[:, slot:slot + 1], None, ALU.mult).then_inc(at_p, 1)

            for n in range(UNITS + 1):
                if n < UNITS:
                    logits(n)
                if n >= 1:
                    normalise(n - 1)
            low_of_banks(4)
            out_used()
            add_product(3)
            norm("ffn_norm", 1)
            ffn(True, 1, 1)
            add_product(2)

            inverse_rms(D)
            dve.wait_ge(gain_in, want(gain_in, 16))
            for tb in range(NTB):
                dve.scalar_tensor_tensor(h[:, tb, :], h[:, tb, :], rstd[:, tb:tb + 1], gain_row, ALU.mult, ALU.mult)\
                    .then_inc(h_ready, 1)
            for l in range(2):
                norm("norm_g_2", l * 6)
                ffn(False, 0, 2 + 2 * l)
                add_normed_product(True)
                norm("norm_g_2", l * 6 + 2)
                if l == 0:
                    hyb = hyb_views()
                    pad = CONV_TAPS - 1
                    base = 4 + 16 + 9
                    copy_four(2, 0)
                    copy_products(2, 8 * 512)
                    dve.wait_ge(proj_free, base + 10)
                    dve.tensor_scalar(hyb["k_all"], hyb["k_all"], 64 ** -0.5, None, ALU.mult).then_inc(sb_k, 1)
                    dve.memset(hyb["pad"][:, :, 0:pad], 0.0)
                    dve.wait_ge(cv_sig, 1)
                    link(dve.tensor_tensor(hyb["pad"][:, :, pad:pad + SEQ], hyb["u"],
                                           hyb["gate"].rearrange("p (c t) -> p c t", t=SEQ), ALU.mult))
                    taps = [(k, c) for k in range(CONV_TAPS) for c in range(4)]

                    def convolve(n):
                        for _ in range(n):
                            if not taps:
                                return
                            k, c = taps.pop(0)
                            src, dst, w = hyb["pad"][:, c, k:k + SEQ], hyb["co"][:, c, :], col("conv_dw_w_2", k * 4 + c)
                            if k == 0:
                                dve.tensor_scalar(dst, src, w, col("conv_dw_b_2", c), ALU.mult, ALU.add).then_inc(cv_tap, 1)
                            else:
                                dve.wait_ge(cv_tap, want(cv_tap))
                                dve.scalar_tensor_tensor(dst, src, w, dst, ALU.mult, ALU.add).then_inc(cv_tap, 1)

                    def stick_softplus(hd):
                        dve.wait_ge(sb_ln, hd + 1)
                        if hd >= 2:
                            dve.wait_ge(sb_rest, hd - 1)
                        dve.scalar_tensor_tensor(hyb["sp"][:, hd % 2, :], ps[:, hd % 4, 0:3 * P], 0.0, hyb["l"][:, hd % 2, :],
                                                 ALU.max, ALU.add).then_inc(sb_sp, 1)

                    for hd in range(SB_HEADS):
                        convolve(15)
                        stick_softplus(hd)
                    convolve(len(taps))
                    low_of_banks(2)
                    dve.wait_ge(cv_tap, 4 * CONV_TAPS)
                    dve.wait_ge(cv_turn, 1)
                    for tb in range(NTB):
                        ins = dve.bn_stats(ln_stats[:, 6 * tb:6 * tb + 6], ps[:, 6 + tb, :])
                    link(ins)
                    for tb in range(NTB):
                        ins = dve.bn_aggr(ln_mv[:, 2 * tb:2 * tb + 2], ln_stats[:, 6 * tb:6 * tb + 6])
                    link(ins)
                    var = ln_mv.rearrange("p (b s) -> p b s", s=2)[:, :, 1]
                    dve.tensor_scalar(var, var, EPS, None, ALU.add).then_inc(cv_ms, 1)
                    dve.wait_ge(cv_std, 1)
                    link(dve.reciprocal(ln_rstd, ln_std))
                    for tb in range(NTB):
                        dve.tensor_scalar(xn[:, tb, 0:512], ps[:, 6 + tb, :], ln_mv[:, 2 * tb:2 * tb + 1], ln_rstd[:, tb:tb + 1],
                                          ALU.subtract, ALU.mult).then_inc(cv_norm, 1)
                    for c in range(4):
                        dve.wait_ge(x_hi_done, want(x_hi_done))
                        dve.tensor_tensor(x_lo[:, 4 + c, :], hyb["cs"][:, c, :], x_hi[:, 4 + c, :].bitcast(F32), ALU.subtract)\
                            .then_inc(x_ready, 1)
                else:
                    la = gla_views()
                    base = 4 + 16 + 9 + 10
                    copy_four(3, 0)
                    copy_products(1, 12 * 512, (GATE_RANK, SEQ))
                    dve.wait_ge(proj_free, base + 13)
                    dve.tensor_scalar(la["q"], la["q"], P ** -0.5, None, ALU.mult).then_inc(la_q, 1)
                    dve.wait_ge(gate_ln, 1)
                    link(dve.scalar_tensor_tensor(la["x"], la["x"], 0.0, la["e"], ALU.min, ALU.subtract))
                    link(dve.tensor_scalar(la["x"], la["x"], 1.0 / GLA_TAU, None, ALU.mult))
                    linear_attention(la, GLA_HEADS, SLAB, [col("gla_norm_g_2", c % 2) for c in range(NK)])
                out_used()
                add_normed_product(False)
                norm("norm_g_2", l * 6 + 4)
                ffn(False, 0, 3 + 2 * l)
                add_normed_product(True)

        @block.tensor
        def _(pe):
            used, want = [0] * RING, Tally()
            products = 0

            def three(out_ap, a, b, start, stop):
                (a_hi, a_lo), (b_hi, b_lo) = a, b
                pe.matmul(out_ap, a_hi, b_hi, start=start, stop=False, skip_group_check=True)
                pe.matmul(out_ap, a_hi, b_lo, start=False, stop=False, skip_group_check=True)
                return pe.matmul(out_ap, a_lo, b_hi, start=False, stop=stop, skip_group_check=True)

            def weights(s, a, n):
                return w_hi[s][:, a:a + n], w_lo[s][:, a:a + n]

            def acts(k, a=0, n=SEQ):
                return x_hi[:, k, a:a + n], x_lo[:, k, a:a + n]

            def features(s, bank, a, n, at):
                for k in range(NK):
                    ins = three(ps[0:n, bank, at:at + SEQ], weights(s, k * SLAB + a, n), acts(k), k == 0, k == NK - 1)
                return ins

            def tokens(s, bank, a, n, at):
                for tb in range(NTB):
                    for k in range(NK):
                        ins = three(ps[:, bank, at + tb * n:at + tb * n + n], acts(k, tb * P, P), weights(s, k * SLAB + a, n),
                                    k == 0, k == NK - 1)
                return ins

            def feature_slab(s):
                features(s, 4 + s, 0, P, 0)
                return features(s, 4 + s, P, P, SEQ)

            def token_slab(s):
                return tokens(s, 4 + s, 0, SLAB, 0)

            def project_four(how, n):
                nonlocal products
                with pe.Fori(0, n) as i:
                    for s in range(RING):
                        pe.wait_ge(slab_ready[s], i + (used[s] + 2))
                        pe.wait_ge(proj_free, i * RING + (products + s + 1))
                        how(s).then_inc(slab_used[s], 1)
                for s in range(RING):
                    used[s] += n
                products += n * RING

            def project(how, s):
                nonlocal products
                pe.wait_ge(slab_ready[s], used[s] + 2)
                pe.wait_ge(proj_free, products + 1)
                how(s).then_inc(slab_used[s], 1)
                used[s] += 1
                products += 1

            def x_split(n=NK):
                pe.wait_ge(x_ready, want(x_ready, n))

            def turn(from_banks=False):
                if from_banks:
                    pe.wait_ge(xn_ready, want(xn_ready, NTB))
                for tb in range(NTB):
                    if not from_banks:
                        pe.wait_ge(xn_ready, want(xn_ready))
                    for c in range(NK):
                        at = c % 2 * SEQ + tb * P
                        ins = pe.transpose(ps[:, 4 + c // 2, at:at + P], xn[:, tb, c * P:c * P + P], ident)
                        if tb == NTB - 1 and c % 2 == 1:
                            ins.then_inc(turned, 1)

            def project_out():
                for s in range(RING):
                    pe.wait_ge(slab_ready[s], used[s] + 2)
                    for kk in range(2):
                        k = 2 * s + kk
                        for tb in range(NTB):
                            for half in range(2):
                                ins = three(ps[:, 2 * tb + half, :], acts(k, tb * P, P), weights(s, kk * D + half * 512, 512),
                                            k == 0, k == NK - 1)
                    ins.then_inc(slab_used[s], 1)
                    used[s] += 1

            def ffn(f):
                q0 = f * NF
                x_split()
                z = zeros.bitcast(BF16)
                for bank in range(4):
                    pe.matmul(ps[:, bank, :], z[:, 0:P], z[:, 0:512], start=True, stop=False, skip_group_check=True)

                def up(i, ahead):
                    pe.wait_ge(slab_ready[0], i + (used[0] + 2 + ahead))
                    for b in range(2):
                        pe.wait_ge(gt_done[b], i + (q0 + 1 + ahead))
                        ins = features(0, 4 + b, b * P, P, 0)
                    ins.then_inc(slab_used[0], 1)
                    pe.wait_ge(slab_ready[1], i + (used[1] + 2 + ahead))
                    features(1, 4, 0, P, SEQ).then_inc(up_half, 1)
                    features(1, 5, P, P, SEQ).then_inc(slab_used[1], 1)

                def down(i):
                    pe.wait_ge(slab_ready[2], i + (used[2] + 2))
                    pe.wait_ge(g_ready, i * 2 + (2 * q0 + 2))
                    for b in range(2):
                        for tb in range(NTB):
                            for half in range(2):
                                a = (g_hi[:, b, tb * P:tb * P + P], g_lo[:, b, tb * P:tb * P + P])
                                ins = three(ps[:, 2 * tb + half, :], a, weights(2, b * D + half * 512, 512), False, False)
                    ins.then_inc(slab_used[2], 1)

                up(0, 0)
                with pe.Fori(0, NF - 1) as i:
                    up(i, 1)
                    down(i)
                down(NF - 1)
                for s in range(3):
                    used[s] += NF

            def linear_attention(la, H, dv):
                banks = H // 2

                def scores(n, k, q):
                    ins = pe.matmul(ps[:, n // 4, n % 4 * P:n % 4 * P + P], k, q, start=True, stop=True, skip_group_check=True)
                    if n % 4 == 3:
                        ins.then_inc(la_scores, 1)

                def block_scores(k, q):
                    for n in range(2 * H):
                        scores(n, k[:, n * P:n * P + P], q[:, n * P:n * P + P])

                pe.wait_ge(la_q, want(la_q))
                block_scores(la["k"], la["q"])
                for m in LEVELS:
                    pe.wait_ge(la_factors, want(la_factors))
                    pe.wait_ge(la_masked, want(la_masked))
                    block_scores(la["kt"], la["qt"])
                pe.wait_ge(la_factors, want(la_factors))
                pe.wait_ge(la_masked, want(la_masked))
                for hd in range(H):
                    a = hd * SEQ
                    scores(hd, la["kt"][:, a:a + P], la["qt"][:, a + P:a + SEQ])
                pe.wait_ge(la_cross, want(la_cross))
                for hd in range(H):
                    c = hd * dv
                    for tb in range(NTB):
                        o = ps[:, 4 + 2 * tb + c // 512, c % 512:c % 512 + dv]
                        n = 2 * hd + tb
                        ins = pe.matmul(o, la["scores"][:, n * P:n * P + P], v_of(la, tb, hd, dv), start=True, stop=tb == 0,
                                        skip_group_check=True)
                        if tb == 1:
                            ins = pe.matmul(o, la["cross"][:, hd * P:hd * P + P], v_of(la, 0, hd, dv), start=False, stop=True,
                                            skip_group_check=True)
                ins.then_inc(la_out, 1)

            n_small = 3 + len(row_src) + 1
            pe.wait_ge(const_in, 16 * n_small)
            for t in range(n_row_tiles):
                k = min(P, n_rows - t * P)
                ins = pe.transpose(ps[:, t // 4, t % 4 * P:t % 4 * P + k], rows[0:k, t, :], ident[0:k, 0:k])
            ins.then_inc(rows_turned, 1)
            pe.matmul(ps[0:ATT_HEADS, 2, 0:DISTS], rel_bias_sb[0:BUCKETS, :], const[0:BUCKETS, ONEHOT:ONEHOT + DISTS],
                      start=True, stop=True).then_inc(bias_vec_done, 1)

            turn()
            x_split()
            project_four(feature_slab, 2)
            project_four(token_slab, 2)
            la = hgrn_views()
            linear_attention(la, HG_HEADS, P)
            turn(from_banks=True)
            x_split()
            project_out()
            turn()
            ffn(0)

            turn()
            x_split()
            project_four(feature_slab, 1)
            for s in range(3):
                project(feature_slab, s)

            def index_keys_and_values(s):
                features(s, 4 + s, 0, P, 0)
                return tokens(s, 4 + s, P, P, SEQ)

            project(index_keys_and_values, 3)
            project(lambda s: tokens(s, 4 + s, 0, IDX_HEADS, 0), 0)
            dsa = dsa_views()
            pe.wait_ge(proj_free, 4 + 16 + 9)
            for tb in range(NTB):
                S = (tb + 1) * P
                for hd in range(IDX_HEADS):
                    n = tb * IDX_HEADS + hd
                    a = hd % 2 * 64
                    if n >= 4:
                        pe.wait_ge(ix_relu, n - 3)
                    pe.matmul(ps[:, n % 4, 0:S], dsa["qi"][a:a + 64, hd // 2, tb * P:tb * P + P], dsa["ki"][a:a + 64, 0:S],
                              start=True, stop=True).then_inc(ix_dots, 1)
            UNITS = NTB * ATT_HEADS
            pe.wait_ge(at_k, 1)
            pe.wait_ge(bias_in, 16)
            pe.wait_ge(ix_relu, NTB * IDX_HEADS)

            def queries_keys(n):
                tb, hd = divmod(n, ATT_HEADS)
                S = (tb + 1) * P
                a = hd % 2 * 64
                if n >= 2:
                    pe.wait_ge(at_max, n - 1)
                pe.matmul(ps[:, n % 2, 0:S], dsa["q"][a:a + 64, hd // 2, tb * P:tb * P + P],
                          dsa["k"][a:a + 64, hd // (ATT_HEADS // 2), 0:S], start=True, stop=False, skip_group_check=True)
                c = (1 - tb) * P
                pe.matmul(ps[:, n % 2, 0:S], ident, bias_x[:, hd, c:c + S], start=False, stop=True, skip_group_check=True)\
                    .then_inc(at_qk, 1)

            def turn_probs(n):
                tb = n // ATT_HEADS
                pe.wait_ge(at_p, n + 1)
                if n >= 2:
                    pe.wait_ge(at_pt, n - 1)
                for sb_ in range(tb + 1):
                    ins = pe.transpose(ps[:, 2 + n % 2, sb_ * P:sb_ * P + P], dsa["a"][:, n % 4, sb_ * P:sb_ * P + P], ident)
                ins.then_inc(at_tr, 1)

            def values(n):
                tb, hd = divmod(n, ATT_HEADS)
                pe.wait_ge(at_pt, n + 1)
                a, c = hd % 2 * 64, hd // 2
                kv = hd // (ATT_HEADS // 2) * 64
                o = ps[a:a + 64, 4 + c // 2, c % 2 * SEQ + tb * P:c % 2 * SEQ + tb * P + P]
                for sb_ in range(tb + 1):
                    ins = pe.matmul(o, dsa["v"][:, sb_, kv:kv + 64], dsa["pt"][:, n % 2, sb_ * P:sb_ * P + P],
                                    start=sb_ == 0, stop=sb_ == tb, skip_group_check=True)
                ins.then_inc(at_pv, 1)

            for n in range(UNITS + 3):
                if n < UNITS:
                    queries_keys(n)
                if 2 <= n < UNITS + 2:
                    turn_probs(n - 2)
                if n >= 3:
                    values(n - 3)
            x_split(4)
            project_out()
            turn()
            ffn(1)

            for l in range(2):
                turn()
                ffn(2 + 2 * l)
                turn()
                x_split()
                if l == 0:
                    hyb = hyb_views()
                    project_four(feature_slab, 2)
                    project(token_slab, 0)
                    project(token_slab, 1)
                    pe.wait_ge(sb_k, 1)

                    def stick_logits(hd):
                        a, c = hd % 2 * 64, hd // 2
                        q, k = hyb["q"][a:a + 64, c, :], hyb["k"][a:a + 64, c, :]
                        bank = ps[:, hd % 4, :]
                        if hd >= 4:
                            pe.wait_ge(sb_w, hd - 3)
                        pe.matmul(bank[:, 0:SEQ], k[:, 0:P], q, start=True, stop=False, skip_group_check=True)
                        pe.matmul(bank[:, SEQ:SEQ + P], k[:, P:SEQ], q[:, P:SEQ], start=False, stop=False, skip_group_check=True)
                        for c0 in (0, SEQ):
                            ins = pe.matmul(bank[:, c0:c0 + P], ident, const[:, STRICT:STRICT + P], start=False, stop=False,
                                            skip_group_check=True)
                        ins.then_inc(sb_z, 1)

                    def stick_rest(hd):
                        pe.wait_ge(sb_sp, hd + 1)
                        bank, sp_ = ps[:, hd % 4, :], hyb["sp"][:, hd % 2, :]
                        tri, minus = const[:, TRI:TRI + P], const[:, ONES:ONES + P]
                        pe.matmul(bank[:, 0:SEQ], tri, sp_[:, 0:SEQ], start=False, stop=False, skip_group_check=True)
                        pe.matmul(bank[:, P:SEQ], minus, sp_[:, SEQ:3 * P], start=False, stop=False, skip_group_check=True)
                        pe.matmul(bank[:, SEQ:3 * P], tri, sp_[:, SEQ:3 * P], start=False, stop=True, skip_group_check=True)\
                            .then_inc(sb_rest, 1)

                    def stick_values(hd):
                        pe.wait_ge(sb_w, hd + 1)
                        a, c = hd % 2 * 64, hd // 2
                        w = hyb["w"][:, hd % 2, :]
                        o = ps[a:a + 64, 4 + c // 2, c % 2 * SEQ:c % 2 * SEQ + SEQ]
                        v0, v1 = v_of(hyb, 0, hd, 64), v_of(hyb, 1, hd, 64)
                        pe.matmul(o[:, 0:P], v0, w[:, 0:P], start=True, stop=True, skip_group_check=True)
                        pe.matmul(o[:, P:SEQ], v0, w[:, P:SEQ], start=True, stop=False, skip_group_check=True)
                        pe.matmul(o[:, P:SEQ], v1, w[:, SEQ:3 * P], start=False, stop=True, skip_group_check=True)\
                            .then_inc(sb_pv, 1)

                    for hd in range(SB_HEADS + 2):
                        if hd < SB_HEADS:
                            stick_logits(hd)
                        if 1 <= hd < SB_HEADS + 1:
                            stick_rest(hd - 1)
                        if hd >= 2:
                            stick_values(hd - 2)
                    pe.wait_ge(cv_tap, 4 * CONV_TAPS)
                    for tb in range(NTB):
                        for c in range(4):
                            ins = pe.transpose(ps[:, 6 + tb, c * P:c * P + P], hyb["co"][:, c, tb * P:tb * P + P], ident)
                    ins.then_inc(cv_turn, 1)
                    pe.wait_ge(cv_norm, NTB)
                    for c in range(4):
                        for tb in range(NTB):
                            at = c % 2 * SEQ + tb * P
                            ins = pe.transpose(ps[:, 2 + c // 2, at:at + P], xn[:, tb, c * P:c * P + P], ident)
                        if c % 2 == 1:
                            ins.then_inc(cv_back, 1)
                    x_split(6)
                else:
                    la = gla_views()
                    project_four(feature_slab, 1)
                    project_four(token_slab, 2)
                    project(lambda s: features(s, 4 + s, 0, GATE_RANK, 0), 0)
                    pe.wait_ge(gate_in, 16)
                    pe.wait_ge(proj_free, 4 + 16 + 9 + 10 + 13)
                    for c in range(4):
                        ins = pe.matmul(ps[:, c // 2, c % 2 * SEQ:c % 2 * SEQ + SEQ], w_gate[0:GATE_RANK, c * P:c * P + P],
                                        la["rank"], start=True, stop=True, skip_group_check=True)
                    ins.then_inc(gate_mm, 1)
                    pe.wait_ge(gate_x, 1)
                    linear_attention(la, GLA_HEADS, SLAB)
                    turn(from_banks=True)
                    x_split()
                project_out()
                turn()
                ffn(3 + 2 * l)


_INS = ["x", "attn_norm", "ffn_norm", "hgrn_w_in", "hgrn_w_out", "hgrn_gate_norm", "hgrn_lower_bounds", "dsa_w_in",
        "dsa_w_out", "rel_bias", "ffn_w_up", "ffn_conv_w", "ffn_conv_b", "ffn_w_down", "final_norm", "norm_g_2",
        "ffn1_w_in_2", "ffn1_w_out_2", "ffn2_w_in_2", "ffn2_w_out_2", "hyb_w_in_2", "hyb_w_out_2", "conv_dw_w_2",
        "conv_dw_b_2", "conv_ln_g_2", "conv_ln_b_2", "gla_w_in_2", "gla_w_gate_2", "gla_b_gate_2", "gla_norm_g_2",
        "gla_w_out_2"]


def kernel(**inputs):
    import concourse.bacc as bacc
    from concourse.bass_utils import run_bass_kernel_spmd as run

    nc = bacc.Bacc("TRN2", target_bir_lowering=False, num_devices=1)
    shape_const, level_masks = shape_constants()
    arrays = {name: np.ascontiguousarray(inputs[name]) for name in _INS}
    arrays["shape_const"] = shape_const
    arrays["level_masks"] = level_masks
    A = {name: nc.dram_tensor("in_" + name, a.shape, mybir.dt.from_np(a.dtype), kind="ExternalInput").ap()
         for name, a in arrays.items()}
    out = nc.dram_tensor("out_0", (1, SEQ, D), F32, kind="ExternalOutput").ap()
    build(nc, A, out)
    r = run(nc, [{"in_" + name: a for name, a in arrays.items()}], core_ids=[0])
    return r.results[0]["out_0"]
```

```python
from contextlib import ExitStack
import math

import numpy as np
import concourse.bass as bass
from concourse import mybir

F32 = mybir.dt.float32
F32R = mybir.dt.float32r
BF16 = mybir.dt.bfloat16
U8 = mybir.dt.uint8
ALU = mybir.AluOpType
ACT = mybir.ActivationFunctionType
AX_X = mybir.AxisListType.X

P = 128
D = 1024
SEQ = 256
NTB = SEQ // P
NK = D // P
FF = 2816
SLAB = 256
NF = FF // SLAB
RING = 4
EPS = 1e-6
NEG_BIG = -1e30
TAKEN = -3e38
TINY = 1e-30
LN_EDGE = 2.0 ** -60

HG_HEADS = 8
GLA_HEADS = 4
ATT_HEADS = 16
IDX_HEADS = 8
TOP_K = 64
SB_HEADS = 8
CONV_TAPS = 31
GATE_RANK = 16
GLA_TAU = 16.0
BUCKETS = 32
MAX_DIST = 128
LEVELS = [64, 32, 16, 8, 4, 2, 1]
DISTS = 3 * P

IDENT, CAUSAL, STRICT, TRI, ONES, ONEHOT, ZEROS = 0, 128, 256, 384, 512, 640, 1024
CONST_COLS = ZEROS + 512


def shape_constants():
    c = np.zeros((P, CONST_COLS), np.float32)
    i = np.arange(P)
    row, col = i[:, None], i[None, :]
    c[:, IDENT:IDENT + P] = np.eye(P)
    c[:, CAUSAL:CAUSAL + P] = np.where(col > row, NEG_BIG, 0.0)
    c[:, STRICT:STRICT + P] = np.where(row >= col, NEG_BIG, 0.0)
    c[:, TRI:TRI + P] = np.where(row >= col, -1.0, 0.0)
    c[:, ONES:ONES + P] = -1.0
    dist = np.maximum(255 - np.arange(DISTS), 0)
    exact = BUCKETS // 2
    far = np.maximum(dist, exact).astype(np.float32)
    large = exact + (np.log(far / np.float32(exact)) / np.float32(math.log(MAX_DIST / exact))
                     * np.float32(BUCKETS - exact)).astype(np.int32)
    bucket = np.where(dist < exact, dist, np.minimum(large, BUCKETS - 1))
    c[bucket, ONEHOT + np.arange(DISTS)] = 1.0
    masks = np.zeros((P, len(LEVELS), P), np.float32)
    for n, m in enumerate(LEVELS):
        same = row // (2 * m) == col // (2 * m)
        masks[:, n] = same & (row // m % 2 == 0) & (col // m % 2 == 1)
    return c, masks


class Tally:

    def __init__(self):
        self.n = {}

    def __call__(self, sem, more=1):
        self.n[sem] = self.n.get(sem, 0) + more
        return self.n[sem]


class Uses:

    def __init__(self):
        self.uses = [0] * RING
        self.dmas = [0] * RING

    def take(self, slot, dmas=1):
        u = self.uses[slot]
        self.uses[slot] += 1
        self.dmas[slot] += 16 * dmas
        return u, self.dmas[slot]

    def skip(self, slot, n):
        self.uses[slot] += n
        self.dmas[slot] += 16 * n


def build(nc, A, out):
    with ExitStack() as ctx:
        def sb(name, shape, dt=F32):
            return ctx.enter_context(nc.sbuf_tensor(name, shape, dt))

        def sem(name):
            return ctx.enter_context(nc.semaphore(name))

        raw = [sb(f"raw{s}", [P, 2048]) for s in range(RING)]
        w_hi = [sb(f"w_hi{s}", [P, 2048], F32R) for s in range(RING)]
        w_lo = [sb(f"w_lo{s}", [P, 2048], F32R) for s in range(RING)]
        h = sb("h", [P, NTB, D])
        x_hi = sb("x_hi", [P, NK, SEQ], F32R)
        x_lo = sb("x_lo", [P, NK, SEQ], F32R)
        xn = sb("xn", [P, NTB, D])
        g_hi = sb("g_hi", [P, 2, SEQ], F32R)
        g_lo = sb("g_lo", [P, 2, SEQ], F32R)
        const = sb("const", [P, CONST_COLS])
        level_mask = sb("level_mask", [P, len(LEVELS), P], U8)
        cols = sb("cols", [P, 640])
        small = sb("small", [P, 160])
        arena = sb("arena", [P, 16384])
        ps = ctx.enter_context(nc.psum_tensor("ps", [P, 8, 512], F32))
        bias_dram = nc.dram_tensor("bias_rows", (ATT_HEADS, P, DISTS), F32, kind="Internal").ap()

        ident = const[:, IDENT:IDENT + P]
        zeros = const[:, ZEROS:ZEROS + 512]
        ssq = small[:, 0:2]
        ms = small[:, 2:4]
        std = small[:, 4:6]
        rstd = small[:, 6:8]
        head_ssq = small[:, 8:24]
        head_ms = small[:, 24:40]
        head_std = small[:, 40:56]
        head_rstd = small[:, 56:72]
        lb = small[:, 72:80]
        one_minus_lb = small[:, 80:88]
        lb_a = small[:, 88:96]
        lb_b = small[:, 96:104]
        top8 = small[:, 104:112]
        att_max = small[:, 112:116]
        att_neg = small[:, 116:120]
        att_sum = small[:, 120:124]
        att_inv = small[:, 124:128]
        ln_stats = small[:, 128:140]
        ln_mv = small[:, 140:144]
        ln_std = small[:, 144:146]
        ln_rstd = small[:, 146:148]

        def words(a, n):
            return arena[:, a:a + n]

        proj = words(0, 16 * 512).rearrange("p (s n) -> p s n", n=512)
        ff_c = words(0, 1024).rearrange("p (b g t) -> p b g t", b=2, g=2)
        ff_s = words(1024, 512).rearrange("p (b t) -> p b t", b=2)
        ff_g = words(1536, 512).rearrange("p (b t) -> p b t", b=2)
        gain_row = words(15360, 1024)
        bias_x = words(8192, 16 * 256).rearrange("p (h c) -> p h c", h=ATT_HEADS)

        row_of, row_src, n_rows = {}, [], 0
        for name, src in [
            ("attn_norm", A["attn_norm"].rearrange("l (c p) -> (l c) p", p=P)),
            ("ffn_norm", A["ffn_norm"].rearrange("l (c p) -> (l c) p", p=P)),
            ("hgrn_gate_norm", A["hgrn_gate_norm"]),
            ("hgrn_lower_bounds", A["hgrn_lower_bounds"].rearrange("l (c p) -> (l c) p", p=P)),
            ("norm_g_2", A["norm_g_2"].rearrange("l g (c p) -> (l g c) p", p=P)),
            ("ffn_conv_w", A["ffn_conv_w"].rearrange("l k (c p) -> (l k c) p", p=P)),
            ("ffn_conv_b", A["ffn_conv_b"].rearrange("l (c p) -> (l c) p", p=P)),
            ("conv_dw_w_2", A["conv_dw_w_2"].rearrange("l k (c p) -> (l k c) p", p=P)),
            ("conv_dw_b_2", A["conv_dw_b_2"].rearrange("l (c p) -> (l c) p", p=P)),
            ("conv_ln_g_2", A["conv_ln_g_2"].rearrange("l (c p) -> (l c) p", p=P)),
            ("conv_ln_b_2", A["conv_ln_b_2"].rearrange("l (c p) -> (l c) p", p=P)),
            ("gla_b_gate_2", A["gla_b_gate_2"].rearrange("l (c p) -> (l c) p", p=P)),
            ("gla_norm_g_2", A["gla_norm_g_2"].rearrange("l (c p) -> (l c) p", p=P)),
        ]:
            row_of[name] = n_rows
            done, n = 0, src.shape[0]
            while done < n:
                k = min(n - done, P - n_rows % P)
                row_src.append((n_rows % P, n_rows // P, k, src[done:done + k, :]))
                done += k
                n_rows += k
        n_row_tiles = -(-n_rows // P)
        rows = words(0, n_row_tiles * P).rearrange("p (t n) -> p t n", n=P)
        masks_in = words(1024, len(LEVELS) * P).rearrange("p (l n) -> p l n", n=P)
        rel_bias_sb = words(15360, ATT_HEADS)
        bias_vec = words(15488, DISTS)
        w_gate = words(14336, 512)

        def col(name, i=0):
            c = row_of[name] + i
            return cols[:, c:c + 1]

        raw_full = [sem(f"raw_full{s}") for s in range(RING)]
        hi_done = [sem(f"hi_done{s}") for s in range(RING)]
        slab_ready = [sem(f"slab_ready{s}") for s in range(RING)]
        slab_used = [sem(f"slab_used{s}") for s in range(RING)]
        seeded = sem("seeded")
        const_in = sem("const_in")
        rows_turned, cols_ready = sem("rows_turned"), sem("cols_ready")
        lb_step = sem("lb_step")
        bias_vec_done, bias_vec_copied, bias_out, bias_in = (
            sem("bias_vec_done"), sem("bias_vec_copied"), sem("bias_out"), sem("bias_in"))
        gain_in, gate_in = sem("gain_in"), sem("gate_in")
        h_ready = sem("h_ready")
        rms_sq, rms_ms, rms_std = sem("rms_sq"), sem("rms_ms"), sem("rms_std")
        xn_ready, turned, x_hi_done, x_ready = sem("xn_ready"), sem("turned"), sem("x_hi_done"), sem("x_ready")
        proj_free = [sem(f"proj_free{s}") for s in range(RING)]
        up_half = sem("up_half")
        half_done = sem("half_done")
        conv_in = [sem(f"conv_in{b}") for b in range(2)]
        tap_done = [sem(f"tap_done{b}") for b in range(2)]
        conv_done = [sem(f"conv_done{b}") for b in range(2)]
        silu_done = [sem(f"silu_done{b}") for b in range(2)]
        gt_done = [sem(f"gt_done{b}") for b in range(2)]
        gt_hi = [sem(f"gt_hi{b}") for b in range(2)]
        g_ready = sem("g_ready")
        dve_step = sem("dve_step")
        act_step = sem("act_step")
        la_gate, la_ln_in, la_ln, la_k = sem("la_gate"), sem("la_ln_in"), sem("la_ln"), sem("la_k")
        la_diff, la_exp, la_factors, la_scores = sem("la_diff"), sem("la_exp"), sem("la_factors"), sem("la_scores")
        la_masked, la_cross = sem("la_masked"), sem("la_cross")
        la_out, la_sq, la_ms, la_std, la_silu = sem("la_out"), sem("la_sq"), sem("la_ms"), sem("la_std"), sem("la_silu")
        la_q = sem("la_q")
        gate_rank, gate_mm, gate_x, gate_ln = sem("gate_rank"), sem("gate_mm"), sem("gate_x"), sem("gate_ln")
        ix_dots, ix_relu, ix_acc = sem("ix_dots"), sem("ix_relu"), sem("ix_acc")
        at_k, at_qk, at_max, at_exp, at_p, at_tr, at_pt, at_pv = (
            sem("at_k"), sem("at_qk"), sem("at_max"), sem("at_exp"), sem("at_p"), sem("at_tr"), sem("at_pt"), sem("at_pv"))
        at_bank = sem("at_bank")
        sb_k, sb_z, sb_ln, sb_sp, sb_rest, sb_w, sb_pv = (
            sem("sb_k"), sem("sb_z"), sem("sb_ln"), sem("sb_sp"), sem("sb_rest"), sem("sb_w"), sem("sb_pv"))
        cv_sig, cv_pad, cv_tap, cv_turn, cv_ms, cv_std, cv_norm, cv_back, cv_silu = (
            sem("cv_sig"), sem("cv_pad"), sem("cv_tap"), sem("cv_turn"), sem("cv_ms"), sem("cv_std"), sem("cv_norm"),
            sem("cv_back"), sem("cv_silu"))
        stored = sem("stored")

        block = ctx.enter_context(nc.Block())

        def col_slab(w, c0, n=SLAB):
            return w[:, bass.ds(c0, n)].rearrange("(c p) n -> p c n", p=P)

        def row_slab(w, r0):
            return w[bass.ds(r0, SLAB), :].rearrange("(c p) n -> p c n", p=P)

        def raw_cols(s, a=0, n=SLAB):
            return raw[s][:, :].rearrange("p (c n) -> p c n", c=NK)[:, :, a:a + n]

        def raw_rows(s):
            return raw[s][:, :].rearrange("p (c n) -> p c n", c=2)

        ffn_w = [(A["ffn_w_up"][l], A["ffn_w_down"][l]) for l in range(2)]
        ffn1_w = [(A["ffn1_w_in_2"][l], A["ffn1_w_out_2"][l]) for l in range(2)]
        ffn2_w = [(A["ffn2_w_in_2"][l], A["ffn2_w_out_2"][l]) for l in range(2)]
        FFNS = [ffn_w[0], ffn_w[1], ffn1_w[0], ffn2_w[0], ffn1_w[1], ffn2_w[1]]
        hgrn_in, hgrn_out = A["hgrn_w_in"][0], A["hgrn_w_out"][0]
        dsa_in, dsa_out = A["dsa_w_in"][0], A["dsa_w_out"][0]
        hyb_in, hyb_out = A["hyb_w_in_2"][0], A["hyb_w_out_2"][0]
        gla_in, gla_out = A["gla_w_in_2"][0], A["gla_w_out_2"][0]
        DSA_K, DSA_V, DSA_QI, DSA_KI, DSA_W = 1024, 1152, 1280, 1792, 1856

        def hgrn_views():
            return dict(
                q=words(0, 2048), f=words(2048, 2048), v=proj[:, 8:12, :], gate=words(6144, 2048),
                k=words(8192, 2048), b=words(10240, 2048), qt=words(12288, 2048), ln2=words(12288, 2048),
                kt=xn[:, :, :].rearrange("p b n -> p (b n)"), scores=words(14336, 2048),
                e=words(2048, 2048), cross=words(2048, 1024), sq=[words(10240, 1024), words(11264, 1024)])

        def gla_views():
            return dict(
                q=words(0, 1024), k=words(1024, 1024), v=proj[:, 4:8, :], gate=words(4096, 2048),
                x=words(6656, 1024), f=words(6656, 1024), b=words(8704, 1024), e=words(9728, 1024),
                qt=words(10752, 1024), kt=xn[:, 0, :], scores=words(12800, 1024), cross=words(13824, 512),
                sq=[words(6656, 1024), words(7680, 1024)], rank=proj[0:GATE_RANK, 12, 0:SEQ])

        def dsa_views():
            return dict(
                q=words(0, 2048).rearrange("p (c t) -> p c t", t=SEQ), k=words(2048, 512).rearrange("p (c t) -> p c t", t=SEQ),
                qi=words(2560, 1024).rearrange("p (c t) -> p c t", t=SEQ), ki=words(3584, SEQ),
                v=words(3584 + SEQ, SEQ).rearrange("p (b n) -> p b n", b=NTB), w=words(4096, 16),
                w_scaled=words(4112, 16), relu=words(4608, 512).rearrange("p (b s) -> p b s", b=2),
                score=words(5120, 512).rearrange("p (b s) -> p b s", b=2), rest=words(5632, SEQ),
                mask=words(6144, 512).rearrange("p (b s) -> p b s", b=2),
                a=words(6656, 1024).rearrange("p (b s) -> p b s", b=4), pt=words(7680, 512).rearrange("p (b s) -> p b s", b=2))

        def hyb_views():
            return dict(
                q=words(0, 1024).rearrange("p (c t) -> p c t", t=SEQ), k_all=words(1024, 1024),
                k=words(1024, 1024).rearrange("p (c t) -> p c t", t=SEQ),
                u=words(2048, 1024).rearrange("p (c t) -> p c t", t=SEQ), gate=words(3072, 1024),
                v=proj[:, 8:10, :], pad=words(5120, 4 * (SEQ + CONV_TAPS - 1)).rearrange("p (c t) -> p c t", c=4),
                co=words(6400, 1024).rearrange("p (c t) -> p c t", t=SEQ), cs=words(7424, 1024).rearrange("p (c t) -> p c t", t=SEQ),
                l=words(9216, 768).rearrange("p (b n) -> p b n", b=2),
                sp=words(9984, 768).rearrange("p (b n) -> p b n", b=2), w=words(10752, 768).rearrange("p (b n) -> p b n", b=2))

        def halves(t, m):
            v = t.rearrange("p (n two m) -> p n two m", two=2, m=m)
            return v[:, :, 0, :], v[:, :, 1, :]

        def v_of(la, tb, hd, dv):
            c = hd * dv
            return la["v"][:, c // SLAB, tb * SLAB + c % SLAB:tb * SLAB + c % SLAB + dv]

        @block.sync
        def _(sp):
            ring = Uses()

            def load(slot, pieces):
                u, _ = ring.take(slot, len(pieces))
                sp.wait_ge(slab_ready[slot], u + 1)
                for dst, src in pieces:
                    sp.dma_start(dst, src).then_inc(raw_full[slot], 16)

            def load_four_columns(w, c0, n, stride=RING * SLAB):
                with sp.Fori(0, n) as i:
                    for s in range(RING):
                        sp.wait_ge(slab_ready[s], i + (ring.uses[s] + 1))
                        sp.dma_start(raw_cols(s), col_slab(w, i * stride + (c0 + s * SLAB))).then_inc(raw_full[s], 16)
                for s in range(RING):
                    ring.skip(s, n)

            def load_out(w):
                for s in range(RING):
                    load(s, [(raw_rows(s), row_slab(w, s * SLAB))])

            def load_ffn(f):
                up, down = FFNS[f]
                load(0, [(raw_cols(0), col_slab(up, 0))])
                load(1, [(raw_cols(1), col_slab(up, FF))])
                with sp.Fori(0, NF - 1) as i:
                    sp.wait_ge(slab_ready[0], i + (ring.uses[0] + 1))
                    sp.dma_start(raw_cols(0), col_slab(up, i * SLAB + SLAB)).then_inc(raw_full[0], 16)
                    sp.wait_ge(slab_ready[1], i + (ring.uses[1] + 1))
                    sp.dma_start(raw_cols(1), col_slab(up, i * SLAB + (FF + SLAB))).then_inc(raw_full[1], 16)
                    sp.wait_ge(slab_ready[2], i + (ring.uses[2] + 1))
                    sp.dma_start(raw_rows(2), row_slab(down, i * SLAB)).then_inc(raw_full[2], 16)
                for s in range(3):
                    ring.skip(s, NF - 1)
                load(3, [(raw_rows(3), row_slab(down, (NF - 1) * SLAB))])

            load_four_columns(hgrn_in, 0, 4)
            load_out(hgrn_out)
            load_ffn(0)
            for s in range(RING):
                load(s, [(raw_cols(s), col_slab(dsa_in, s * SLAB))])
            k0, k1 = (dsa_in[:, DSA_K + 64 * j:DSA_K + 64 * j + 64].rearrange("(c p) n -> p c n", p=P) for j in range(2))
            ki = dsa_in[:, DSA_KI:DSA_KI + 64].rearrange("(c p) n -> p c n", p=P)
            load(0, [(raw_cols(0, 64 * j, 64), k) for j, k in enumerate([k0, k0, k1, k1])])
            load(1, [(raw_cols(1), col_slab(dsa_in, DSA_QI))])
            load(2, [(raw_cols(2), col_slab(dsa_in, DSA_QI + SLAB))])
            load(3, [(raw_cols(3, 0, 64), ki), (raw_cols(3, 64, 64), ki), (raw_cols(3, P, P), col_slab(dsa_in, DSA_V, P))])
            load(0, [(raw_cols(0, 0, IDX_HEADS), col_slab(dsa_in, DSA_W, IDX_HEADS))])
            load_out(dsa_out)
            load_ffn(1)
            load_ffn(2)
            load_four_columns(hyb_in, 0, 2, stride=6 * SLAB)
            for s in range(2):
                load(s, [(raw_cols(s), col_slab(hyb_in, 4 * SLAB + s * SLAB))])
            load_out(hyb_out)
            load_ffn(3)
            load_ffn(4)
            load(2, [(raw_cols(2, 0, GATE_RANK), col_slab(gla_in, 12 * SLAB, GATE_RANK))])
            load_four_columns(gla_in, 0, 3)
            load_out(gla_out)
            load_ffn(5)
            sp.wait_ge(h_ready, 2 * 11)
            sp.dma_start(out[0].rearrange("(b p) d -> p b d", p=P), h[:, :, :]).then_inc(stored, 16)
            sp.wait_ge(stored, 16)

        @block.gpsimd
        def _(pool):
            ring = Uses()

            def low(slot, u):
                pool.wait_ge(hi_done[slot], u + 1)
                pool.tensor_tensor(w_lo[slot][:, :], raw[slot][:, :], w_hi[slot][:, :].bitcast(F32), ALU.subtract)\
                    .then_inc(slab_ready[slot], 1)

            def low_one(slot):
                u, _ = ring.take(slot)
                low(slot, u)

            def low_four(n):
                with pool.Fori(0, n) as i:
                    for s in range(RING):
                        low(s, i + ring.uses[s])
                for s in range(RING):
                    ring.skip(s, n)

            def low_ffn():
                low_one(0)
                low_one(1)
                with pool.Fori(0, NF - 1) as i:
                    for s in range(2):
                        low(s, i + ring.uses[s])
                for s in range(3):
                    ring.skip(s, NF - 1)
                low_one(3)

            low_four(3)
            pool.wait_ge(la_gate, 1)
            for hd in range(HG_HEADS):
                k = hgrn_views()["k"][:, hd * SEQ:hd * SEQ + SEQ]
                ins = pool.tensor_scalar(k, k, one_minus_lb[:, hd:hd + 1], None, ALU.mult)
            ins.then_inc(la_k, 1)
            low_four(2)
            low_ffn()
            low_four(2)
            low_one(0)
            low_four(1)
            low_ffn()
            low_ffn()
            low_four(2)
            low_one(0)
            low_one(1)
            low_four(1)
            low_ffn()
            low_ffn()
            low_one(2)
            low_four(4)
            low_ffn()

        @block.scalar
        def _(act):
            ring, want = Uses(), Tally()
            consts = 0
            products_done = 4
            made = [0] * RING

            def fetch(dst, src):
                nonlocal consts
                act.dma_start(dst, src).then_inc(const_in, 16)
                consts += 16

            def link(ins):
                ins.then_inc(act_step, 1)
                act.wait_ge(act_step, want(act_step))

            def high(slot, u, full):
                act.wait_ge(raw_full[slot], full)
                act.wait_ge(slab_used[slot], u + 1)
                act.activation(w_hi[slot][:, :], raw[slot][:, :], ACT.Copy).then_inc(hi_done[slot], 1)

            def high_one(slot, dmas=1):
                high(slot, *ring.take(slot, dmas))

            def high_four(n):
                with act.Fori(0, n) as i:
                    for s in range(RING):
                        high(s, i + ring.uses[s], i * 16 + (ring.dmas[s] + 16))
                for s in range(RING):
                    ring.skip(s, n)

            def all_copied():
                for s in range(RING):
                    act.wait_ge(proj_free[s], made[s] + 1)

            def evacuate(s, dst):
                act.wait_ge(slab_used[s], ring.uses[s] + 1)
                act.activation(dst, ps[:, 4 + s, :], ACT.Copy).then_inc(proj_free[s], 1)
                made[s] += 1

            def rms(src, ready):
                act.activation(small[:, 152:153], const[:, ZEROS:ZEROS + 1], ACT.Sqrt)
                for tb in range(NTB):
                    ready(tb)
                    act.activation(xn[:, tb, :], src(tb), ACT.Square, accum_out=ssq[:, tb:tb + 1]).then_inc(rms_sq, 1)
                    act.wait_ge(rms_ms, want(rms_ms))
                    act.activation(std[:, tb:tb + 1], ms[:, tb:tb + 1], ACT.Sqrt).then_inc(rms_std, 1)

            def rms_residual(updates):
                rms(lambda tb: h[:, tb, :], lambda tb: act.wait_ge(h_ready, 2 * updates - 1 + tb) if updates else None)

            def split_turned(gains):
                for c in range(NK):
                    if c % 2 == 0:
                        act.wait_ge(turned, want(turned))
                    act.activation(x_hi[:, c, :], ps[:, 4 + c // 2, c % 2 * SEQ:c % 2 * SEQ + SEQ], ACT.Copy,
                                   scale=gains[c]).then_inc(x_hi_done, 1)

            def norm(name, i, updates):
                rms_residual(updates)
                split_turned([col(name, i * NK + c) for c in range(NK)])

            def product_done(tb):
                if tb == 0:
                    act.wait_ge(half_done, products_done + 1)
                else:
                    act.wait_ge(slab_used[3], ring.uses[3] + 1)

            def rms_product():
                nonlocal products_done
                rms(lambda tb: ps[:, 2 * tb:2 * tb + 2, :].rearrange("p b n -> p (b n)"), product_done)
                products_done += 1

            def ffn(conv, f_conv, f):
                b0, b1, b2 = ring.uses[0], ring.uses[1], ring.uses[2]
                m0, m1, m2 = ring.dmas[0], ring.dmas[1], ring.dmas[2]
                q0 = f * NF

                def up_done(b, i):
                    if b == 0:
                        act.wait_ge(up_half, i + (q0 + 1))
                    else:
                        act.wait_ge(slab_used[1], i + (b1 - 1 + 2))

                def start_gate(b, i):
                    up_done(b, i)
                    bank = ps[:, 4 + b, :]
                    if conv:
                        for g in range(2):
                            c = i * 2 + (row_of["ffn_conv_w"] + f_conv * 132 + 88 + g * 22 + b)
                            cb = i * 2 + (row_of["ffn_conv_b"] + f_conv * 44 + g * 22 + b)
                            ins = act.activation(ff_c[:, b, g, :], bank[:, g * SEQ:g * SEQ + SEQ], ACT.Identity,
                                                 bias=cols[:, bass.ds(cb, 1)], scale=cols[:, bass.ds(c, 1)])
                        ins.then_inc(conv_in[b], 1)
                    else:
                        act.activation(ff_s[:, b, :], bank[:, 0:SEQ], ACT.Silu).then_inc(silu_done[b], 1)

                def conv_silu(b, i):
                    act.wait_ge(conv_done[b], i + (f_conv * NF + 1))
                    act.activation(ff_s[:, b, :], ff_c[:, b, 0, :], ACT.Silu).then_inc(silu_done[b], 1)

                def split(b, i):
                    act.wait_ge(gt_done[b], i + (q0 + 2))
                    if b == 0:
                        act.wait_ge(slab_used[2], i + (b2 + 1))
                    act.activation(g_hi[:, b, :], ff_g[:, b, :], ACT.Copy).then_inc(gt_hi[b], 1)

                def body(i, last):
                    if last:
                        high_one(3)
                    else:
                        high(0, i + b0, i * 16 + (m0 + 16))
                    start_gate(0, i)
                    start_gate(1, i)
                    if conv:
                        conv_silu(0, i)
                    if not last:
                        high(1, i + b1, i * 16 + (m1 + 16))
                    if conv:
                        conv_silu(1, i)
                    split(0, i)
                    split(1, i)
                    if not last:
                        high(2, i + b2, i * 16 + (m2 + 16))

                with act.Fori(0, NF - 1) as i:
                    body(i, False)
                body(NF - 1, True)
                for s in range(3):
                    ring.skip(s, NF - 1)

            fetch(h[:, :, :], A["x"][0].rearrange("(b p) d -> p b d", p=P))
            fetch(const[:, :], A["shape_const"])
            fetch(masks_in, A["level_masks"])
            for p0, t, k, src in row_src:
                fetch(rows[p0:p0 + k, t, :], src)
            fetch(rel_bias_sb[0:BUCKETS, :], A["rel_bias"])
            high_one(0)
            act.wait_ge(const_in, consts)
            act.wait_ge(rows_turned, 1)
            act.activation(cols[:, 0:n_rows], ps[:, 0:2, :].rearrange("p b n -> p (b n)")[:, 0:n_rows], ACT.Copy).then_inc(cols_ready, 1)
            act.wait_ge(lb_step, 1)
            act.activation(lb_b, lb_a, ACT.Exp).then_inc(lb_step, 1)
            act.wait_ge(bias_vec_done, 1)
            link(act.activation(bias_vec[0:ATT_HEADS, :], ps[0:ATT_HEADS, 2, 0:DISTS], ACT.Copy))
            act.dma_start(bias_dram, bias_vec[0:ATT_HEADS, :].unsqueeze(1).broadcast_to([ATT_HEADS, P, DISTS]))\
                .then_inc(bias_out, 16)
            norm("attn_norm", 0, 0)
            for s in range(1, RING):
                high_one(s)

            def linear_attention(H, slabs):
                for n, m in enumerate(LEVELS + [P]):
                    for half in halves(la["e"], m):
                        act.wait_ge(la_diff, want(la_diff))
                        act.activation(half, half, ACT.Exp).then_inc(la_exp, 1)
                    for s, dst in slabs.get(n, []):
                        evacuate(s, dst)
                        high_one(s)
                all_copied()
                act.activation(la["gate"], la["gate"], ACT.Silu).then_inc(la_silu, 1)
                act.activation(small[:, 152:153], const[:, ZEROS:ZEROS + 1], ACT.Sqrt)
                for tb in range(NTB):
                    act.wait_ge(la_out, want(la_out))
                    act.activation(la["sq"][tb], ps[:, 2 * tb:2 * tb + 2, :].rearrange("p b n -> p (b n)"), ACT.Square)\
                        .then_inc(la_sq, 1)
                    act.wait_ge(la_ms, want(la_ms))
                    at = tb * H
                    act.activation(head_std[:, at:at + H], head_ms[:, at:at + H], ACT.Sqrt).then_inc(la_std, 1)

            la = hgrn_views()
            high_four(2)
            for s in range(RING):
                made[s] += 2
            all_copied()
            act.activation(la["k"], la["f"], ACT.Sigmoid, scale=-1.0)
            act.activation(la["f"], la["f"], ACT.Sigmoid).then_inc(la_gate, 1)
            for s in range(RING):
                evacuate(s, proj[:, 8 + s, :])
                high_one(s)
                if s == 0:
                    act.wait_ge(la_ln_in, 1)
                    act.activation(la["f"], la["f"], ACT.Ln)
                    act.activation(la["ln2"], la["ln2"], ACT.Ln, scale=1.0 / LN_EDGE).then_inc(la_ln, 1)
            linear_attention(HG_HEADS, {min(2 * s + 2, 7): [(s, proj[:, 12 + s, :])] for s in range(RING)})
            split_turned([col("hgrn_gate_norm")] * NK)
            high_one(0)
            high_one(1)
            norm("ffn_norm", 0, 1)
            ffn(True, 0, 0)

            act.wait_ge(bias_out, 16)
            act.wait_ge(h_ready, 2 * 1)
            act.dma_start(bias_x[:, :, :], bass.AP(bias_dram.tensor, P - 1, [[DISTS - 1, P], [P * DISTS, ATT_HEADS], [1, SEQ]]))\
                .then_inc(bias_in, 16)
            high_one(0)
            high_one(1)
            norm("attn_norm", 1, 2)
            high_one(2)
            high_one(3)
            high_one(0, 4)
            high_one(1)
            high_one(2)
            high_one(3, 3)
            high_one(0)
            high_four(1)
            for j in range(9):
                made[j % RING] += 1
            dsa = dsa_views()
            for tb in range(NTB):
                S = (tb + 1) * P
                for hd in range(IDX_HEADS):
                    n = tb * IDX_HEADS + hd
                    act.wait_ge(ix_dots, n + 1)
                    if n >= 2:
                        act.wait_ge(ix_acc, n - 1)
                    act.activation(dsa["relu"][:, n % 2, 0:S], ps[:, n % 4, 0:S], ACT.Relu).then_inc(ix_relu, 1)
            UNITS = NTB * ATT_HEADS

            def exps(n):
                S = (n // ATT_HEADS + 1) * P
                act.wait_ge(at_max, n + 1)
                act.activation(dsa["a"][:, n % 4, 0:S], dsa["a"][:, n % 4, 0:S], ACT.Exp, bias=att_neg[:, n % 4:n % 4 + 1],
                               accum_out=att_sum[:, n % 4:n % 4 + 1]).then_inc(at_exp, 1)

            def copy_turned(n):
                S = (n // ATT_HEADS + 1) * P
                act.wait_ge(at_tr, n + 1)
                if n >= 2:
                    act.wait_ge(at_pv, n - 1)
                act.activation(dsa["pt"][:, n % 2, 0:S], ps[:, 2 + n % 2, 0:S], ACT.Copy).then_inc(at_pt, 1)

            for n in range(UNITS + 2):
                if n < UNITS:
                    exps(n)
                if n >= 2:
                    copy_turned(n - 2)
            act.wait_ge(at_pv, UNITS)
            for b in range(4):
                act.activation(x_hi[:, 2 * b:2 * b + 2, :].rearrange("p c t -> p (c t)"), ps[:, 4 + b, :], ACT.Copy)\
                    .then_inc(x_hi_done, 1)
            high_one(0)
            high_one(1)
            norm("ffn_norm", 1, 3)
            ffn(True, 1, 1)

            def fetch_gain(src):
                act.dma_start(gain_row, src.unsqueeze(0).broadcast_to([P, D])).then_inc(gain_in, 16)

            def pre(l, g, updates):
                norm("norm_g_2", l * 6 + g, updates)

            high_one(0)
            high_one(1)
            fetch_gain(A["final_norm"])
            rms_residual(4)
            updates = 5
            for l in range(2):
                pre(l, 0, updates)
                act.wait_ge(h_ready, 2 * updates)
                fetch_gain(A["norm_g_2"][l, 1])
                ffn(False, 0, 2 + 2 * l)
                if l == 1:
                    high_one(2)
                high_one(0)
                high_one(1)
                rms_product()
                updates += 1
                pre(l, 2, updates)
                high_one(2)
                high_one(3)
                act.wait_ge(h_ready, 2 * updates)
                fetch_gain(A["norm_g_2"][l, 3])
                if l == 0:
                    hyb = hyb_views()
                    high_four(1)
                    high_one(0)
                    high_one(1)
                    high_four(1)
                    for s in range(RING):
                        made[s] += 2
                    all_copied()
                    made[0] += 1
                    made[1] += 1
                    act.activation(hyb["gate"], hyb["gate"], ACT.Sigmoid).then_inc(cv_sig, 1)

                    def stick_exp(hd):
                        act.wait_ge(sb_z, hd + 1)
                        if hd >= 2:
                            act.wait_ge(sb_sp, hd - 1)
                        link(act.activation(hyb["l"][:, hd % 2, :], ps[:, hd % 4, 0:3 * P], ACT.Abs))
                        link(act.activation(hyb["l"][:, hd % 2, :], hyb["l"][:, hd % 2, :], ACT.Exp, scale=-1.0))
                        act.activation(hyb["l"][:, hd % 2, :], hyb["l"][:, hd % 2, :], ACT.Ln, bias=1.0).then_inc(sb_ln, 1)

                    def stick_weights(hd):
                        act.wait_ge(sb_rest, hd + 1)
                        if hd >= 2:
                            act.wait_ge(sb_pv, hd - 1)
                        act.activation(hyb["w"][:, hd % 2, :], ps[:, hd % 4, 0:3 * P], ACT.Exp).then_inc(sb_w, 1)

                    for hd in range(SB_HEADS + 1):
                        if hd < SB_HEADS:
                            stick_exp(hd)
                        if hd >= 1:
                            stick_weights(hd - 1)
                    act.wait_ge(sb_pv, SB_HEADS)
                    for b in range(2):
                        act.activation(x_hi[:, 2 * b:2 * b + 2, :].rearrange("p c t -> p (c t)"), ps[:, 4 + b, :], ACT.Copy)\
                            .then_inc(x_hi_done, 1)
                    act.wait_ge(cv_ms, 1)
                    act.activation(ln_std, ln_mv.rearrange("p (b s) -> p b s", s=2)[:, :, 1], ACT.Sqrt).then_inc(cv_std, 1)
                    for c in range(4):
                        act.wait_ge(cv_back, c // 2 + 1)
                        act.activation(hyb["cs"][:, c, :], ps[:, 2 + c // 2, c % 2 * SEQ:c % 2 * SEQ + SEQ], ACT.Silu,
                                       bias=col("conv_ln_b_2", c), scale=col("conv_ln_g_2", c)).then_inc(cv_silu, 1)
                    for c in range(4):
                        act.wait_ge(cv_silu, c + 1)
                        act.activation(x_hi[:, 4 + c, :], hyb["cs"][:, c, :], ACT.Copy).then_inc(x_hi_done, 1)
                else:
                    la = gla_views()
                    act.dma_start(w_gate[0:GATE_RANK, :], A["gla_w_gate_2"][0]).then_inc(gate_in, 16)
                    for s in range(RING):
                        made[s] += 1
                    for c in range(4):
                        act.wait_ge(gate_mm, 1)
                        ins = act.activation(la["x"][:, c * SEQ:c * SEQ + SEQ], ps[:, 1 + c // 2, c % 2 * SEQ:c % 2 * SEQ + SEQ],
                                             ACT.Identity, bias=col("gla_b_gate_2", c))
                    ins.then_inc(gate_x, 1)
                    act.wait_ge(gate_x, 1)
                    link(act.activation(la["e"], la["x"], ACT.Abs))
                    link(act.activation(la["e"], la["e"], ACT.Exp, scale=-1.0))
                    act.activation(la["e"], la["e"], ACT.Ln, bias=1.0).then_inc(gate_ln, 1)
                    high_four(1)
                    linear_attention(GLA_HEADS, {min(j + 1, 7): [(j % RING, proj[:, 4 + j, :])] for j in range(7)} |
                                     {7: [(j % RING, proj[:, 4 + j, :]) for j in (6, 7)]})
                    split_turned([col("gla_norm_g_2", c % 2) for c in range(NK)])
                high_one(0)
                high_one(1)
                rms_product()
                updates += 1
                pre(l, 4, updates)
                act.wait_ge(h_ready, 2 * updates)
                fetch_gain(A["norm_g_2"][l, 5])
                ffn(False, 0, 3 + 2 * l)
                if l == 0:
                    high_one(0)
                    high_one(1)
                rms_product()
                updates += 1

        @block.vector
        def _(dve):
            used, made, want = [0] * RING, [0] * RING, Tally()

            def all_copied():
                for s in range(RING):
                    dve.wait_ge(proj_free[s], made[s] + 1)

            def link(ins):
                ins.then_inc(dve_step, 1)
                dve.wait_ge(dve_step, want(dve_step))

            def flat(bank, n=1):
                return ps[:, bank:bank + n, :].rearrange("p b n -> p (b n)")

            def copy_product(s, at, parts=(P, 512), scale=1.0):
                used[s] += 1
                made[s] += 1
                dve.wait_ge(slab_used[s], used[s] + 1)
                dst, src = arena[0:parts[0], at:at + parts[1]], ps[0:parts[0], 4 + s, 0:parts[1]]
                dve.tensor_scalar(dst, src, scale, None, ALU.mult).then_inc(proj_free[s], 1)

            def copy_products(n, at):
                for j in range(n):
                    copy_product(j % RING, at + j * 512)

            def copy_four(n, at):
                with dve.Fori(0, n) as i:
                    for s in range(RING):
                        dve.wait_ge(slab_used[s], i + (used[s] + 2))
                        dve.tensor_copy(arena[:, bass.ds(i * 2048 + (at + s * 512), 512)], ps[:, 4 + s, :]).then_inc(proj_free[s], 1)
                for s in range(RING):
                    used[s] += n
                    made[s] += n

            def inverse_rms(tb, half=False):
                one = slice(tb, tb + 1)
                dve.wait_ge(rms_sq, want(rms_sq))
                dve.tensor_scalar(ms[:, one], ssq[:, one], 1.0 / D, EPS, ALU.mult, ALU.add).then_inc(rms_ms, 1)
                dve.wait_ge(rms_std, want(rms_std))
                link(dve.reciprocal(rstd[:, one], std[:, one]))
                if half:
                    link(dve.tensor_scalar(rstd[:, one], rstd[:, one], 0.5, None, ALU.mult))
                return rstd[:, one]

            def split_turned(gains):
                for c in range(NK):
                    if c % 2 == 0:
                        dve.wait_ge(x_hi_done, want(x_hi_done, 2))
                    dve.scalar_tensor_tensor(x_lo[:, c, :], ps[:, 4 + c // 2, c % 2 * SEQ:c % 2 * SEQ + SEQ], gains[c],
                                             x_hi[:, c, :].bitcast(F32), ALU.mult, ALU.subtract).then_inc(x_ready, 1)

            def norm(name, i):
                for tb in range(NTB):
                    r = inverse_rms(tb)
                    dve.tensor_scalar(xn[:, tb, :], h[:, tb, :], r, None, ALU.mult).then_inc(xn_ready, 1)
                split_turned([col(name, i * NK + c) for c in range(NK)])

            def product_done(tb):
                if tb == 0:
                    dve.wait_ge(half_done, want(half_done))
                else:
                    dve.wait_ge(slab_used[3], used[3] + 1)

            def add_product():
                for tb in range(NTB):
                    product_done(tb)
                    dve.tensor_tensor(h[:, tb, :], h[:, tb, :], flat(2 * tb, 2), ALU.add).then_inc(h_ready, 1)

            def add_normed_product(half):
                want(half_done)
                dve.wait_ge(gain_in, want(gain_in, 16))
                for tb in range(NTB):
                    r = inverse_rms(tb, half)
                    link(dve.scalar_tensor_tensor(xn[:, tb, :], flat(2 * tb, 2), r, gain_row, ALU.mult, ALU.mult))
                    dve.tensor_tensor(h[:, tb, :], h[:, tb, :], xn[:, tb, :], ALU.add).then_inc(h_ready, 1)

            def out_used():
                for s in range(RING):
                    used[s] += 1

            def ffn(conv, f_conv, f):
                q0 = f * NF

                def body(i, last):
                    if conv:
                        for b in range(2):
                            bank = ps[:, 4 + b, :]

                            def tap(g, k):
                                shift = 2 - k
                                c = i * 2 + (row_of["ffn_conv_w"] + f_conv * 132 + k * 44 + g * 22 + b)
                                dst = ff_c[:, b, g, shift:SEQ]
                                return dve.scalar_tensor_tensor(dst, bank[:, g * SEQ:g * SEQ + SEQ - shift],
                                                                cols[:, bass.ds(c, 1)], dst, ALU.mult, ALU.add)
                            dve.wait_ge(conv_in[b], i + (f_conv * NF + 1))
                            tap(0, 1).then_inc(tap_done[b], 1)
                            tap(1, 1).then_inc(tap_done[b], 1)
                            dve.wait_ge(tap_done[b], i * 2 + (f_conv * NF * 2 + 2))
                            tap(0, 0)
                            tap(1, 0).then_inc(conv_done[b], 1)
                    for b in range(2):
                        dve.wait_ge(silu_done[b], i + (q0 + 1))
                        if not conv and b == 0:
                            dve.wait_ge(g_ready, i * 2 + 2 * q0)
                        up = ff_c[:, b, 1, :] if conv else ps[:, 4 + b, SEQ:2 * SEQ]
                        dve.tensor_tensor(ff_g[:, b, :], ff_s[:, b, :], up, ALU.mult).then_inc(gt_done[b], 1)
                    for b in range(2):
                        dve.wait_ge(gt_hi[b], i + (q0 + 1))
                        dve.tensor_tensor(g_lo[:, b, :], ff_g[:, b, :], g_hi[:, b, :].bitcast(F32), ALU.subtract)\
                            .then_inc(g_ready, 1)
                    if not last:
                        dve.wait_ge(hi_done[2], i + (used[2] + 1))
                        dve.tensor_tensor(w_lo[2][:, :], raw[2][:, :], w_hi[2][:, :].bitcast(F32), ALU.subtract)\
                            .then_inc(slab_ready[2], 1)

                with dve.Fori(0, NF - 1) as i:
                    body(i, False)
                body(NF - 1, True)
                used[0] += NF
                used[1] += NF
                used[2] += NF - 1
                used[3] += 1

            def linear_attention(la, H, dv, gains):
                q, k, qt, kt, b, e = la["q"], la["k"], la["qt"], la["kt"], la["b"], la["e"]
                scores = la["scores"]
                banks = H // 2

                def differences(n):
                    m = levels[n]
                    b_lo, b_up = halves(b, m)
                    e_lo, e_up = halves(e, m)
                    r = b_lo[:, :, m - 1:m].broadcast_to([P, H * SEQ // (2 * m), m])
                    if n:
                        dve.wait_ge(la_factors, want(la_factors, 2))
                    for dst, x, y in ((e_lo, r, b_lo), (e_up, b_up, r)):
                        dve.tensor_tensor(dst, x, y, ALU.subtract).then_inc(la_diff, 1)

                def by_head(t, bank):
                    return t[:, bank * 512:bank * 512 + 512].rearrange("p (n t) -> p n t", t=P)

                for hd in range(H):
                    a = hd * SEQ
                    ins = dve.tensor_tensor_scan(b[:, a:a + SEQ], la["f"][:, a:a + SEQ], zeros[:, 0:SEQ], 0.0, ALU.add, ALU.add)
                link(ins)
                levels = LEVELS + [P]
                differences(0)
                for n in range(banks):
                    dve.wait_ge(la_scores, want(la_scores))
                    ins = dve.tensor_tensor(by_head(scores, n), by_head(flat(n), 0),
                                            ident.unsqueeze(1).broadcast_to([P, 4, P]), ALU.mult)
                ins.then_inc(la_masked, 1)
                for n, m in enumerate(levels):
                    for t, x, part in ((kt, k, 0), (qt, q, 1)):
                        dve.wait_ge(la_exp, want(la_exp))
                        dve.tensor_tensor(halves(t, m)[part], halves(x, m)[part], halves(e, m)[part], ALU.mult)\
                            .then_inc(la_factors, 1)
                    if n + 1 < len(levels):
                        differences(n + 1)
                        mask = level_mask[:, n, :].rearrange("p (n two m) -> p n two m", two=2, m=m)[:, :, 1, :]
                        mask = mask.unsqueeze(1).broadcast_to([P, 8, P // (2 * m), m])
                        dve.wait_ge(la_masked, want(la_masked))
                        for bank in range(H // 4):
                            dve.wait_ge(la_scores, want(la_scores))
                            at = scores[:, bank * 1024:bank * 1024 + 1024]\
                                .rearrange("p (b n two m) -> p b n two m", b=8, two=2, m=m)[:, :, :, 1, :]
                            src = flat(2 * (n % 2) + bank).rearrange("p (b n m) -> p b n m", b=8, m=m)
                            ins = dve.copy_predicated(at, mask, src)
                        ins.then_inc(la_masked, 1)
                want(la_masked)
                dve.wait_ge(la_factors, want(la_factors, 2))
                dve.wait_ge(la_scores, want(la_scores, H // 4))
                dve.tensor_copy(la["cross"][:, 0:H * P], flat(2, H // 4)).then_inc(la_cross, 1)
                gate = la["gate"].rearrange("p (s n) -> p s n", n=512)
                for tb in range(NTB):
                    a, z = tb * H, tb * H + H
                    dve.wait_ge(la_sq, want(la_sq))
                    link(dve.tensor_reduce(head_ssq[:, a:z], la["sq"][tb].rearrange("p (h d) -> p h d", d=dv), AX_X, ALU.add))
                    dve.tensor_scalar(head_ms[:, a:z], head_ssq[:, a:z], 1.0 / dv, EPS, ALU.mult, ALU.add).then_inc(la_ms, 1)
                    dve.wait_ge(la_std, want(la_std))
                    link(dve.reciprocal(head_rstd[:, a:z], head_std[:, a:z]))
                    if tb == 0:
                        dve.wait_ge(la_silu, want(la_silu))
                    for hd in range(H):
                        c = hd * dv
                        ins = dve.scalar_tensor_tensor(
                            xn[:, tb, c:c + dv], ps[:, 2 * tb + c // 512, c % 512:c % 512 + dv], head_rstd[:, a + hd:a + hd + 1],
                            gate[:, c // SLAB, tb * SLAB + c % SLAB:tb * SLAB + c % SLAB + dv], ALU.mult, ALU.mult)
                    ins.then_inc(xn_ready, 1)
                split_turned(gains)

            def low_of_banks(n):
                for b in range(n):
                    dve.wait_ge(x_hi_done, want(x_hi_done))
                    dve.tensor_tensor(x_lo[:, 2 * b:2 * b + 2, :].rearrange("p c t -> p (c t)"), ps[:, 4 + b, :],
                                      x_hi[:, 2 * b:2 * b + 2, :].bitcast(F32).rearrange("p c t -> p (c t)"), ALU.subtract)\
                        .then_inc(x_ready, 1)

            for s in range(RING):
                dve.sem_inc(slab_ready[s], 1)
                dve.sem_inc(slab_used[s], 1)
                dve.sem_inc(proj_free[s], 1)
            for b in range(2):
                dve.sem_inc(gt_done[b], 1)
            dve.wait_ge(cols_ready, 1)
            link(dve.tensor_copy(level_mask[:, :, :], masks_in))
            lb_col = cols[:, row_of["hgrn_lower_bounds"]:row_of["hgrn_lower_bounds"] + NK]
            dve.tensor_tensor(lb_a, lb_col, lb_col, ALU.subtract).then_inc(lb_step, 1)
            dve.wait_ge(lb_step, 2)
            link(dve.reciprocal(lb_a, lb_b))
            link(dve.tensor_tensor(lb_b, lb_b, lb_a, ALU.mult))
            link(dve.tensor_tensor(lb, lb_b, lb_b, ALU.subtract))
            link(dve.tensor_scalar(one_minus_lb, lb, -1.0, 1.0, ALU.mult, ALU.add))

            norm("attn_norm", 0)
            copy_four(2, 0)
            for s in range(RING):
                used[s] += 2
                made[s] += 2
            la = hgrn_views()
            dve.wait_ge(la_gate, 1)
            for hd in range(HG_HEADS):
                f = la["f"][:, hd * SEQ:hd * SEQ + SEQ]
                ins = dve.tensor_scalar(f, f, one_minus_lb[:, hd:hd + 1], lb[:, hd:hd + 1], ALU.mult, ALU.add)
            link(ins)
            dve.tensor_scalar(la["ln2"], la["f"], TINY, LN_EDGE, ALU.max, ALU.min)
            dve.tensor_scalar(la["f"], la["f"], LN_EDGE, None, ALU.max).then_inc(la_ln_in, 1)
            dve.wait_ge(la_ln, 1)
            dve.tensor_tensor(la["f"], la["f"], la["ln2"], ALU.add).then_inc(la_q, 1)
            dve.wait_ge(la_q, 1)
            dve.wait_ge(bias_out, 16)
            linear_attention(la, HG_HEADS, P, [col("hgrn_gate_norm")] * NK)
            out_used()
            add_product()
            norm("ffn_norm", 0)
            ffn(True, 0, 0)
            add_product()

            norm("attn_norm", 1)
            dsa = dsa_views()
            copy_products(8, 0)
            copy_product(0, 4096, (P, 2 * IDX_HEADS))
            all_copied()
            dve.tensor_scalar(words(2048, 512), words(2048, 512), 64 ** -0.5, None, ALU.mult).then_inc(at_k, 1)
            link(dve.tensor_scalar(dsa["w_scaled"], dsa["w"], IDX_HEADS ** -0.5 * 64 ** -0.5, None, ALU.mult))
            for tb in range(NTB):
                S = (tb + 1) * P
                score = dsa["score"][:, tb, 0:S]
                diag = dsa["score"][:, tb, S - P:S]
                for hd in range(IDX_HEADS):
                    n = tb * IDX_HEADS + hd
                    w = dsa["w_scaled"][:, tb * IDX_HEADS + hd:tb * IDX_HEADS + hd + 1]
                    dve.wait_ge(ix_relu, n + 1)
                    r = dsa["relu"][:, n % 2, 0:S]
                    if hd == 0:
                        dve.tensor_scalar(score, r, w, None, ALU.mult).then_inc(ix_acc, 1)
                    else:
                        dve.wait_ge(ix_acc, n)
                        dve.scalar_tensor_tensor(score, r, w, score, ALU.mult, ALU.add).then_inc(ix_acc, 1)
                dve.wait_ge(ix_acc, n + 1)
                link(dve.tensor_tensor(diag, diag, const[:, CAUSAL:CAUSAL + P], ALU.add))
                rest, src = dsa["rest"][:, 0:S], score
                for _ in range(TOP_K // 8):
                    link(dve.max(top8, src))
                    link(dve.match_replace(rest, top8, src, TAKEN))
                    src = rest
                mask = dsa["mask"][:, tb, 0:S]
                link(dve.tensor_scalar(mask, rest, TAKEN, NEG_BIG, ALU.is_gt, ALU.mult))
                diag = dsa["mask"][:, tb, S - P:S]
                link(dve.tensor_tensor(diag, diag, const[:, CAUSAL:CAUSAL + P], ALU.add))
            UNITS = NTB * ATT_HEADS

            def logits(n):
                S = (n // ATT_HEADS + 1) * P
                slot = n % 4
                dve.wait_ge(at_qk, n + 1)
                if n >= 4:
                    dve.wait_ge(at_tr, n - 3)
                link(dve.tensor_tensor_reduce(dsa["a"][:, slot, 0:S], ps[:, n % 2, 0:S], dsa["mask"][:, n // ATT_HEADS, 0:S],
                                              1.0, -3.0e38, ALU.add, ALU.max, att_max[:, slot:slot + 1]))
                dve.tensor_scalar(att_neg[:, slot:slot + 1], att_max[:, slot:slot + 1], -1.0, None, ALU.mult).then_inc(at_max, 1)

            def normalise(n):
                S = (n // ATT_HEADS + 1) * P
                slot = n % 4
                dve.wait_ge(at_exp, n + 1)
                link(dve.reciprocal(att_inv[:, slot:slot + 1], att_sum[:, slot:slot + 1]))
                a = dsa["a"][:, slot, 0:S]
                dve.tensor_scalar(a, a, att_inv[:, slot:slot + 1], None, ALU.mult).then_inc(at_p, 1)

            for n in range(UNITS + 1):
                if n < UNITS:
                    logits(n)
                if n >= 1:
                    normalise(n - 1)
            low_of_banks(4)
            out_used()
            add_product()
            norm("ffn_norm", 1)
            ffn(True, 1, 1)
            add_product()

            dve.wait_ge(gain_in, want(gain_in, 16))
            for tb in range(NTB):
                r = inverse_rms(tb)
                dve.scalar_tensor_tensor(h[:, tb, :], h[:, tb, :], r, gain_row, ALU.mult, ALU.mult)\
                    .then_inc(h_ready, 1)
            for l in range(2):
                norm("norm_g_2", l * 6)
                ffn(False, 0, 2 + 2 * l)
                add_normed_product(True)
                norm("norm_g_2", l * 6 + 2)
                if l == 0:
                    hyb = hyb_views()
                    pad = CONV_TAPS - 1
                    copy_four(2, 0)
                    copy_products(2, 8 * 512)
                    all_copied()
                    dve.tensor_scalar(hyb["k_all"], hyb["k_all"], 64 ** -0.5, None, ALU.mult).then_inc(sb_k, 1)
                    dve.memset(hyb["pad"][:, :, 0:pad], 0.0)
                    dve.wait_ge(cv_sig, 1)
                    link(dve.tensor_tensor(hyb["pad"][:, :, pad:pad + SEQ], hyb["u"],
                                           hyb["gate"].rearrange("p (c t) -> p c t", t=SEQ), ALU.mult))
                    taps = [(k, c) for k in range(CONV_TAPS) for c in range(4)]

                    def convolve(n):
                        for _ in range(n):
                            if not taps:
                                return
                            k, c = taps.pop(0)
                            src, dst, w = hyb["pad"][:, c, k:k + SEQ], hyb["co"][:, c, :], col("conv_dw_w_2", k * 4 + c)
                            if k == 0:
                                dve.tensor_scalar(dst, src, w, col("conv_dw_b_2", c), ALU.mult, ALU.add).then_inc(cv_tap, 1)
                            else:
                                dve.wait_ge(cv_tap, want(cv_tap))
                                dve.scalar_tensor_tensor(dst, src, w, dst, ALU.mult, ALU.add).then_inc(cv_tap, 1)

                    def stick_softplus(hd):
                        dve.wait_ge(sb_ln, hd + 1)
                        if hd >= 2:
                            dve.wait_ge(sb_rest, hd - 1)
                        dve.scalar_tensor_tensor(hyb["sp"][:, hd % 2, :], ps[:, hd % 4, 0:3 * P], 0.0, hyb["l"][:, hd % 2, :],
                                                 ALU.max, ALU.add).then_inc(sb_sp, 1)

                    for hd in range(SB_HEADS):
                        convolve(15)
                        stick_softplus(hd)
                    convolve(len(taps))
                    low_of_banks(2)
                    dve.wait_ge(cv_tap, 4 * CONV_TAPS)
                    dve.wait_ge(cv_turn, 1)
                    for tb in range(NTB):
                        ins = dve.bn_stats(ln_stats[:, 6 * tb:6 * tb + 6], ps[:, 6 + tb, :])
                    link(ins)
                    for tb in range(NTB):
                        ins = dve.bn_aggr(ln_mv[:, 2 * tb:2 * tb + 2], ln_stats[:, 6 * tb:6 * tb + 6])
                    link(ins)
                    var = ln_mv.rearrange("p (b s) -> p b s", s=2)[:, :, 1]
                    dve.tensor_scalar(var, var, EPS, None, ALU.add).then_inc(cv_ms, 1)
                    dve.wait_ge(cv_std, 1)
                    link(dve.reciprocal(ln_rstd, ln_std))
                    for tb in range(NTB):
                        dve.tensor_scalar(xn[:, tb, 0:512], ps[:, 6 + tb, :], ln_mv[:, 2 * tb:2 * tb + 1], ln_rstd[:, tb:tb + 1],
                                          ALU.subtract, ALU.mult).then_inc(cv_norm, 1)
                    for c in range(4):
                        dve.wait_ge(x_hi_done, want(x_hi_done))
                        dve.tensor_tensor(x_lo[:, 4 + c, :], hyb["cs"][:, c, :], x_hi[:, 4 + c, :].bitcast(F32), ALU.subtract)\
                            .then_inc(x_ready, 1)
                else:
                    la = gla_views()
                    used[2] += 1
                    dve.wait_ge(slab_used[2], used[2] + 1)
                    dve.tensor_copy(la["rank"], ps[0:GATE_RANK, 0, 0:SEQ]).then_inc(gate_rank, 1)
                    for s in range(2):
                        copy_product(s, s * 512, scale=P ** -0.5)
                    dve.wait_ge(gate_ln, 1)
                    link(dve.scalar_tensor_tensor(la["x"], la["x"], 0.0, la["e"], ALU.min, ALU.subtract))
                    link(dve.tensor_scalar(la["x"], la["x"], 1.0 / GLA_TAU, None, ALU.mult))
                    for s in range(2, RING):
                        copy_product(s, s * 512)
                    all_copied()
                    for s in range(RING):
                        used[s] += 2
                        made[s] += 2
                    dve.sem_inc(la_q, 1)
                    linear_attention(la, GLA_HEADS, SLAB, [col("gla_norm_g_2", c % 2) for c in range(NK)])
                out_used()
                add_normed_product(False)
                norm("norm_g_2", l * 6 + 4)
                ffn(False, 0, 3 + 2 * l)
                add_normed_product(True)

        @block.tensor
        def _(pe):
            used, made, want = [0] * RING, [0] * RING, Tally()

            def three(out_ap, a, b, start, stop):
                (a_hi, a_lo), (b_hi, b_lo) = a, b
                pe.matmul(out_ap, a_hi, b_hi, start=start, stop=False, skip_group_check=True)
                pe.matmul(out_ap, a_hi, b_lo, start=False, stop=False, skip_group_check=True)
                return pe.matmul(out_ap, a_lo, b_hi, start=False, stop=stop, skip_group_check=True)

            def weights(s, a, n):
                return w_hi[s][:, a:a + n], w_lo[s][:, a:a + n]

            def acts(k, a=0, n=SEQ):
                return x_hi[:, k, a:a + n], x_lo[:, k, a:a + n]

            def features(s, bank, a, n, at, fresh=None):
                for k in range(NK):
                    if fresh is not None:
                        pe.wait_ge(x_ready, fresh + max(k + 1, 2 * (bank - 4) + 2))
                    ins = three(ps[0:n, bank, at:at + SEQ], weights(s, k * SLAB + a, n), acts(k), k == 0, k == NK - 1)
                return ins

            def tokens(s, bank, a, n, at, blocks=range(NTB)):
                for tb in blocks:
                    for k in range(NK):
                        ins = three(ps[:, bank, at + tb * n:at + tb * n + n], acts(k, tb * P, P), weights(s, k * SLAB + a, n),
                                    k == 0, k == NK - 1)
                return ins

            def feature_slab(s, fresh=None):
                features(s, 4 + s, 0, P, 0, fresh)
                return features(s, 4 + s, P, P, SEQ)

            def token_slab(s):
                return tokens(s, 4 + s, 0, SLAB, 0)

            def project_four(how, n, fresh=None):
                with pe.Fori(0, n) as i:
                    for s in range(RING):
                        pe.wait_ge(slab_ready[s], i + (used[s] + 2))
                        pe.wait_ge(proj_free[s], i + (made[s] + 1))
                        (how(s) if s or fresh is None else how(s, fresh)).then_inc(slab_used[s], 1)
                for s in range(RING):
                    used[s] += n
                    made[s] += n

            def begin(s):
                pe.wait_ge(slab_ready[s], used[s] + 2)
                pe.wait_ge(proj_free[s], made[s] + 1)
                used[s] += 1
                made[s] += 1

            def project(how, s):
                begin(s)
                how(s).then_inc(slab_used[s], 1)

            def half_token_slab(s, tb):
                if tb == 0:
                    begin(s)
                ins = tokens(s, 4 + s, 0, SLAB, 0, [tb])
                if tb == NTB - 1:
                    ins.then_inc(slab_used[s], 1)

            def all_copied():
                for s in range(RING):
                    pe.wait_ge(proj_free[s], made[s] + 1)

            def x_new():
                return want(x_ready, NK) - NK

            def x_split(n=NK):
                pe.wait_ge(x_ready, want(x_ready, n))

            def turn():
                for tb in range(NTB):
                    pe.wait_ge(xn_ready, want(xn_ready))
                    for c in range(NK):
                        at = c % 2 * SEQ + tb * P
                        ins = pe.transpose(ps[:, 4 + c // 2, at:at + P], xn[:, tb, c * P:c * P + P], ident)
                        if tb == NTB - 1 and c % 2 == 1:
                            ins.then_inc(turned, 1)

            def project_out(fresh=None):
                for s in range(RING):
                    pe.wait_ge(slab_ready[s], used[s] + 2)
                    for tb in range(NTB):
                        for kk in range(2):
                            k = 2 * s + kk
                            if fresh is not None and tb == 0:
                                pe.wait_ge(x_ready, fresh + k + 1)
                            for half in range(2):
                                ins = three(ps[:, 2 * tb + half, :], acts(k, tb * P, P), weights(s, kk * D + half * 512, 512),
                                            k == 0, k == NK - 1)
                        if s == RING - 1 and tb == 0:
                            ins.then_inc(half_done, 1)
                    ins.then_inc(slab_used[s], 1)
                    used[s] += 1

            def ffn(f):
                q0 = f * NF
                z = zeros.bitcast(BF16)
                for bank in range(4):
                    pe.matmul(ps[:, bank, :], z[:, 0:P], z[:, 0:512], start=True, stop=False, skip_group_check=True)

                def up(i, ahead):
                    pe.wait_ge(slab_ready[0], i + (used[0] + 2 + ahead))
                    fresh = None if ahead else x_new()
                    for b in range(2):
                        pe.wait_ge(gt_done[b], i + (q0 + 1 + ahead))
                        ins = features(0, 4 + b, b * P, P, 0, fresh)
                    ins.then_inc(slab_used[0], 1)
                    pe.wait_ge(slab_ready[1], i + (used[1] + 2 + ahead))
                    features(1, 4, 0, P, SEQ).then_inc(up_half, 1)
                    features(1, 5, P, P, SEQ).then_inc(slab_used[1], 1)

                def down(s, u, i, last):
                    pe.wait_ge(slab_ready[s], u + 2)
                    pe.wait_ge(g_ready, i * 2 + (2 * q0 + 2))
                    for tb in range(NTB):
                        for b in range(2):
                            for half in range(2):
                                a = (g_hi[:, b, tb * P:tb * P + P], g_lo[:, b, tb * P:tb * P + P])
                                ins = three(ps[:, 2 * tb + half, :], a, weights(s, b * D + half * 512, 512), False, last and b == 1)
                        if last and tb == 0:
                            ins.then_inc(half_done, 1)
                    ins.then_inc(slab_used[s], 1)

                up(0, 0)
                with pe.Fori(0, NF - 1) as i:
                    up(i, 1)
                    down(2, i + used[2], i, False)
                down(3, used[3], NF - 1, True)
                used[0] += NF
                used[1] += NF
                used[2] += NF - 1
                used[3] += 1

            def linear_attention(la, H, dv, between):
                def scores(per, n, bank, k, q):
                    out_ap = ps[:, bank + n // per, n % per * (512 // per):(n % per + 1) * (512 // per)]
                    if len(q.shape) == 3:
                        out_ap = out_ap.rearrange("p (n m) -> p n m", m=q.shape[2])
                    ins = pe.matmul(out_ap, k, q, start=True, stop=True, skip_group_check=True)
                    if n % per == per - 1:
                        ins.then_inc(la_scores, 1)

                masked = want(la_masked, 0)
                for n in range(2 * H):
                    scores(4, n, 0, la["k"][:, n * P:n * P + P], la["q"][:, n * P:n * P + P])
                for n, m in enumerate(LEVELS):
                    between(n)
                    pe.wait_ge(la_factors, want(la_factors, 2))
                    pe.wait_ge(la_masked, masked + max(n, 1))
                    for i in range(2 * H):
                        scores(8, i, 2 * (n % 2), la["kt"][:, i * P:i * P + P], halves(la["qt"][:, i * P:i * P + P], m)[1])
                between(len(LEVELS))

                def outputs(tb):
                    for hd in range(H):
                        c = hd * dv
                        o = ps[:, 2 * tb + c // 512, c % 512:c % 512 + dv]
                        n = 2 * hd + tb
                        ins = pe.matmul(o, la["scores"][:, n * P:n * P + P], v_of(la, tb, hd, dv), start=True, stop=tb == 0,
                                        skip_group_check=True)
                        if tb == 1:
                            ins = pe.matmul(o, la["cross"][:, hd * P:hd * P + P], v_of(la, 0, hd, dv), start=False, stop=True,
                                            skip_group_check=True)
                    ins.then_inc(la_out, 1)

                pe.wait_ge(la_masked, want(la_masked, 1 + len(LEVELS)))
                all_copied()
                outputs(0)
                pe.wait_ge(la_factors, want(la_factors, 2))
                for hd in range(H):
                    a = hd * SEQ
                    scores(4, hd, 2, la["kt"][:, a:a + P], la["qt"][:, a + P:a + SEQ])
                pe.wait_ge(la_cross, want(la_cross))
                outputs(1)

            n_small = 3 + len(row_src) + 1
            pe.wait_ge(const_in, 16 * n_small)
            for t in range(n_row_tiles):
                k = min(P, n_rows - t * P)
                ins = pe.transpose(ps[:, t // 4, t % 4 * P:t % 4 * P + k], rows[0:k, t, :], ident[0:k, 0:k])
            ins.then_inc(rows_turned, 1)
            pe.matmul(ps[0:ATT_HEADS, 2, 0:DISTS], rel_bias_sb[0:BUCKETS, :], const[0:BUCKETS, ONEHOT:ONEHOT + DISTS],
                      start=True, stop=True).then_inc(bias_vec_done, 1)

            turn()
            project_four(feature_slab, 2, x_new())
            project_four(token_slab, 1)
            la = hgrn_views()
            pe.wait_ge(la_q, 1)
            pe.wait_ge(la_k, 1)
            linear_attention(la, HG_HEADS, P, lambda n: half_token_slab(n // 2, n % 2))
            turn()
            project_out(x_new())
            turn()
            ffn(0)

            turn()
            project_four(feature_slab, 1, x_new())
            for s in range(3):
                project(feature_slab, s)

            def index_keys_and_values(s):
                features(s, 4 + s, 0, P, 0)
                return tokens(s, 4 + s, P, P, SEQ)

            project(index_keys_and_values, 3)
            project(lambda s: tokens(s, 4 + s, 0, IDX_HEADS, 0), 0)
            dsa = dsa_views()
            all_copied()
            for tb in range(NTB):
                S = (tb + 1) * P
                for hd in range(IDX_HEADS):
                    n = tb * IDX_HEADS + hd
                    a = hd % 2 * 64
                    if n >= 4:
                        pe.wait_ge(ix_relu, n - 3)
                    pe.matmul(ps[:, n % 4, 0:S], dsa["qi"][a:a + 64, hd // 2, tb * P:tb * P + P], dsa["ki"][a:a + 64, 0:S],
                              start=True, stop=True).then_inc(ix_dots, 1)
            UNITS = NTB * ATT_HEADS
            pe.wait_ge(at_k, 1)
            pe.wait_ge(bias_in, 16)
            pe.wait_ge(ix_relu, NTB * IDX_HEADS)

            def queries_keys(n):
                tb, hd = divmod(n, ATT_HEADS)
                S = (tb + 1) * P
                a = hd % 2 * 64
                if n >= 2:
                    pe.wait_ge(at_max, n - 1)
                pe.matmul(ps[:, n % 2, 0:S], dsa["q"][a:a + 64, hd // 2, tb * P:tb * P + P],
                          dsa["k"][a:a + 64, hd // (ATT_HEADS // 2), 0:S], start=True, stop=False, skip_group_check=True)
                c = (1 - tb) * P
                pe.matmul(ps[:, n % 2, 0:S], ident, bias_x[:, hd, c:c + S], start=False, stop=True, skip_group_check=True)\
                    .then_inc(at_qk, 1)

            def turn_probs(n):
                tb = n // ATT_HEADS
                pe.wait_ge(at_p, n + 1)
                if n >= 2:
                    pe.wait_ge(at_pt, n - 1)
                for sb_ in range(tb + 1):
                    ins = pe.transpose(ps[:, 2 + n % 2, sb_ * P:sb_ * P + P], dsa["a"][:, n % 4, sb_ * P:sb_ * P + P], ident)
                ins.then_inc(at_tr, 1)

            def values(n):
                tb, hd = divmod(n, ATT_HEADS)
                pe.wait_ge(at_pt, n + 1)
                a, c = hd % 2 * 64, hd // 2
                kv = hd // (ATT_HEADS // 2) * 64
                o = ps[a:a + 64, 4 + c // 2, c % 2 * SEQ + tb * P:c % 2 * SEQ + tb * P + P]
                for sb_ in range(tb + 1):
                    ins = pe.matmul(o, dsa["v"][:, sb_, kv:kv + 64], dsa["pt"][:, n % 2, sb_ * P:sb_ * P + P],
                                    start=sb_ == 0, stop=sb_ == tb, skip_group_check=True)
                ins.then_inc(at_pv, 1)

            for n in range(UNITS + 3):
                if n < UNITS:
                    queries_keys(n)
                if 2 <= n < UNITS + 2:
                    turn_probs(n - 2)
                if n >= 3:
                    values(n - 3)
            x_split(4)
            project_out()
            turn()
            ffn(1)

            for l in range(2):
                turn()
                ffn(2 + 2 * l)
                turn()
                if l == 0:
                    hyb = hyb_views()
                    project_four(feature_slab, 2, x_new())
                    project(token_slab, 0)
                    project(token_slab, 1)
                    pe.wait_ge(sb_k, 1)

                    def stick_logits(hd):
                        a, c = hd % 2 * 64, hd // 2
                        q, k = hyb["q"][a:a + 64, c, :], hyb["k"][a:a + 64, c, :]
                        bank = ps[:, hd % 4, :]
                        if hd >= 4:
                            pe.wait_ge(sb_w, hd - 3)
                        pe.matmul(bank[:, 0:SEQ], k[:, 0:P], q, start=True, stop=False, skip_group_check=True)
                        pe.matmul(bank[:, SEQ:SEQ + P], k[:, P:SEQ], q[:, P:SEQ], start=False, stop=False, skip_group_check=True)
                        for c0 in (0, SEQ):
                            ins = pe.matmul(bank[:, c0:c0 + P], ident, const[:, STRICT:STRICT + P], start=False, stop=False,
                                            skip_group_check=True)
                        ins.then_inc(sb_z, 1)

                    def stick_rest(hd):
                        pe.wait_ge(sb_sp, hd + 1)
                        bank, sp_ = ps[:, hd % 4, :], hyb["sp"][:, hd % 2, :]
                        tri, minus = const[:, TRI:TRI + P], const[:, ONES:ONES + P]
                        pe.matmul(bank[:, 0:SEQ], tri, sp_[:, 0:SEQ], start=False, stop=False, skip_group_check=True)
                        pe.matmul(bank[:, P:SEQ], minus, sp_[:, SEQ:3 * P], start=False, stop=False, skip_group_check=True)
                        pe.matmul(bank[:, SEQ:3 * P], tri, sp_[:, SEQ:3 * P], start=False, stop=True, skip_group_check=True)\
                            .then_inc(sb_rest, 1)

                    def stick_values(hd):
                        pe.wait_ge(sb_w, hd + 1)
                        a, c = hd % 2 * 64, hd // 2
                        w = hyb["w"][:, hd % 2, :]
                        o = ps[a:a + 64, 4 + c // 2, c % 2 * SEQ:c % 2 * SEQ + SEQ]
                        v0, v1 = v_of(hyb, 0, hd, 64), v_of(hyb, 1, hd, 64)
                        pe.matmul(o[:, 0:P], v0, w[:, 0:P], start=True, stop=True, skip_group_check=True)
                        pe.matmul(o[:, P:SEQ], v0, w[:, P:SEQ], start=True, stop=False, skip_group_check=True)
                        pe.matmul(o[:, P:SEQ], v1, w[:, SEQ:3 * P], start=False, stop=True, skip_group_check=True)\
                            .then_inc(sb_pv, 1)

                    for hd in range(SB_HEADS + 2):
                        if hd < SB_HEADS:
                            stick_logits(hd)
                        if 1 <= hd < SB_HEADS + 1:
                            stick_rest(hd - 1)
                        if hd >= 2:
                            stick_values(hd - 2)
                    pe.wait_ge(cv_tap, 4 * CONV_TAPS)
                    for tb in range(NTB):
                        for c in range(4):
                            ins = pe.transpose(ps[:, 6 + tb, c * P:c * P + P], hyb["co"][:, c, tb * P:tb * P + P], ident)
                    ins.then_inc(cv_turn, 1)
                    pe.wait_ge(cv_norm, NTB)
                    for c in range(4):
                        for tb in range(NTB):
                            at = c % 2 * SEQ + tb * P
                            ins = pe.transpose(ps[:, 2 + c // 2, at:at + P], xn[:, tb, c * P:c * P + P], ident)
                        if c % 2 == 1:
                            ins.then_inc(cv_back, 1)
                    x_split(6)
                else:
                    la = gla_views()
                    pe.wait_ge(slab_ready[2], used[2] + 2)
                    features(2, 0, 0, GATE_RANK, 0, x_new()).then_inc(slab_used[2], 1)
                    used[2] += 1
                    project(feature_slab, 0)
                    pe.wait_ge(gate_in, 16)
                    pe.wait_ge(gate_rank, 1)
                    for c in range(4):
                        ins = pe.matmul(ps[:, 1 + c // 2, c % 2 * SEQ:c % 2 * SEQ + SEQ], w_gate[0:GATE_RANK, c * P:c * P + P],
                                        la["rank"], start=True, stop=True, skip_group_check=True)
                    ins.then_inc(gate_mm, 1)
                    for s in range(1, RING):
                        project(feature_slab, s)
                    pe.wait_ge(gate_x, 1)
                    pe.wait_ge(la_q, 2)

                    def values_and_gates(n):
                        for tb in range(NTB):
                            half_token_slab(n % RING, tb)

                    linear_attention(la, GLA_HEADS, SLAB, values_and_gates)
                    turn()
                    fresh = x_new()
                project_out(fresh if l else None)
                turn()
                ffn(3 + 2 * l)


_INS = ["x", "attn_norm", "ffn_norm", "hgrn_w_in", "hgrn_w_out", "hgrn_gate_norm", "hgrn_lower_bounds", "dsa_w_in",
        "dsa_w_out", "rel_bias", "ffn_w_up", "ffn_conv_w", "ffn_conv_b", "ffn_w_down", "final_norm", "norm_g_2",
        "ffn1_w_in_2", "ffn1_w_out_2", "ffn2_w_in_2", "ffn2_w_out_2", "hyb_w_in_2", "hyb_w_out_2", "conv_dw_w_2",
        "conv_dw_b_2", "conv_ln_g_2", "conv_ln_b_2", "gla_w_in_2", "gla_w_gate_2", "gla_b_gate_2", "gla_norm_g_2",
        "gla_w_out_2"]


def kernel(**inputs):
    import concourse.bacc as bacc
    from concourse.bass_utils import run_bass_kernel_spmd as run

    nc = bacc.Bacc("TRN2", target_bir_lowering=False, num_devices=1)
    shape_const, level_masks = shape_constants()
    arrays = {name: np.ascontiguousarray(inputs[name]) for name in _INS}
    arrays["shape_const"] = shape_const
    arrays["level_masks"] = level_masks
    A = {name: nc.dram_tensor("in_" + name, a.shape, mybir.dt.from_np(a.dtype), kind="ExternalInput").ap()
         for name, a in arrays.items()}
    out = nc.dram_tensor("out_0", (1, SEQ, D), F32, kind="ExternalOutput").ap()
    build(nc, A, out)
    r = run(nc, [{"in_" + name: a for name, a in arrays.items()}], core_ids=[0])
    return r.results[0]["out_0"]
```

```python
from contextlib import ExitStack
import math

import numpy as np
import concourse.bass as bass
from concourse import mybir

F32 = mybir.dt.float32
F32R = mybir.dt.float32r
BF16 = mybir.dt.bfloat16
U8 = mybir.dt.uint8
ALU = mybir.AluOpType
ACT = mybir.ActivationFunctionType
AX_X = mybir.AxisListType.X

P = 128
D = 1024
SEQ = 256
NTB = SEQ // P
NK = D // P
FF = 2816
SLAB = 256
NF = FF // SLAB
RING = 4
EPS = 1e-6
NEG_BIG = -1e30
TAKEN = -3e38
TINY = 1e-30
LN_EDGE = 2.0 ** -60

HG_HEADS = 8
GLA_HEADS = 4
ATT_HEADS = 16
IDX_HEADS = 8
TOP_K = 64
SB_HEADS = 8
CONV_TAPS = 31
GATE_RANK = 16
GLA_TAU = 16.0
SOFTPLUS_EDGE = 20.0
CONV_CHUNKS = 4
TAPS_AHEAD, TAPS_BETWEEN = 64, 8
BUCKETS = 32
MAX_DIST = 128
LEVELS = [64, 32, 16, 8, 4, 2, 1]
DISTS = 3 * P
WARM_STEP, WARM_HEADS = 4, 3
WARM, WARM_NORMED = 12, 18
AT_BANKS = [0, 1, 6]

IDENT, CAUSAL, STRICT, TRI, ONES, ONEHOT, ZEROS = 0, 128, 256, 384, 512, 640, 1024
CONST_COLS = ZEROS + 512


def shape_constants():
    c = np.zeros((P, ZEROS), np.float32)
    i = np.arange(P)
    row, col = i[:, None], i[None, :]
    c[:, IDENT:IDENT + P] = np.eye(P)
    c[:, CAUSAL:CAUSAL + P] = np.where(col > row, NEG_BIG, 0.0)
    c[:, STRICT:STRICT + P] = np.where(row >= col, NEG_BIG, 0.0)
    c[:, TRI:TRI + P] = np.where(row >= col, -1.0, 0.0)
    c[:, ONES:ONES + P] = -1.0
    dist = np.maximum(255 - np.arange(DISTS), 0)
    exact = BUCKETS // 2
    far = np.maximum(dist, exact).astype(np.float32)
    large = exact + (np.log(far / np.float32(exact)) / np.float32(math.log(MAX_DIST / exact))
                     * np.float32(BUCKETS - exact)).astype(np.int32)
    bucket = np.where(dist < exact, dist, np.minimum(large, BUCKETS - 1))
    c[bucket, ONEHOT + np.arange(DISTS)] = 1.0
    masks = np.zeros((P, len(LEVELS), P), np.float32)
    for n, m in enumerate(LEVELS):
        same = row // (2 * m) == col // (2 * m)
        masks[:, n] = same & (row // m % 2 == 0) & (col // m % 2 == 1)
    return c, masks


class Tally:

    def __init__(self):
        self.n = {}

    def __call__(self, sem, more=1):
        self.n[sem] = self.n.get(sem, 0) + more
        return self.n[sem]


class Uses:

    def __init__(self):
        self.uses = [0] * RING
        self.dmas = [0] * RING

    def take(self, slot, dmas=1):
        u = self.uses[slot]
        self.uses[slot] += 1
        self.dmas[slot] += 16 * dmas
        return u, self.dmas[slot]

    def skip(self, slot, n):
        self.uses[slot] += n
        self.dmas[slot] += 16 * n


def build(nc, A, out):
    with ExitStack() as ctx:
        def sb(name, shape, dt=F32):
            return ctx.enter_context(nc.sbuf_tensor(name, shape, dt))

        def sem(name):
            return ctx.enter_context(nc.semaphore(name))

        raw = [sb(f"raw{s}", [P, 2048]) for s in range(RING)]
        w_hi = [sb(f"w_hi{s}", [P, 2048], F32R) for s in range(RING)]
        w_lo = [sb(f"w_lo{s}", [P, 2048], F32R) for s in range(RING)]
        h = sb("h", [P, NTB, D])
        x_hi = sb("x_hi", [P, NK, SEQ], F32R)
        x_lo = sb("x_lo", [P, NK, SEQ], F32R)
        xn = sb("xn", [P, NTB, D])
        g_hi = sb("g_hi", [P, 2, SEQ], F32R)
        g_lo = sb("g_lo", [P, 2, SEQ], F32R)
        const = sb("const", [P, CONST_COLS])
        level_mask = sb("level_mask", [P, len(LEVELS), P], U8)
        cols = sb("cols", [P, 640])
        small = sb("small", [P, 160])
        rms_diag = sb("rms_diag", [P, NTB, P])
        arena = sb("arena", [P, 16384])
        ps = ctx.enter_context(nc.psum_tensor("ps", [P, 8, 512], F32))
        bias_dram = nc.dram_tensor("bias_rows", (ATT_HEADS, P, DISTS), F32, kind="Internal").ap()

        ident = const[:, IDENT:IDENT + P]
        zeros = const[:, ZEROS:ZEROS + 512]
        ssq = small[:, 0:2]
        ms = small[:, 2:4]
        std = small[:, 4:6]
        rstd = small[:, 6:8]
        head_ssq = small[:, 8:24]
        head_ms = small[:, 24:40]
        head_std = small[:, 40:56]
        head_rstd = small[:, 56:72]
        lb = small[:, 72:80]
        one_minus_lb = small[:, 80:88]
        lb_a = small[:, 88:96]
        lb_b = small[:, 96:104]
        top8 = small[:, 104:112]
        ln_stats = small[:, 128:140]
        ln_mv = small[:, 140:144]
        ln_std = small[:, 144:146]
        ln_rstd = small[:, 146:148]

        def words(a, n):
            return arena[:, a:a + n]

        proj = words(0, 16 * 512).rearrange("p (s n) -> p s n", n=512)
        ff_c = words(0, 1024).rearrange("p (b g t) -> p b g t", b=2, g=2)
        ff_s = words(1024, 512).rearrange("p (b t) -> p b t", b=2)
        ff_g = words(1536, 512).rearrange("p (b t) -> p b t", b=2)
        gain_row = words(15360, 1024)
        squares = words(13312, 1024)
        bias_x = words(8192, 16 * 256).rearrange("p (h c) -> p h c", h=ATT_HEADS)

        row_of, row_src, n_rows = {}, [], 0
        for name, src in [
            ("attn_norm", A["attn_norm"].rearrange("l (c p) -> (l c) p", p=P)),
            ("ffn_norm", A["ffn_norm"].rearrange("l (c p) -> (l c) p", p=P)),
            ("hgrn_gate_norm", A["hgrn_gate_norm"]),
            ("hgrn_lower_bounds", A["hgrn_lower_bounds"].rearrange("l (c p) -> (l c) p", p=P)),
            ("norm_g_2", A["norm_g_2"].rearrange("l g (c p) -> (l g c) p", p=P)),
            ("ffn_conv_w", A["ffn_conv_w"].rearrange("l k (c p) -> (l k c) p", p=P)),
            ("ffn_conv_b", A["ffn_conv_b"].rearrange("l (c p) -> (l c) p", p=P)),
            ("conv_dw_w_2", A["conv_dw_w_2"].rearrange("l k (c p) -> (l k c) p", p=P)),
            ("conv_dw_b_2", A["conv_dw_b_2"].rearrange("l (c p) -> (l c) p", p=P)),
            ("conv_ln_g_2", A["conv_ln_g_2"].rearrange("l (c p) -> (l c) p", p=P)),
            ("conv_ln_b_2", A["conv_ln_b_2"].rearrange("l (c p) -> (l c) p", p=P)),
            ("gla_b_gate_2", A["gla_b_gate_2"].rearrange("l (c p) -> (l c) p", p=P)),
            ("gla_norm_g_2", A["gla_norm_g_2"].rearrange("l (c p) -> (l c) p", p=P)),
        ]:
            row_of[name] = n_rows
            done, n = 0, src.shape[0]
            while done < n:
                k = min(n - done, P - n_rows % P)
                row_src.append((n_rows % P, n_rows // P, k, src[done:done + k, :]))
                done += k
                n_rows += k
        n_row_tiles = -(-n_rows // P)
        n_first = row_src[0][2]
        rows = words(8192, n_row_tiles * P).rearrange("p (t n) -> p t n", n=P)
        masks_in = words(10240, len(LEVELS) * P).rearrange("p (l n) -> p l n", n=P)
        rel_bias_sb = words(15360, ATT_HEADS)
        bias_vec = words(15488, DISTS)
        w_gate = words(14336, 512)

        def col(name, i=0):
            c = row_of[name] + i
            return cols[:, c:c + 1]

        raw_full = [sem(f"raw_full{s}") for s in range(RING)]
        hi_done = [sem(f"hi_done{s}") for s in range(RING)]
        slab_ready = [sem(f"slab_ready{s}") for s in range(RING)]
        slab_used = [sem(f"slab_used{s}") for s in range(RING)]
        x_in = [sem(f"x_in{tb}") for tb in range(NTB)]
        zeros_set, first_in, rows_in, tables_in = sem("zeros_set"), sem("first_in"), sem("rows_in"), sem("tables_in")
        rows_turned, cols_ready = sem("rows_turned"), sem("cols_ready")
        lb_step = sem("lb_step")
        bias_vec_done, bias_out, bias_in = sem("bias_vec_done"), sem("bias_out"), sem("bias_in")
        gain_in, gate_in = sem("gain_in"), sem("gate_in")
        h_ready, y_gained = sem("h_ready"), sem("y_gained")
        rms_sq, rms_ms, rms_std = sem("rms_sq"), sem("rms_ms"), sem("rms_std")
        xn_ready, turned, x_hi_done, x_ready = sem("xn_ready"), sem("turned"), sem("x_hi_done"), sem("x_ready")
        proj_free = [sem(f"proj_free{s}") for s in range(RING)]
        up_half = sem("up_half")
        half_done = sem("half_done")
        conv_in = [sem(f"conv_in{b}") for b in range(2)]
        tap_done = [sem(f"tap_done{b}") for b in range(2)]
        conv_done = [sem(f"conv_done{b}") for b in range(2)]
        silu_done = [sem(f"silu_done{b}") for b in range(2)]
        gt_done = [sem(f"gt_done{b}") for b in range(2)]
        gt_hi = [sem(f"gt_hi{b}") for b in range(2)]
        g_ready = sem("g_ready")
        dve_step = sem("dve_step")
        act_step = sem("act_step")
        la_gate, la_ln_in, la_ln, la_k = sem("la_gate"), sem("la_ln_in"), sem("la_ln"), sem("la_k")
        la_diff, la_exp, la_factors, la_scores = sem("la_diff"), sem("la_exp"), sem("la_factors"), sem("la_scores")
        la_masked, la_cross = sem("la_masked"), sem("la_cross")
        la_out, la_sq, la_ms, la_std, la_silu = sem("la_out"), sem("la_sq"), sem("la_ms"), sem("la_std"), sem("la_silu")
        la_q = sem("la_q")
        gate_rank, gate_mm, gate_x, gate_ln = sem("gate_rank"), sem("gate_mm"), sem("gate_x"), sem("gate_ln")
        ix_dots, ix_relu, ix_acc = sem("ix_dots"), sem("ix_relu"), sem("ix_acc")
        at_mask, at_bias, at_qk, at_max, at_exp, at_tr, at_pt, at_pv = (
            sem("at_mask"), sem("at_bias"), sem("at_qk"), sem("at_max"), sem("at_exp"), sem("at_tr"), sem("at_pt"), sem("at_pv"))
        sb_z, sb_min, sb_ln, sb_sp, sb_rest, sb_w, sb_pv = (
            sem("sb_z"), sem("sb_min"), sem("sb_ln"), sem("sb_sp"), sem("sb_rest"), sem("sb_w"), sem("sb_pv"))
        cv_tap, cv_turn, cv_ms, cv_std, cv_norm, cv_back, cv_silu = (
            sem("cv_tap"), sem("cv_turn"), sem("cv_ms"), sem("cv_std"), sem("cv_norm"), sem("cv_back"), sem("cv_silu"))
        stored = sem("stored")

        block = ctx.enter_context(nc.Block())

        def col_slab(w, c0, n=SLAB):
            return w[:, bass.ds(c0, n)].rearrange("(c p) n -> p c n", p=P)

        def row_slab(w, r0):
            return w[bass.ds(r0, SLAB), :].rearrange("(c p) n -> p c n", p=P)

        def raw_cols(s, a=0, n=SLAB):
            return raw[s][:, :].rearrange("p (c n) -> p c n", c=NK)[:, :, a:a + n]

        def raw_rows(s):
            return raw[s][:, :].rearrange("p (c n) -> p c n", c=2)

        ffn_w = [(A["ffn_w_up"][l], A["ffn_w_down"][l]) for l in range(2)]
        ffn1_w = [(A["ffn1_w_in_2"][l], A["ffn1_w_out_2"][l]) for l in range(2)]
        ffn2_w = [(A["ffn2_w_in_2"][l], A["ffn2_w_out_2"][l]) for l in range(2)]
        FFNS = [ffn_w[0], ffn_w[1], ffn1_w[0], ffn2_w[0], ffn1_w[1], ffn2_w[1]]
        hgrn_in, hgrn_out = A["hgrn_w_in"][0], A["hgrn_w_out"][0]
        dsa_in, dsa_out = A["dsa_w_in"][0], A["dsa_w_out"][0]
        hyb_in, hyb_out = A["hyb_w_in_2"][0], A["hyb_w_out_2"][0]
        gla_in, gla_out = A["gla_w_in_2"][0], A["gla_w_out_2"][0]
        DSA_K, DSA_V, DSA_QI, DSA_KI, DSA_W = 1024, 1152, 1280, 1792, 1856

        def hgrn_views():
            return dict(
                q=words(0, 2048), f=words(2048, 2048), v=proj[:, 8:12, :], gate=words(6144, 2048),
                k=words(8192, 2048), b=words(10240, 2048), qt=words(12288, 2048), ln2=words(12288, 2048),
                kt=xn[:, :, :].rearrange("p b n -> p (b n)"), scores=words(14336, 2048),
                e=words(2048, 2048), cross=words(2048, 1024), sq=[words(10240, 1024), words(11264, 1024)])

        def gla_views():
            return dict(
                q=words(0, 1024), k=words(1024, 1024), v=proj[:, 4:8, :], gate=words(4096, 2048),
                x=words(6656, 1024), f=words(6656, 1024), b=words(8704, 1024), e=words(9728, 1024),
                qt=words(10752, 1024), kt=xn[:, 0, :], scores=words(12800, 1024), cross=words(13824, 512),
                sq=[words(6656, 1024), words(7680, 1024)], rank=proj[0:GATE_RANK, 12, 0:SEQ])

        def dsa_views():
            return dict(
                q=words(0, 2048).rearrange("p (c t) -> p c t", t=SEQ), k=words(2048, 512).rearrange("p (c t) -> p c t", t=SEQ),
                qi=words(2560, 1024).rearrange("p (c t) -> p c t", t=SEQ), ki=words(3584, SEQ),
                v=words(3584 + SEQ, SEQ).rearrange("p (b n) -> p b n", b=NTB), w=words(4096, 16),
                w_scaled=words(4112, 16), att_min=words(4128, 32), att_sum=words(4160, 32), att_inv=words(4192, 32),
                relu=words(12288, 6 * 512).rearrange("p (b s) -> p b s", b=6),
                bias_0=words(12288, ATT_HEADS * P).rearrange("p (h c) -> p h c", h=ATT_HEADS),
                score=words(5120, 512).rearrange("p (b s) -> p b s", b=2), rest=words(5632, SEQ),
                mask=words(6144, 512).rearrange("p (b s) -> p b s", b=2),
                a=words(6656, 1536).rearrange("p (b s) -> p b s", b=6), pt=words(15360, 1024).rearrange("p (b s) -> p b s", b=4))

        def hyb_views():
            return dict(
                q=words(0, 1024).rearrange("p (c t) -> p c t", t=SEQ), k_all=words(1024, 1024),
                k=words(1024, 1024).rearrange("p (c t) -> p c t", t=SEQ),
                gate=words(3072, 1024).rearrange("p (s c t) -> p s c t", s=2, t=SEQ),
                v=proj[:, 8:10, :], pad=words(5120, 4 * (SEQ + CONV_TAPS - 1)).rearrange("p (c t) -> p c t", c=4),
                co=words(6400, 1024).rearrange("p (c t) -> p c t", t=SEQ), cs=words(7424, 1024).rearrange("p (c t) -> p c t", t=SEQ),
                l=words(8448, 1536).rearrange("p (b n) -> p b n", b=4),
                sp=words(9984, 1536).rearrange("p (b n) -> p b n", b=4), w=words(11520, 1536).rearrange("p (b n) -> p b n", b=4))

        def halves(t, m):
            v = t.rearrange("p (n two m) -> p n two m", two=2, m=m)
            return v[:, :, 0, :], v[:, :, 1, :]

        def v_of(la, tb, hd, dv):
            c = hd * dv
            return la["v"][:, c // SLAB, tb * SLAB + c % SLAB:tb * SLAB + c % SLAB + dv]

        @block.sync
        def _(sp):
            ring = Uses()

            def load(slot, pieces):
                u, _ = ring.take(slot, len(pieces))
                sp.wait_ge(slab_ready[slot], u + 1)
                for dst, src in pieces:
                    sp.dma_start(dst, src).then_inc(raw_full[slot], 16)

            def load_four_columns(w, c0, n):
                with sp.Fori(0, n) as i:
                    for s in range(RING):
                        sp.wait_ge(slab_ready[s], i + (ring.uses[s] + 1))
                        sp.dma_start(raw_cols(s), col_slab(w, i * (RING * SLAB) + (c0 + s * SLAB))).then_inc(raw_full[s], 16)
                for s in range(RING):
                    ring.skip(s, n)

            def load_out(w):
                for s in range(RING):
                    load(s, [(raw_rows(s), row_slab(w, s * SLAB))])

            def load_ffn(f):
                up, down = FFNS[f]
                load(0, [(raw_cols(0), col_slab(up, 0))])
                load(1, [(raw_cols(1), col_slab(up, FF))])
                with sp.Fori(0, NF - 1) as i:
                    sp.wait_ge(slab_ready[0], i + (ring.uses[0] + 1))
                    sp.dma_start(raw_cols(0), col_slab(up, i * SLAB + SLAB)).then_inc(raw_full[0], 16)
                    sp.wait_ge(slab_ready[1], i + (ring.uses[1] + 1))
                    sp.dma_start(raw_cols(1), col_slab(up, i * SLAB + (FF + SLAB))).then_inc(raw_full[1], 16)
                    sp.wait_ge(slab_ready[2], i + (ring.uses[2] + 1))
                    sp.dma_start(raw_rows(2), row_slab(down, i * SLAB)).then_inc(raw_full[2], 16)
                for s in range(3):
                    ring.skip(s, NF - 1)
                load(3, [(raw_rows(3), row_slab(down, (NF - 1) * SLAB))])

            for tb in range(NTB):
                sp.dma_start(h[:, tb, :], A["x"][0, tb * P:tb * P + P, :]).then_inc(x_in[tb], 16)
            for s in range(RING):
                load(s, [(raw_cols(s), col_slab(hgrn_in, s * SLAB))])
            for p0, t, k, src in row_src[1:]:
                sp.dma_start(rows[p0:p0 + k, t, :], src).then_inc(rows_in, 16)
            sp.dma_start(const[:, CAUSAL:ZEROS], A["shape_const"][:, CAUSAL:ZEROS]).then_inc(tables_in, 16)
            sp.dma_start(masks_in, A["level_masks"]).then_inc(tables_in, 16)
            sp.dma_start(rel_bias_sb[0:BUCKETS, :], A["rel_bias"]).then_inc(tables_in, 16)
            load_four_columns(hgrn_in, RING * SLAB, 3)
            load_out(hgrn_out)
            load_ffn(0)
            ki = dsa_in[:, DSA_KI:DSA_KI + 64].rearrange("(c p) n -> p c n", p=P)
            load(0, [(raw_cols(0, 0, 64), ki), (raw_cols(0, 64, 64), ki), (raw_cols(0, P, P), col_slab(dsa_in, DSA_V, P))])
            load(1, [(raw_cols(1), col_slab(dsa_in, DSA_QI))])
            load(2, [(raw_cols(2), col_slab(dsa_in, DSA_QI + SLAB))])
            load(3, [(raw_cols(3, 0, IDX_HEADS), col_slab(dsa_in, DSA_W, IDX_HEADS))])
            for s in range(RING):
                load(s, [(raw_cols(s), col_slab(dsa_in, s * SLAB))])
            k0, k1 = (dsa_in[:, DSA_K + 64 * j:DSA_K + 64 * j + 64].rearrange("(c p) n -> p c n", p=P) for j in range(2))
            load(0, [(raw_cols(0, 64 * j, 64), k) for j, k in enumerate([k0, k0, k1, k1])])
            load_out(dsa_out)
            load_ffn(1)
            load_ffn(2)
            load_four_columns(hyb_in, 6 * SLAB, 1)
            load_four_columns(hyb_in, 0, 1)
            for s in range(2):
                load(s, [(raw_cols(s), col_slab(hyb_in, 4 * SLAB + s * SLAB))])
            load_out(hyb_out)
            load_ffn(3)
            load_ffn(4)
            load(2, [(raw_cols(2, 0, GATE_RANK), col_slab(gla_in, 12 * SLAB, GATE_RANK))])
            load_four_columns(gla_in, 0, 3)
            load_out(gla_out)
            load_ffn(5)
            for tb in range(NTB):
                sp.wait_ge(h_ready, 2 * 11 - 1 + tb)
                sp.dma_start(out[0, tb * P:tb * P + P, :], h[:, tb, :]).then_inc(stored, 16)
            sp.wait_ge(stored, 16 * NTB)

        @block.gpsimd
        def _(pool):
            ring = Uses()

            def low(slot, u):
                pool.wait_ge(hi_done[slot], u + 1)
                pool.tensor_tensor(w_lo[slot][:, :], raw[slot][:, :], w_hi[slot][:, :].bitcast(F32), ALU.subtract)\
                    .then_inc(slab_ready[slot], 1)

            def low_one(slot):
                u, _ = ring.take(slot)
                low(slot, u)

            def low_four(n):
                with pool.Fori(0, n) as i:
                    for s in range(RING):
                        low(s, i + ring.uses[s])
                for s in range(RING):
                    ring.skip(s, n)

            def low_ffn():
                low_one(0)
                low_one(1)
                with pool.Fori(0, NF - 1) as i:
                    low(2, i + ring.uses[2])
                for s in range(3):
                    ring.skip(s, NF - 1)
                low_one(3)

            pool.memset(zeros, 0.0).then_inc(zeros_set, 1)
            pool.memset(xn[:, :, :], 0.0)
            low_four(3)
            pool.wait_ge(la_gate, 1)
            for hd in range(HG_HEADS):
                k = hgrn_views()["k"][:, hd * SEQ:hd * SEQ + SEQ]
                ins = pool.tensor_scalar(k, k, one_minus_lb[:, hd:hd + 1], None, ALU.mult)
            ins.then_inc(la_k, 1)
            low_four(2)
            low_ffn()
            low_four(2)
            low_one(0)
            pool.wait_ge(bias_in, 16)
            dsa = dsa_views()
            for tb in range(NTB):
                pool.wait_ge(at_mask, tb + 1)
                if tb:
                    pool.wait_ge(at_bias, 4)
                for g in range(0, ATT_HEADS, 4):
                    S = (tb + 1) * P
                    dst = bias_x[:, g:g + 4, :] if tb else dsa["bias_0"][:, g:g + 4, :]
                    pool.tensor_tensor(dst, bias_x[:, g:g + 4, SEQ - S:SEQ],
                                       dsa["mask"][:, tb, 0:S].unsqueeze(1).broadcast_to([P, 4, S]), ALU.add).then_inc(at_bias, 1)
            for s in (1, 2, 3, 0):
                low_one(s)
            low_ffn()
            low_ffn()
            low_four(2)
            low_one(0)
            low_one(1)
            low_four(1)
            low_ffn()
            low_ffn()
            low_one(2)
            low_four(4)
            low_ffn()

        @block.scalar
        def _(act):
            ring, want = Uses(), Tally()
            products_done = 4
            made = [0] * RING

            def link(ins):
                ins.then_inc(act_step, 1)
                act.wait_ge(act_step, want(act_step))

            def high(slot, u, full):
                act.wait_ge(raw_full[slot], full)
                act.wait_ge(slab_used[slot], u + 1)
                act.activation(w_hi[slot][:, :], raw[slot][:, :], ACT.Copy).then_inc(hi_done[slot], 1)

            def high_one(slot, dmas=1):
                high(slot, *ring.take(slot, dmas))

            def high_four(n):
                with act.Fori(0, n) as i:
                    for s in range(RING):
                        high(s, i + ring.uses[s], i * 16 + (ring.dmas[s] + 16))
                for s in range(RING):
                    ring.skip(s, n)

            def all_copied():
                for s in range(RING):
                    act.wait_ge(proj_free[s], made[s] + 1)

            def evacuate(s, dst, scale=1.0, func=ACT.Copy):
                act.wait_ge(slab_used[s], ring.uses[s] + 1)
                ins = act.activation(dst, ps[:, 4 + s, :], func, scale=scale).then_inc(proj_free[s], 1)
                made[s] += 1
                return ins

            def preload_sqrt():
                return act.activation(small[:, 152:153], const[:, ZEROS:ZEROS + 1], ACT.Sqrt)

            def root(tb):
                act.wait_ge(rms_ms, want(rms_ms))
                act.activation(std[:, tb:tb + 1], ms[:, tb:tb + 1], ACT.Sqrt).then_inc(rms_std, 1)

            def rms_residual(updates):
                preload_sqrt()
                for tb in range(NTB):
                    if updates:
                        act.wait_ge(h_ready, 2 * updates - 1 + tb)
                    else:
                        act.wait_ge(x_in[tb], 16)
                    act.activation(squares, h[:, tb, :], ACT.Square, accum_out=ssq[:, tb:tb + 1]).then_inc(rms_sq, 1)
                    root(tb)

            def split_turned(gains):
                for c in range(NK):
                    if c % 2 == 0:
                        act.wait_ge(turned, want(turned))
                    act.activation(x_hi[:, c, :], ps[:, 4 + c // 2, c % 2 * SEQ:c % 2 * SEQ + SEQ], ACT.Copy,
                                   scale=gains[c]).then_inc(x_hi_done, 1)

            def norm(name, i, updates):
                rms_residual(updates)
                split_turned([col(name, i * NK + c) for c in range(NK)])

            def product_done(tb):
                if tb == 0:
                    act.wait_ge(half_done, products_done + 1)
                else:
                    act.wait_ge(slab_used[3], ring.uses[3] + 1)

            def rms_product():
                nonlocal products_done
                preload_sqrt()
                for tb in range(NTB):
                    product_done(tb)
                    act.activation(squares, ps[:, 2 * tb:2 * tb + 2, :].rearrange("p b n -> p (b n)"), ACT.Square,
                                   accum_out=ssq[:, tb:tb + 1]).then_inc(rms_sq, 1)
                    root(tb)
                products_done += 1

            def ffn(conv, f_conv, f):
                b0, b1, b2 = ring.uses[0], ring.uses[1], ring.uses[2]
                m0, m1, m2 = ring.dmas[0], ring.dmas[1], ring.dmas[2]
                q0 = f * NF

                def up_done(b, i):
                    if b == 0:
                        act.wait_ge(up_half, i + (q0 + 1))
                    else:
                        act.wait_ge(slab_used[1], i + (b1 - 1 + 2))

                def start_gate(b, i, odd):
                    up_done(b, i)
                    bank = ps[:, 4 + 2 * odd + b, :]
                    if conv:
                        for g in range(2):
                            c = i * 2 + (row_of["ffn_conv_w"] + f_conv * 132 + 88 + g * 22 + b)
                            cb = i * 2 + (row_of["ffn_conv_b"] + f_conv * 44 + g * 22 + b)
                            ins = act.activation(ff_c[:, b, g, :], bank[:, g * SEQ:g * SEQ + SEQ], ACT.Identity,
                                                 bias=cols[:, bass.ds(cb, 1)], scale=cols[:, bass.ds(c, 1)])
                        ins.then_inc(conv_in[b], 1)
                    else:
                        act.activation(ff_s[:, b, :], bank[:, 0:SEQ], ACT.Silu).then_inc(silu_done[b], 1)

                def conv_silu(b, i):
                    act.wait_ge(conv_done[b], i + (f_conv * NF + 1))
                    act.activation(ff_s[:, b, :], ff_c[:, b, 0, :], ACT.Silu).then_inc(silu_done[b], 1)

                def split(b, i, last):
                    act.wait_ge(gt_done[b], i + (q0 + 2))
                    if b == 0 and not last:
                        act.wait_ge(slab_used[2], i + (b2 + 1))
                    dst = x_hi if last else g_hi
                    act.activation(dst[:, b, :], ff_g[:, b, :], ACT.Copy).then_inc(gt_hi[b], 1)

                def body(i, odd, last):
                    if last:
                        high_one(3)
                    else:
                        high(0, i + b0, i * 16 + (m0 + 16))
                    start_gate(0, i, odd)
                    start_gate(1, i, odd)
                    if conv:
                        conv_silu(0, i)
                    if not last:
                        high(1, i + b1, i * 16 + (m1 + 16))
                    if conv:
                        conv_silu(1, i)
                    split(0, i, last)
                    split(1, i, last)
                    if not last:
                        high(2, i + b2, i * 16 + (m2 + 16))

                with act.Fori(0, NF // 2) as j:
                    for odd in range(2):
                        body(j * 2 + odd, odd, False)
                body(NF - 1, 0, True)
                for s in range(3):
                    ring.skip(s, NF - 1)

            act.dma_start(ident, A["shape_const"][:, IDENT:IDENT + P]).then_inc(first_in, 16)
            p0, t, k, src = row_src[0]
            act.dma_start(rows[p0:p0 + k, t, :], src).then_inc(first_in, 16)
            act.wait_ge(zeros_set, 1)
            rms_residual(0)

            def columns(a, z, times):
                act.wait_ge(rows_turned, times)
                act.activation(cols[:, a:z], ps[:, 0:2, :].rearrange("p b n -> p (b n)")[:, a:z], ACT.Copy).then_inc(cols_ready, 1)

            columns(0, n_first, 1)
            high_one(0)
            act.wait_ge(cols_ready, 1)
            split_turned([col("attn_norm", c) for c in range(NK)])
            for s in range(1, RING):
                high_one(s)

            def linear_attention(H, slabs, last):
                for n, m in enumerate(LEVELS + [P]):
                    for half in halves(la["e"], m):
                        act.wait_ge(la_diff, want(la_diff))
                        act.activation(half, half, ACT.Exp).then_inc(la_exp, 1)
                    if n in slabs:
                        s, dst = slabs[n]
                        evacuate(s, dst)
                        high_one(s)
                n = SLAB * 2 * (RING - len(last))
                for s in range(RING - len(last)):
                    act.wait_ge(proj_free[s], made[s] + 1)
                act.activation(la["gate"][:, 0:n], la["gate"][:, 0:n], ACT.Silu)
                for s in last:
                    evacuate(s, la["gate"][:, s * 512:s * 512 + 512], func=ACT.Silu)
                preload_sqrt().then_inc(la_silu, 1)
                for tb in range(NTB):
                    act.wait_ge(la_out, want(la_out))
                    act.activation(la["sq"][tb], ps[:, 2 * tb:2 * tb + 2, :].rearrange("p b n -> p (b n)"), ACT.Square)\
                        .then_inc(la_sq, 1)
                    act.wait_ge(la_ms, want(la_ms))
                    at = tb * H
                    act.activation(head_std[:, at:at + H], head_ms[:, at:at + H], ACT.Sqrt).then_inc(la_std, 1)
                for s in last:
                    high_one(s)

            la = hgrn_views()
            high_four(1)
            columns(n_first, n_rows, 2)
            act.wait_ge(lb_step, 1)
            act.activation(lb_b, lb_a, ACT.Exp).then_inc(lb_step, 1)
            act.wait_ge(bias_vec_done, 1)
            link(act.activation(bias_vec[0:ATT_HEADS, :], ps[0:ATT_HEADS, 2, 0:DISTS], ACT.Copy, scale=-1.0))
            act.dma_start(bias_dram, bias_vec[0:ATT_HEADS, :].unsqueeze(1).broadcast_to([ATT_HEADS, P, DISTS]))\
                .then_inc(bias_out, 16)
            high_four(1)
            for s in range(RING):
                made[s] += 2
            all_copied()
            act.activation(la["k"], la["f"], ACT.Sigmoid, scale=-1.0)
            act.activation(la["f"], la["f"], ACT.Sigmoid).then_inc(la_gate, 1)
            for s in range(RING):
                evacuate(s, proj[:, 8 + s, :])
                high_one(s)
                if s == 0:
                    act.wait_ge(la_ln_in, 1)
                    act.activation(la["f"], la["f"], ACT.Ln)
                    act.activation(la["ln2"], la["ln2"], ACT.Ln, scale=1.0 / LN_EDGE).then_inc(la_ln, 1)
            linear_attention(HG_HEADS, {2 * s + 2: (s, proj[:, 12 + s, :]) for s in range(3)}, [3])
            split_turned([col("hgrn_gate_norm")] * NK)
            high_one(0)
            high_one(1)
            norm("ffn_norm", 0, 1)
            ffn(True, 0, 0)

            act.wait_ge(bias_out, 16)
            act.wait_ge(h_ready, 2 * 1)
            act.dma_start(bias_x[:, :, :], bass.AP(bias_dram.tensor, P - 1, [[DISTS - 1, P], [P * DISTS, ATT_HEADS], [1, SEQ]]))\
                .then_inc(bias_in, 16)
            high_one(0, 3)
            high_one(1)
            norm("attn_norm", 1, 2)
            high_one(2)
            high_one(3)
            for s in range(RING):
                made[s] += 1
            high_four(1)
            dsa = dsa_views()

            def index_relu(bank):
                act.wait_ge(ix_dots, bank + 1)
                act.activation(dsa["relu"][:, bank, :], ps[:, bank % 4, :], ACT.Relu).then_inc(ix_relu, 1)

            q_words = words(0, 2048).rearrange("p (s n) -> p s n", s=RING)
            evacuate(0, q_words[:, 0, :])
            high_one(0, 4)
            for bank in range(4):
                index_relu(bank)
            evacuate(1, q_words[:, 1, :])
            for bank in range(4, 6):
                index_relu(bank)
            for s in range(2, RING):
                evacuate(s, q_words[:, s, :])
            evacuate(0, words(2048, 512), -64 ** -0.5)
            UNITS = NTB * ATT_HEADS

            def exps(n):
                S = (n // ATT_HEADS + 1) * P
                act.wait_ge(at_max, n + 1)
                act.activation(dsa["a"][:, n % 6, 0:S], dsa["a"][:, n % 6, 0:S], ACT.Exp, scale=-1.0,
                               bias=dsa["att_min"][:, n:n + 1], accum_out=dsa["att_sum"][:, n:n + 1]).then_inc(at_exp, 1)

            SPLITS = range(10, 30, 5)
            for n in range(UNITS):
                exps(n)
                if n in SPLITS:
                    high_one((1 + SPLITS.index(n)) % RING)
            split_turned([1.0] * NK)
            high_one(0)
            high_one(1)
            norm("ffn_norm", 1, 3)
            ffn(True, 1, 1)

            def fetch_gain(src):
                act.dma_start(gain_row, src.unsqueeze(0).broadcast_to([P, D])).then_inc(gain_in, 16)

            def pre(l, g, updates):
                norm("norm_g_2", l * 6 + g, updates)

            high_one(0)
            high_one(1)
            fetch_gain(A["final_norm"])
            rms_residual(4)
            updates = 5
            for l in range(2):
                pre(l, 0, updates)
                act.wait_ge(h_ready, 2 * updates)
                fetch_gain(A["norm_g_2"][l, 1])
                ffn(False, 0, 2 + 2 * l)
                if l == 1:
                    high_one(2)
                high_one(0)
                if l == 0:
                    high_one(1)
                rms_product()
                updates += 1
                pre(l, 2, updates)
                if l == 1:
                    high_one(1)
                high_one(2)
                high_one(3)
                act.wait_ge(h_ready, 2 * updates)
                fetch_gain(A["norm_g_2"][l, 3])
                if l == 0:
                    hyb = hyb_views()
                    made[0] += 1
                    made[1] += 1
                    high_one(0)
                    high_one(1)
                    for s in (2, 3):
                        evacuate(s, hyb["gate"][:, s - 2, :, :].rearrange("p c t -> p (c t)"), func=ACT.Sigmoid)
                        high_one(s)
                    for s in range(RING):
                        evacuate(s, words(s * 512, 512), 1.0 if s < 2 else 64 ** -0.5)
                        high_one(s)

                    def values_half(s):
                        evacuate(s, hyb["v"][:, s, :])
                        high_one(s)

                    values_half(0)
                    for pair in range(SB_HEADS // 2 + 1):
                        if pair < SB_HEADS // 2:
                            for hd in (2 * pair, 2 * pair + 1):
                                act.wait_ge(sb_min, hd + 1)
                                logs = hyb["l"][:, hd % 4, :]
                                link(act.activation(logs, logs, ACT.Exp))
                            for hd in (2 * pair, 2 * pair + 1):
                                logs = hyb["l"][:, hd % 4, :]
                                act.activation(logs, logs, ACT.Ln, bias=1.0).then_inc(sb_ln, 1)
                        if pair == 0:
                            values_half(1)
                        if pair >= 1:
                            for hd in (2 * pair - 2, 2 * pair - 1):
                                act.wait_ge(sb_rest, hd + 1)
                                if hd >= 4:
                                    act.wait_ge(sb_pv, hd - 3)
                                act.activation(hyb["w"][:, hd % 4, :], ps[:, hd % 4, 0:3 * P], ACT.Exp).then_inc(sb_w, 1)
                    act.wait_ge(cv_ms, 1)
                    act.activation(ln_std, ln_mv.rearrange("p (b s) -> p b s", s=2)[:, :, 1], ACT.Sqrt).then_inc(cv_std, 1)
                    act.wait_ge(sb_pv, SB_HEADS)
                    for b in range(2):
                        act.activation(x_hi[:, 2 * b:2 * b + 2, :].rearrange("p c t -> p (c t)"), ps[:, 4 + b, :], ACT.Copy)\
                            .then_inc(x_hi_done, 1)
                    for c in range(4):
                        act.wait_ge(cv_back, c // 2 + 1)
                        act.activation(hyb["cs"][:, c, :], ps[:, 6 + c // 2, c % 2 * SEQ:c % 2 * SEQ + SEQ], ACT.Silu,
                                       bias=col("conv_ln_b_2", c), scale=col("conv_ln_g_2", c)).then_inc(cv_silu, 1)
                    for c in range(4):
                        act.wait_ge(cv_silu, c + 1)
                        act.activation(x_hi[:, 4 + c, :], hyb["cs"][:, c, :], ACT.Copy).then_inc(x_hi_done, 1)
                else:
                    la = gla_views()
                    act.dma_start(w_gate[0:GATE_RANK, :], A["gla_w_gate_2"][0]).then_inc(gate_in, 16)
                    for s in range(RING):
                        made[s] += 1
                    for c in range(4):
                        act.wait_ge(gate_mm, 1)
                        ins = act.activation(la["x"][:, c * SEQ:c * SEQ + SEQ], ps[:, 1 + c // 2, c % 2 * SEQ:c % 2 * SEQ + SEQ],
                                             ACT.Identity, bias=col("gla_b_gate_2", c))
                    ins.then_inc(gate_x, 1)
                    act.wait_ge(gate_x, 1)
                    link(act.activation(la["e"], la["x"], ACT.Abs))
                    link(act.activation(la["e"], la["e"], ACT.Exp, scale=-1.0))
                    act.activation(la["e"], la["e"], ACT.Ln, bias=1.0).then_inc(gate_ln, 1)
                    high_four(1)
                    linear_attention(GLA_HEADS, {j + 1: (j % RING, proj[:, 4 + j, :]) for j in range(6)}, [2, 3])
                    split_turned([col("gla_norm_g_2", c % 2) for c in range(NK)])
                high_one(0)
                high_one(1)
                rms_product()
                updates += 1
                pre(l, 4, updates)
                act.wait_ge(h_ready, 2 * updates)
                fetch_gain(A["norm_g_2"][l, 5])
                ffn(False, 0, 3 + 2 * l)
                if l == 0:
                    high_one(0)
                    high_one(1)
                rms_product()
                updates += 1

        @block.vector
        def _(dve):
            used, made, want = [0] * RING, [0] * RING, Tally()

            def all_copied():
                for s in range(RING):
                    dve.wait_ge(proj_free[s], made[s] + 1)

            def link(ins):
                ins.then_inc(dve_step, 1)
                dve.wait_ge(dve_step, want(dve_step))

            def flat(bank, n=1):
                return ps[:, bank:bank + n, :].rearrange("p b n -> p (b n)")

            def copy_product(s, at, parts=(P, 512), scale=1.0):
                used[s] += 1
                made[s] += 1
                dve.wait_ge(slab_used[s], used[s] + 1)
                dst, src = arena[0:parts[0], at:at + parts[1]], ps[0:parts[0], 4 + s, 0:parts[1]]
                dve.tensor_scalar(dst, src, scale, None, ALU.mult).then_inc(proj_free[s], 1)

            def copy_products(n, at):
                for j in range(n):
                    copy_product(j % RING, at + j * 512)

            def copy_four(n, at):
                with dve.Fori(0, n) as i:
                    for s in range(RING):
                        dve.wait_ge(slab_used[s], i + (used[s] + 2))
                        dve.tensor_copy(arena[:, bass.ds(i * 2048 + (at + s * 512), 512)], ps[:, 4 + s, :]).then_inc(proj_free[s], 1)
                for s in range(RING):
                    used[s] += n
                    made[s] += n

            def mean_square(tb):
                dve.wait_ge(rms_sq, want(rms_sq))
                dve.tensor_scalar(ms[:, tb:tb + 1], ssq[:, tb:tb + 1], 1.0 / D, EPS, ALU.mult, ALU.add).then_inc(rms_ms, 1)

            def inverse_root(tb, half=False):
                one = slice(tb, tb + 1)
                dve.wait_ge(rms_std, want(rms_std))
                link(dve.reciprocal(rstd[:, one], std[:, one]))
                if half:
                    link(dve.tensor_scalar(rstd[:, one], rstd[:, one], 0.5, None, ALU.mult))
                return rstd[:, one]

            def inverse_rms(tb):
                mean_square(tb)
                return inverse_root(tb)

            def split_turned(gains):
                for c in range(NK):
                    if c % 2 == 0:
                        dve.wait_ge(x_hi_done, want(x_hi_done, 2))
                    dve.scalar_tensor_tensor(x_lo[:, c, :], ps[:, 4 + c // 2, c % 2 * SEQ:c % 2 * SEQ + SEQ], gains[c],
                                             x_hi[:, c, :].bitcast(F32), ALU.mult, ALU.subtract).then_inc(x_ready, 1)

            def norm_block(tb):
                r = inverse_rms(tb)
                dve.tensor_scalar(rms_diag[:, tb, :], ident, r, None, ALU.mult).then_inc(xn_ready, 1)

            def split_normed(name, i):
                split_turned([col(name, i * NK + c) for c in range(NK)])

            def norm(name, i):
                for tb in range(NTB):
                    norm_block(tb)
                split_normed(name, i)

            def product_done(tb):
                if tb == 0:
                    dve.wait_ge(half_done, want(half_done))
                else:
                    dve.wait_ge(slab_used[3], used[3] + 1)

            def add_product(then=lambda tb: None):
                for tb in range(NTB):
                    product_done(tb)
                    dve.tensor_tensor(h[:, tb, :], h[:, tb, :], flat(2 * tb, 2), ALU.add).then_inc(h_ready, 1)
                    then(tb)

            def add_normed_product(half):
                dve.wait_ge(gain_in, want(gain_in, 16))
                for tb in range(NTB):
                    product_done(tb)
                    mean_square(tb)
                    dve.tensor_tensor(xn[:, tb, 0:512], flat(2 * tb), gain_row[:, 0:512], ALU.mult).then_inc(y_gained, 1)
                    r = inverse_root(tb, half)
                    dve.tensor_tensor(xn[:, tb, 512:1024], flat(2 * tb + 1), gain_row[:, 512:1024], ALU.mult).then_inc(y_gained, 1)
                    dve.wait_ge(y_gained, want(y_gained, 2))
                    dve.scalar_tensor_tensor(h[:, tb, :], xn[:, tb, :], r, h[:, tb, :], ALU.mult, ALU.add).then_inc(h_ready, 1)

            def out_used():
                for s in range(RING):
                    used[s] += 1

            def ffn(conv, f_conv, f):
                q0 = f * NF

                def body(i, odd, last):
                    def low(slot):
                        dve.wait_ge(hi_done[slot], i + (used[slot] + 2))
                        dve.tensor_tensor(w_lo[slot][:, :], raw[slot][:, :], w_hi[slot][:, :].bitcast(F32), ALU.subtract)\
                            .then_inc(slab_ready[slot], 1)

                    if not last:
                        low(0)
                    if conv:
                        for b in range(2):
                            bank = ps[:, 4 + 2 * odd + b, :]

                            def tap(g, k):
                                shift = 2 - k
                                c = i * 2 + (row_of["ffn_conv_w"] + f_conv * 132 + k * 44 + g * 22 + b)
                                dst = ff_c[:, b, g, shift:SEQ]
                                return dve.scalar_tensor_tensor(dst, bank[:, g * SEQ:g * SEQ + SEQ - shift],
                                                                cols[:, bass.ds(c, 1)], dst, ALU.mult, ALU.add)
                            dve.wait_ge(conv_in[b], i + (f_conv * NF + 1))
                            tap(0, 1).then_inc(tap_done[b], 1)
                            tap(1, 1).then_inc(tap_done[b], 1)
                            dve.wait_ge(tap_done[b], i * 2 + (f_conv * NF * 2 + 2))
                            tap(0, 0)
                            tap(1, 0).then_inc(conv_done[b], 1)
                    for b in range(2):
                        dve.wait_ge(silu_done[b], i + (q0 + 1))
                        if b == 0:
                            dve.wait_ge(g_ready, i * 2 + 2 * q0)
                        up = ff_c[:, b, 1, :] if conv else ps[:, 4 + 2 * odd + b, SEQ:2 * SEQ]
                        dve.tensor_tensor(ff_g[:, b, :], ff_s[:, b, :], up, ALU.mult).then_inc(gt_done[b], 1)
                    if not last:
                        low(1)
                    for b in range(2):
                        dve.wait_ge(gt_hi[b], i + (q0 + 1))
                        lo, hi = (x_lo, x_hi) if last else (g_lo, g_hi)
                        dve.tensor_tensor(lo[:, b, :], ff_g[:, b, :], hi[:, b, :].bitcast(F32), ALU.subtract)\
                            .then_inc(g_ready, 1)

                with dve.Fori(0, NF // 2) as j:
                    for odd in range(2):
                        body(j * 2 + odd, odd, False)
                body(NF - 1, 0, True)
                used[0] += NF
                used[1] += NF
                used[2] += NF - 1
                used[3] += 1

            def linear_attention(la, H, dv, gains):
                q, k, qt, kt, b, e = la["q"], la["k"], la["qt"], la["kt"], la["b"], la["e"]
                scores = la["scores"]
                banks = H // 2

                def differences(n):
                    m = levels[n]
                    b_lo, b_up = halves(b, m)
                    e_lo, e_up = halves(e, m)
                    r = b_lo[:, :, m - 1:m].broadcast_to([P, H * SEQ // (2 * m), m])
                    if n:
                        dve.wait_ge(la_factors, want(la_factors, 2))
                    for dst, x, y in ((e_lo, r, b_lo), (e_up, b_up, r)):
                        dve.tensor_tensor(dst, x, y, ALU.subtract).then_inc(la_diff, 1)

                def by_head(t, bank):
                    return t[:, bank * 512:bank * 512 + 512].rearrange("p (n t) -> p n t", t=P)

                for hd in range(H):
                    a = hd * SEQ
                    ins = dve.tensor_tensor_scan(b[:, a:a + SEQ], la["f"][:, a:a + SEQ], zeros[:, 0:SEQ], 0.0, ALU.add, ALU.add)
                link(ins)
                levels = LEVELS + [P]
                differences(0)
                for n in range(banks):
                    dve.wait_ge(la_scores, want(la_scores))
                    ins = dve.tensor_tensor(by_head(scores, n), by_head(flat(n), 0),
                                            ident.unsqueeze(1).broadcast_to([P, 4, P]), ALU.mult)
                ins.then_inc(la_masked, 1)
                def masked(n):
                    m = levels[n]
                    mask = level_mask[:, n, :].rearrange("p (n two m) -> p n two m", two=2, m=m)[:, :, 1, :]
                    mask = mask.unsqueeze(1).broadcast_to([P, 8, P // (2 * m), m])
                    dve.wait_ge(la_masked, want(la_masked))
                    for bank in range(H // 4):
                        dve.wait_ge(la_scores, want(la_scores))
                        at = scores[:, bank * 1024:bank * 1024 + 1024]\
                            .rearrange("p (b n two m) -> p b n two m", b=8, two=2, m=m)[:, :, :, 1, :]
                        src = flat(2 * (n % 2) + bank).rearrange("p (b n m) -> p b n m", b=8, m=m)
                        ins = dve.copy_predicated(at, mask, src)
                    ins.then_inc(la_masked, 1)

                for n, m in enumerate(levels):
                    if 1 <= n < len(LEVELS):
                        dve.wait_ge(la_scores, want(la_scores, 0) + H // 4)
                    for t, x, part in ((kt, k, 0), (qt, q, 1)):
                        dve.wait_ge(la_exp, want(la_exp))
                        dve.tensor_tensor(halves(t, m)[part], halves(x, m)[part], halves(e, m)[part], ALU.mult)\
                            .then_inc(la_factors, 1)
                    if n < len(LEVELS):
                        differences(n + 1)
                        if n:
                            masked(n - 1)
                    if n == len(LEVELS) - 1:
                        masked(n)
                want(la_masked)
                dve.wait_ge(la_factors, want(la_factors, 2))
                dve.wait_ge(la_scores, want(la_scores, H // 4))
                dve.tensor_copy(la["cross"][:, 0:H * P], flat(4, H // 4)).then_inc(la_cross, 1)
                gate = la["gate"].rearrange("p (s n) -> p s n", n=512)
                for tb in range(NTB):
                    a, z = tb * H, tb * H + H
                    dve.wait_ge(la_sq, want(la_sq))
                    link(dve.tensor_reduce(head_ssq[:, a:z], la["sq"][tb].rearrange("p (h d) -> p h d", d=dv), AX_X, ALU.add))
                    dve.tensor_scalar(head_ms[:, a:z], head_ssq[:, a:z], 1.0 / dv, EPS, ALU.mult, ALU.add).then_inc(la_ms, 1)
                    dve.wait_ge(la_std, want(la_std))
                    link(dve.reciprocal(head_rstd[:, a:z], head_std[:, a:z]))
                    if tb == 0:
                        dve.wait_ge(la_silu, want(la_silu))
                    for hd in range(H):
                        c = hd * dv
                        ins = dve.scalar_tensor_tensor(
                            xn[:, tb, c:c + dv], ps[:, 2 * tb + c // 512, c % 512:c % 512 + dv], head_rstd[:, a + hd:a + hd + 1],
                            gate[:, c // SLAB, tb * SLAB + c % SLAB:tb * SLAB + c % SLAB + dv], ALU.mult, ALU.mult)
                    ins.then_inc(xn_ready, 1)
                split_turned(gains)

            def low_of_banks(n):
                for b in range(n):
                    dve.wait_ge(x_hi_done, want(x_hi_done))
                    dve.tensor_tensor(x_lo[:, 2 * b:2 * b + 2, :].rearrange("p c t -> p (c t)"), ps[:, 4 + b, :],
                                      x_hi[:, 2 * b:2 * b + 2, :].bitcast(F32).rearrange("p c t -> p (c t)"), ALU.subtract)\
                        .then_inc(x_ready, 1)

            for s in range(RING):
                dve.sem_inc(slab_ready[s], 1)
                dve.sem_inc(slab_used[s], 1)
                dve.sem_inc(proj_free[s], 1)
            for b in range(2):
                dve.sem_inc(gt_done[b], 1)
            dve.wait_ge(first_in, 2 * 16)
            for tb in range(NTB):
                norm_block(tb)
            dve.wait_ge(cols_ready, 1)
            split_normed("attn_norm", 0)
            copy_four(1, 0)
            dve.wait_ge(tables_in, 3 * 16)
            dve.wait_ge(cols_ready, 2)
            link(dve.tensor_copy(level_mask[:, :, :], masks_in))
            lb_col = cols[:, row_of["hgrn_lower_bounds"]:row_of["hgrn_lower_bounds"] + NK]
            dve.tensor_tensor(lb_a, lb_col, lb_col, ALU.subtract).then_inc(lb_step, 1)
            dve.wait_ge(lb_step, 2)
            link(dve.reciprocal(lb_a, lb_b))
            link(dve.tensor_tensor(lb_b, lb_b, lb_a, ALU.mult))
            link(dve.tensor_tensor(lb, lb_b, lb_b, ALU.subtract))
            link(dve.tensor_scalar(one_minus_lb, lb, -1.0, 1.0, ALU.mult, ALU.add))
            copy_four(1, 2048)
            for s in range(RING):
                used[s] += 2
                made[s] += 2
            la = hgrn_views()
            dve.wait_ge(la_gate, 1)
            for hd in range(HG_HEADS):
                f = la["f"][:, hd * SEQ:hd * SEQ + SEQ]
                ins = dve.tensor_scalar(f, f, one_minus_lb[:, hd:hd + 1], lb[:, hd:hd + 1], ALU.mult, ALU.add)
            link(ins)
            dve.tensor_scalar(la["ln2"], la["f"], TINY, LN_EDGE, ALU.max, ALU.min)
            dve.tensor_scalar(la["f"], la["f"], LN_EDGE, None, ALU.max).then_inc(la_ln_in, 1)
            dve.wait_ge(la_ln, 1)
            dve.tensor_tensor(la["f"], la["f"], la["ln2"], ALU.add).then_inc(la_q, 1)
            dve.wait_ge(la_q, 1)
            dve.wait_ge(bias_out, 16)
            linear_attention(la, HG_HEADS, P, [col("hgrn_gate_norm")] * NK)
            out_used()
            add_product(norm_block)
            split_normed("ffn_norm", 0)
            ffn(True, 0, 0)
            add_product(norm_block)

            split_normed("attn_norm", 1)
            dsa = dsa_views()
            copy_product(0, 3584)
            copy_product(1, 2560)
            copy_product(2, 3072)
            copy_product(3, 4096, (P, 2 * IDX_HEADS))
            all_copied()
            for s in (0, 1, 2, 3, 0):
                used[s] += 1
                made[s] += 1
            link(dve.tensor_scalar(dsa["w_scaled"], dsa["w"], IDX_HEADS ** -0.5 * 64 ** -0.5, None, ALU.mult))
            for tb in range(NTB):
                S = (tb + 1) * P
                score = dsa["score"][:, tb, 0:S]
                for hd in range(IDX_HEADS):
                    w = dsa["w_scaled"][:, tb * IDX_HEADS + hd:tb * IDX_HEADS + hd + 1]
                    bank, at = (2 * (1 + hd // 4) + hd % 2, hd // 2 % 2) if tb else (hd % 2, hd // 2)
                    dve.wait_ge(ix_relu, bank + 1)
                    r = dsa["relu"][:, bank, at * S:at * S + S]
                    if hd == 0:
                        dve.tensor_scalar(score, r, w, None, ALU.mult).then_inc(ix_acc, 1)
                    else:
                        dve.wait_ge(ix_acc, tb * IDX_HEADS + hd)
                        dve.scalar_tensor_tensor(score, r, w, score, ALU.mult, ALU.add).then_inc(ix_acc, 1)
            dve.wait_ge(ix_acc, NTB * IDX_HEADS)
            for tb in range(NTB):
                S = (tb + 1) * P
                score = dsa["score"][:, tb, 0:S]
                diag = dsa["score"][:, tb, S - P:S]
                link(dve.tensor_tensor(diag, diag, const[:, CAUSAL:CAUSAL + P], ALU.add))
                rest, src = dsa["rest"][:, 0:S], score
                for _ in range(TOP_K // 8):
                    link(dve.max(top8, src))
                    link(dve.match_replace(rest, top8, src, TAKEN))
                    src = rest
                mask = dsa["mask"][:, tb, 0:S]
                link(dve.tensor_scalar(mask, rest, TAKEN, -NEG_BIG, ALU.is_gt, ALU.mult))
                diag = dsa["mask"][:, tb, S - P:S]
                dve.tensor_tensor(diag, diag, const[:, CAUSAL:CAUSAL + P], ALU.subtract).then_inc(at_mask, 1)
            UNITS = NTB * ATT_HEADS

            def logits(n):
                tb, hd = divmod(n, ATT_HEADS)
                S = (tb + 1) * P
                slot = n % 6
                dve.wait_ge(at_bias, 4 * tb + hd // 4 + 1)
                dve.wait_ge(at_qk, n + 1)
                if n >= 6:
                    dve.wait_ge(at_tr, n - 5)
                bias = bias_x[:, hd, :] if tb else dsa["bias_0"][:, hd, :]
                dve.tensor_tensor_reduce(dsa["a"][:, slot, 0:S], ps[:, AT_BANKS[n % 3], 0:S], bias, 1.0, 3.0e38, ALU.add, ALU.min,
                                         dsa["att_min"][:, n:n + 1]).then_inc(at_max, 1)

            def copy_turned(n):
                S = (n // ATT_HEADS + 1) * P
                dve.wait_ge(at_tr, n + 1)
                if n >= 4:
                    dve.wait_ge(at_pv, n - 3)
                dve.tensor_copy(dsa["pt"][:, n % 4, 0:S], ps[:, 2 + n % 2, 0:S]).then_inc(at_pt, 1)

            def normalise(tb):
                a, z = tb * ATT_HEADS, (tb + 1) * ATT_HEADS
                dve.wait_ge(at_exp, z)
                link(dve.reciprocal(dsa["att_inv"][:, a:z], dsa["att_sum"][:, a:z]))
                dve.wait_ge(at_pv, z)
                dve.tensor_tensor(xn[:, tb, :].rearrange("p (h d) -> p h d", d=64),
                                  flat(4, 2).rearrange("p (h d) -> p h d", d=64),
                                  dsa["att_inv"][:, a:z].unsqueeze(2).broadcast_to([P, ATT_HEADS, 64]), ALU.mult)\
                    .then_inc(xn_ready, 1)

            for n in range(UNITS + 3):
                if n < UNITS:
                    logits(n)
                if n >= 3:
                    copy_turned(n - 3)
                if n == ATT_HEADS + 3:
                    normalise(0)
            normalise(1)
            split_turned([1.0] * NK)
            out_used()
            add_product(norm_block)
            split_normed("ffn_norm", 1)
            ffn(True, 1, 1)
            add_product()

            dve.wait_ge(gain_in, want(gain_in, 16))
            for tb in range(NTB):
                r = inverse_rms(tb)
                dve.scalar_tensor_tensor(h[:, tb, :], h[:, tb, :], r, gain_row, ALU.mult, ALU.mult)\
                    .then_inc(h_ready, 1)
            for l in range(2):
                norm("norm_g_2", l * 6)
                ffn(False, 0, 2 + 2 * l)
                add_normed_product(True)
                norm("norm_g_2", l * 6 + 2)
                if l == 0:
                    hyb = hyb_views()
                    pad = CONV_TAPS - 1
                    dve.memset(hyb["pad"][:, :, 0:pad], 0.0)
                    made[2] += 1
                    made[3] += 1
                    for s in range(2):
                        used[s] += 1
                        made[s] += 1
                        dve.wait_ge(slab_used[s], used[s] + 1)
                        dve.wait_ge(proj_free[2 + s], made[2 + s] + 1)
                        dve.tensor_tensor(hyb["pad"][:, 2 * s:2 * s + 2, pad:pad + SEQ],
                                          ps[:, 4 + s, :].rearrange("p (c t) -> p c t", t=SEQ), hyb["gate"][:, s, :, :], ALU.mult)\
                            .then_inc(proj_free[s], 1)
                    for s in range(2):
                        dve.wait_ge(proj_free[s], made[s] + 1)
                    for s in (2, 3, 0, 1, 2, 3, 0, 1):
                        used[s] += 1
                    for s in (0, 1, 2, 3, 0, 1):
                        made[s] += 1
                    taps = [(k, c) for k in range(CONV_TAPS) for c in range(CONV_CHUNKS)]

                    def convolve(n):
                        for _ in range(n):
                            if not taps:
                                return
                            k, c = taps.pop(0)
                            src, dst, w = hyb["pad"][:, c, k:k + SEQ], hyb["co"][:, c, :], col("conv_dw_w_2", k * 4 + c)
                            if k == 0:
                                dve.tensor_scalar(dst, src, w, col("conv_dw_b_2", c), ALU.mult, ALU.add).then_inc(cv_tap, 1)
                            else:
                                dve.wait_ge(cv_tap, want(cv_tap))
                                dve.scalar_tensor_tensor(dst, src, w, dst, ALU.mult, ALU.add).then_inc(cv_tap, 1)

                    def stick_bound(hd):
                        dve.wait_ge(sb_z, hd + 1)
                        if hd >= 4:
                            dve.wait_ge(sb_sp, hd - 3)
                        dve.tensor_scalar(hyb["l"][:, hd % 4, :], ps[:, hd % 4, 0:3 * P], SOFTPLUS_EDGE, None, ALU.min)\
                            .then_inc(sb_min, 1)

                    def stick_softplus(hd):
                        dve.wait_ge(sb_ln, hd + 1)
                        if hd >= 4:
                            dve.wait_ge(sb_rest, hd - 3)
                        dve.tensor_tensor(hyb["sp"][:, hd % 4, :], ps[:, hd % 4, 0:3 * P], hyb["l"][:, hd % 4, :], ALU.max)\
                            .then_inc(sb_sp, 1)

                    convolve(TAPS_AHEAD)
                    for pair in range(SB_HEADS // 2):
                        for hd in (2 * pair, 2 * pair + 1):
                            stick_bound(hd)
                        convolve(TAPS_BETWEEN)
                        for hd in (2 * pair, 2 * pair + 1):
                            stick_softplus(hd)
                        convolve(TAPS_BETWEEN)
                    assert not taps
                    dve.wait_ge(cv_tap, CONV_CHUNKS * CONV_TAPS)
                    dve.wait_ge(cv_turn, 1)
                    for tb in range(NTB):
                        ins = dve.bn_stats(ln_stats[:, 6 * tb:6 * tb + 6], ps[:, 6 + tb, :])
                    link(ins)
                    for tb in range(NTB):
                        ins = dve.bn_aggr(ln_mv[:, 2 * tb:2 * tb + 2], ln_stats[:, 6 * tb:6 * tb + 6])
                    link(ins)
                    var = ln_mv.rearrange("p (b s) -> p b s", s=2)[:, :, 1]
                    dve.tensor_scalar(var, var, EPS, None, ALU.add).then_inc(cv_ms, 1)
                    dve.wait_ge(cv_std, 1)
                    link(dve.reciprocal(ln_rstd, ln_std))
                    for tb in range(NTB):
                        dve.tensor_scalar(xn[:, tb, 0:512], ps[:, 6 + tb, :], ln_mv[:, 2 * tb:2 * tb + 1], ln_rstd[:, tb:tb + 1],
                                          ALU.subtract, ALU.mult).then_inc(cv_norm, 1)
                    low_of_banks(2)
                    for c in range(4):
                        dve.wait_ge(x_hi_done, want(x_hi_done))
                        dve.tensor_tensor(x_lo[:, 4 + c, :], hyb["cs"][:, c, :], x_hi[:, 4 + c, :].bitcast(F32), ALU.subtract)\
                            .then_inc(x_ready, 1)
                else:
                    la = gla_views()
                    used[2] += 1
                    dve.wait_ge(slab_used[2], used[2] + 1)
                    dve.tensor_copy(la["rank"], ps[0:GATE_RANK, 0, 0:SEQ]).then_inc(gate_rank, 1)
                    for s in range(2):
                        copy_product(s, s * 512, scale=P ** -0.5)
                    dve.wait_ge(gate_ln, 1)
                    link(dve.scalar_tensor_tensor(la["x"], la["x"], 0.0, la["e"], ALU.min, ALU.subtract))
                    link(dve.tensor_scalar(la["x"], la["x"], 1.0 / GLA_TAU, None, ALU.mult))
                    for s in range(2, RING):
                        copy_product(s, s * 512)
                    all_copied()
                    for s in range(RING):
                        used[s] += 2
                        made[s] += 2
                    dve.sem_inc(la_q, 1)
                    linear_attention(la, GLA_HEADS, SLAB, [col("gla_norm_g_2", c % 2) for c in range(NK)])
                out_used()
                add_normed_product(False)
                norm("norm_g_2", l * 6 + 4)
                ffn(False, 0, 3 + 2 * l)
                add_normed_product(True)

        @block.tensor
        def _(pe):
            used, made, want = [0] * RING, [0] * RING, Tally()

            def three(out_ap, a, b, start, stop):
                (a_hi, a_lo), (b_hi, b_lo) = a, b
                pe.matmul(out_ap, a_hi, b_hi, start=start, stop=False, skip_group_check=True)
                pe.matmul(out_ap, a_hi, b_lo, start=False, stop=False, skip_group_check=True)
                return pe.matmul(out_ap, a_lo, b_hi, start=False, stop=stop, skip_group_check=True)

            def weights(s, a, n):
                return w_hi[s][:, a:a + n], w_lo[s][:, a:a + n]

            def acts(k, a=0, n=SEQ):
                return x_hi[:, k, a:a + n], x_lo[:, k, a:a + n]

            def features(s, bank, a, n, at, fresh=None):
                for k in range(NK):
                    if fresh is not None:
                        pe.wait_ge(x_ready, fresh + max(k + 1, 2 * (bank - 4) + 2))
                    ins = three(ps[0:n, bank, at:at + SEQ], weights(s, k * SLAB + a, n), acts(k), k == 0, k == NK - 1)
                return ins

            def tokens(s, bank, a, n, at, blocks=range(NTB)):
                for tb in blocks:
                    for k in range(NK):
                        ins = three(ps[:, bank, at + tb * n:at + tb * n + n], acts(k, tb * P, P), weights(s, k * SLAB + a, n),
                                    k == 0, k == NK - 1)
                return ins

            def feature_slab(s, fresh=None):
                features(s, 4 + s, 0, P, 0, fresh)
                return features(s, 4 + s, P, P, SEQ)

            def token_slab(s):
                return tokens(s, 4 + s, 0, SLAB, 0)

            def project_four(how, n, fresh=None):
                with pe.Fori(0, n) as i:
                    for s in range(RING):
                        pe.wait_ge(slab_ready[s], i + (used[s] + 2))
                        pe.wait_ge(proj_free[s], i + (made[s] + 1))
                        (how(s) if s or fresh is None else how(s, fresh)).then_inc(slab_used[s], 1)
                for s in range(RING):
                    used[s] += n
                    made[s] += n

            def begin(s):
                pe.wait_ge(slab_ready[s], used[s] + 2)
                pe.wait_ge(proj_free[s], made[s] + 1)
                used[s] += 1
                made[s] += 1

            def project(how, s):
                begin(s)
                how(s).then_inc(slab_used[s], 1)

            def half_token_slab(s, tb):
                if tb == 0:
                    begin(s)
                ins = tokens(s, 4 + s, 0, SLAB, 0, [tb])
                if tb == NTB - 1:
                    ins.then_inc(slab_used[s], 1)

            def all_copied():
                for s in range(RING):
                    pe.wait_ge(proj_free[s], made[s] + 1)

            def x_new():
                return want(x_ready, NK) - NK

            def x_split(n=NK):
                pe.wait_ge(x_ready, want(x_ready, n))

            def keep_warm(n):
                z = zeros.bitcast(BF16)
                for _ in range(n):
                    pe.matmul(ps[:, 7, :], z[:, 0:P], z[:, 0:512], start=True, stop=True, skip_group_check=True)

            def turn(src=None):
                for tb in range(NTB):
                    pe.wait_ge(xn_ready, want(xn_ready))
                    for c in range(NK):
                        at = c % 2 * SEQ + tb * P
                        dst = ps[:, 4 + c // 2, at:at + P]
                        if src is None:
                            ins = pe.matmul(dst, h[:, tb, c * P:c * P + P], rms_diag[:, tb, :], start=True, stop=True,
                                            skip_group_check=True)
                        else:
                            ins = pe.transpose(dst, src[:, tb, c * P:c * P + P], ident)
                        if tb == NTB - 1 and c % 2 == 1:
                            ins.then_inc(turned, 1)

            def project_out(fresh=None):
                for s in range(RING):
                    pe.wait_ge(slab_ready[s], used[s] + 2)
                    for tb in range(NTB):
                        for kk in range(2):
                            k = 2 * s + kk
                            if fresh is not None and tb == 0:
                                pe.wait_ge(x_ready, fresh + k + 1)
                            for half in range(2):
                                ins = three(ps[:, 2 * tb + half, :], acts(k, tb * P, P), weights(s, kk * D + half * 512, 512),
                                            k == 0, k == NK - 1)
                        if s == RING - 1 and tb == 0:
                            ins.then_inc(half_done, 1)
                    ins.then_inc(slab_used[s], 1)
                    used[s] += 1

            def ffn(f):
                q0 = f * NF
                z = zeros.bitcast(BF16)
                for bank in range(4):
                    pe.matmul(ps[:, bank, :], z[:, 0:P], z[:, 0:512], start=True, stop=False, skip_group_check=True)

                def up(i, odd, first=False):
                    pe.wait_ge(slab_ready[0], i + (used[0] + 2))
                    fresh = x_new() if first else None
                    for b in range(2):
                        pe.wait_ge(gt_done[b], q0 + 1 if first else i + q0)
                        ins = features(0, 4 + 2 * odd + b, b * P, P, 0, fresh)
                    ins.then_inc(slab_used[0], 1)
                    pe.wait_ge(slab_ready[1], i + (used[1] + 2))
                    features(1, 4 + 2 * odd, 0, P, SEQ).then_inc(up_half, 1)
                    features(1, 5 + 2 * odd, P, P, SEQ).then_inc(slab_used[1], 1)

                def down(s, u, i, last):
                    pe.wait_ge(slab_ready[s], u + 2)
                    pe.wait_ge(g_ready, i * 2 + (2 * q0 + 2))
                    for tb in range(NTB):
                        for b in range(2):
                            for half in range(2):
                                hi, lo = (x_hi, x_lo) if last else (g_hi, g_lo)
                                a = (hi[:, b, tb * P:tb * P + P], lo[:, b, tb * P:tb * P + P])
                                ins = three(ps[:, 2 * tb + half, :], a, weights(s, b * D + half * 512, 512), False, last and b == 1)
                        if last and tb == 0:
                            ins.then_inc(half_done, 1)
                    ins.then_inc(slab_used[s], 1)

                up(0, 0, True)
                with pe.Fori(0, NF // 2) as j:
                    for odd in range(2):
                        up(j * 2 + (odd + 1), 1 - odd)
                        i = j * 2 + odd
                        down(2, i + used[2], i, False)
                down(3, used[3], NF - 1, True)
                used[0] += NF
                used[1] += NF
                used[2] += NF - 1
                used[3] += 1

            def linear_attention(la, H, dv, between):
                def scores(per, n, bank, k, q):
                    out_ap = ps[:, bank + n // per, n % per * (512 // per):(n % per + 1) * (512 // per)]
                    if len(q.shape) == 3:
                        out_ap = out_ap.rearrange("p (n m) -> p n m", m=q.shape[2])
                    ins = pe.matmul(out_ap, k, q, start=True, stop=True, skip_group_check=True)
                    if n % per == per - 1:
                        ins.then_inc(la_scores, 1)

                masked = want(la_masked, 0)
                for n in range(2 * H):
                    scores(4, n, 0, la["k"][:, n * P:n * P + P], la["q"][:, n * P:n * P + P])
                for n, m in enumerate(LEVELS):
                    between(n)
                    pe.wait_ge(la_factors, want(la_factors, 2))
                    pe.wait_ge(la_masked, masked + max(n, 1))
                    for i in range(2 * H):
                        scores(8, i, 2 * (n % 2), la["kt"][:, i * P:i * P + P], halves(la["qt"][:, i * P:i * P + P], m)[1])
                between(len(LEVELS))

                def outputs(tb, within):
                    for hd in range(H):
                        c = hd * dv
                        o = ps[:, 2 * tb + c // 512, c % 512:c % 512 + dv]
                        n = 2 * hd + tb
                        if within:
                            ins = pe.matmul(o, la["scores"][:, n * P:n * P + P], v_of(la, tb, hd, dv),
                                            start=c % 512 == 0, stop=tb == 0,
                                            skip_group_check=True)
                        else:
                            ins = pe.matmul(o, la["cross"][:, hd * P:hd * P + P], v_of(la, 0, hd, dv), start=False, stop=True,
                                            skip_group_check=True)
                    return ins

                pe.wait_ge(la_masked, want(la_masked, 1 + len(LEVELS)))
                outputs(0, True).then_inc(la_out, 1)
                for s in range(H // 4):
                    pe.wait_ge(proj_free[s], made[s] + 1)
                pe.wait_ge(la_factors, want(la_factors, 2))
                for hd in range(H):
                    a = hd * SEQ
                    scores(4, hd, 4, la["kt"][:, a:a + P], la["qt"][:, a + P:a + SEQ])
                outputs(1, True)
                pe.wait_ge(la_cross, want(la_cross))
                outputs(1, False).then_inc(la_out, 1)
                pe.wait_ge(proj_free[3], made[3] + 1)
                keep_warm(WARM_HEADS)

            def turn_rows(n):
                for t in range(-(-n // P)):
                    k = min(P, n - t * P)
                    ins = pe.transpose(ps[:, t // 4, t % 4 * P:t % 4 * P + k], rows[0:k, t, :], ident[0:k, 0:k])
                ins.then_inc(rows_turned, 1)

            pe.wait_ge(zeros_set, 1)
            pe.wait_ge(first_in, 2 * 16)
            turn_rows(n_first)

            keep_warm(8)
            turn()
            project_four(feature_slab, 1, x_new())
            pe.wait_ge(rows_in, 16 * (len(row_src) - 1))
            pe.wait_ge(cols_ready, 1)
            turn_rows(n_rows)
            pe.wait_ge(tables_in, 3 * 16)
            pe.matmul(ps[0:ATT_HEADS, 2, 0:DISTS], rel_bias_sb[0:BUCKETS, :], const[0:BUCKETS, ONEHOT:ONEHOT + DISTS],
                      start=True, stop=True).then_inc(bias_vec_done, 1)
            project_four(feature_slab, 1)
            project_four(token_slab, 1)
            la = hgrn_views()
            pe.wait_ge(la_q, 1)
            pe.wait_ge(la_k, 1)
            linear_attention(la, HG_HEADS, P, lambda n: half_token_slab(n // 2, n % 2))
            turn(xn)
            project_out(x_new())
            keep_warm(WARM)
            turn()
            ffn(0)

            keep_warm(WARM)
            turn()
            fresh = x_new()

            def index_keys_and_values(s):
                features(s, 4 + s, 0, P, 0, fresh)
                return tokens(s, 4 + s, P, P, SEQ)

            project(index_keys_and_values, 0)
            for s in range(1, 3):
                project(feature_slab, s)
            project(lambda s: tokens(s, 4 + s, 0, IDX_HEADS, 0), 3)
            dsa = dsa_views()

            def index_dots(pair):
                tb = min(pair, 1)
                S = (tb + 1) * P
                per = 512 // S
                if pair == 2:
                    pe.wait_ge(ix_relu, 2)
                for i in range(per):
                    for odd in range(2):
                        hd = (max(pair - 1, 0) * per + i) * 2 + odd
                        ins = pe.matmul(ps[:, 2 * pair % 4 + odd, i * S:i * S + S],
                                        dsa["qi"][odd * 64:odd * 64 + 64, hd // 2, tb * P:tb * P + P],
                                        dsa["ki"][odd * 64:odd * 64 + 64, 0:S], start=True, stop=True, skip_group_check=True)
                        if i == per - 1:
                            ins.then_inc(ix_dots, 1)

            copied = list(made)
            project(feature_slab, 0)
            for s in range(RING):
                pe.wait_ge(proj_free[s], copied[s] + 1)
            index_dots(0)
            index_dots(1)
            project(feature_slab, 1)
            index_dots(2)
            for s in (2, 3, 0):
                project(feature_slab, s)
            all_copied()
            pe.wait_ge(ix_relu, 6)
            UNITS = NTB * ATT_HEADS

            def queries_keys(n):
                tb, hd = divmod(n, ATT_HEADS)
                S = (tb + 1) * P
                a = hd % 2 * 64
                if n >= 3:
                    pe.wait_ge(at_max, n - 2)
                pe.matmul(ps[:, AT_BANKS[n % 3], 0:S], dsa["q"][a:a + 64, hd // 2, tb * P:tb * P + P],
                          dsa["k"][a:a + 64, hd // (ATT_HEADS // 2), 0:S], start=True, stop=True, skip_group_check=True)\
                    .then_inc(at_qk, 1)

            def turn_probs(n):
                tb = n // ATT_HEADS
                pe.wait_ge(at_exp, n + 1)
                if n >= 2:
                    pe.wait_ge(at_pt, n - 1)
                for sb_ in range(tb + 1):
                    ins = pe.transpose(ps[:, 2 + n % 2, sb_ * P:sb_ * P + P], dsa["a"][:, n % 6, sb_ * P:sb_ * P + P], ident)
                ins.then_inc(at_tr, 1)

            def values(n):
                tb, hd = divmod(n, ATT_HEADS)
                pe.wait_ge(at_pt, n + 1)
                kv = hd // (ATT_HEADS // 2) * 64
                if n == ATT_HEADS:
                    pe.wait_ge(xn_ready, turned_blocks + 1)
                o = ps[:, 4 + hd // 8, hd % 8 * 64:hd % 8 * 64 + 64]
                for sb_ in range(tb + 1):
                    ins = pe.matmul(o, dsa["pt"][:, n % 4, sb_ * P:sb_ * P + P], dsa["v"][:, sb_, kv:kv + 64],
                                    start=sb_ == 0, stop=sb_ == tb, skip_group_check=True)
                ins.then_inc(at_pv, 1)

            turned_blocks = want(xn_ready, 0)
            keep_warm(8)
            for n in range(UNITS + 4):
                keep_warm(1)
                if n < UNITS:
                    queries_keys(n)
                if 2 <= n < UNITS + 2:
                    turn_probs(n - 2)
                if n >= 4:
                    values(n - 4)
            pe.wait_ge(xn_ready, turned_blocks + NTB)
            turn(xn)
            project_out(x_new())
            keep_warm(WARM)
            turn()
            ffn(1)

            for l in range(2):
                keep_warm(WARM_NORMED)
                turn()
                ffn(2 + 2 * l)
                keep_warm(WARM_NORMED)
                turn()
                if l == 0:
                    hyb = hyb_views()
                    project_four(feature_slab, 1, x_new())
                    project_four(feature_slab, 1)
                    project(token_slab, 0)
                    for s in (2, 3):
                        pe.wait_ge(proj_free[s], made[s] + 1)

                    def stick_logits(hd):
                        a, c = hd % 2 * 64, hd // 2
                        q, k = hyb["q"][a:a + 64, c, :], hyb["k"][a:a + 64, c, :]
                        bank = ps[:, hd % 4, :]
                        if hd >= 4:
                            pe.wait_ge(sb_w, hd - 3)
                        pe.matmul(bank[:, 0:SEQ], k[:, 0:P], q, start=True, stop=False, skip_group_check=True)
                        pe.matmul(bank[:, SEQ:SEQ + P], k[:, P:SEQ], q[:, P:SEQ], start=False, stop=False, skip_group_check=True)
                        for c0 in (0, SEQ):
                            ins = pe.matmul(bank[:, c0:c0 + P], ident, const[:, STRICT:STRICT + P], start=False, stop=False,
                                            skip_group_check=True)
                        ins.then_inc(sb_z, 1)

                    def stick_rest(hd):
                        pe.wait_ge(sb_sp, hd + 1)
                        bank, sp_ = ps[:, hd % 4, :], hyb["sp"][:, hd % 4, :]
                        tri, minus = const[:, TRI:TRI + P], const[:, ONES:ONES + P]
                        pe.matmul(bank[:, 0:SEQ], tri, sp_[:, 0:SEQ], start=False, stop=False, skip_group_check=True)
                        pe.matmul(bank[:, P:SEQ], minus, sp_[:, SEQ:3 * P], start=False, stop=False, skip_group_check=True)
                        pe.matmul(bank[:, SEQ:3 * P], tri, sp_[:, SEQ:3 * P], start=False, stop=True, skip_group_check=True)\
                            .then_inc(sb_rest, 1)

                    def stick_values(hd):
                        pe.wait_ge(sb_w, hd + 1)
                        a, c = hd % 2 * 64, hd // 2
                        w = hyb["w"][:, hd % 4, :]
                        o = ps[a:a + 64, 4 + c // 2, c % 2 * SEQ:c % 2 * SEQ + SEQ]
                        v0, v1 = v_of(hyb, 0, hd, 64), v_of(hyb, 1, hd, 64)
                        pe.matmul(o[:, 0:P], v0, w[:, 0:P], start=True, stop=True, skip_group_check=True)
                        pe.matmul(o[:, P:SEQ], v0, w[:, P:SEQ], start=True, stop=False, skip_group_check=True)
                        pe.matmul(o[:, P:SEQ], v1, w[:, SEQ:3 * P], start=False, stop=True, skip_group_check=True)\
                            .then_inc(sb_pv, 1)

                    def conv_turned():
                        pe.wait_ge(cv_tap, CONV_CHUNKS * CONV_TAPS)
                        for tb in range(NTB):
                            for c in range(4):
                                ins = pe.transpose(ps[:, 6 + tb, c * P:c * P + P], hyb["co"][:, c, tb * P:tb * P + P], ident)
                        ins.then_inc(cv_turn, 1)

                    for step in range(SB_HEADS // 2 + 2):
                        if step < SB_HEADS // 2:
                            stick_logits(2 * step)
                            stick_logits(2 * step + 1)
                        if step == 0:
                            project(token_slab, 1)
                        elif step < SB_HEADS // 2:
                            keep_warm(WARM_STEP)
                        if step == 2:
                            all_copied()
                        if step == SB_HEADS // 2:
                            conv_turned()
                        if 1 <= step < SB_HEADS // 2 + 1:
                            stick_rest(2 * step - 2)
                            stick_rest(2 * step - 1)
                        if step >= 2:
                            stick_values(2 * step - 4)
                            stick_values(2 * step - 3)
                    pe.wait_ge(cv_norm, NTB)
                    for c in range(4):
                        for tb in range(NTB):
                            at = c % 2 * SEQ + tb * P
                            ins = pe.transpose(ps[:, 6 + c // 2, at:at + P], xn[:, tb, c * P:c * P + P], ident)
                        if c % 2 == 1:
                            ins.then_inc(cv_back, 1)
                    x_split(6)
                else:
                    la = gla_views()
                    pe.wait_ge(slab_ready[2], used[2] + 2)
                    features(2, 0, 0, GATE_RANK, 0, x_new()).then_inc(slab_used[2], 1)
                    used[2] += 1
                    project(feature_slab, 0)
                    pe.wait_ge(gate_in, 16)
                    pe.wait_ge(gate_rank, 1)
                    for c in range(4):
                        ins = pe.matmul(ps[:, 1 + c // 2, c % 2 * SEQ:c % 2 * SEQ + SEQ], w_gate[0:GATE_RANK, c * P:c * P + P],
                                        la["rank"], start=True, stop=True, skip_group_check=True)
                    ins.then_inc(gate_mm, 1)
                    for s in range(1, RING):
                        project(feature_slab, s)
                    pe.wait_ge(gate_x, 1)
                    pe.wait_ge(la_q, 2)

                    def values_and_gates(n):
                        for tb in range(NTB):
                            half_token_slab(n % RING, tb)

                    linear_attention(la, GLA_HEADS, SLAB, values_and_gates)
                    turn(xn)
                    fresh = x_new()
                project_out(fresh if l else None)
                keep_warm(WARM_NORMED)
                turn()
                ffn(3 + 2 * l)


_INS = ["x", "attn_norm", "ffn_norm", "hgrn_w_in", "hgrn_w_out", "hgrn_gate_norm", "hgrn_lower_bounds", "dsa_w_in",
        "dsa_w_out", "rel_bias", "ffn_w_up", "ffn_conv_w", "ffn_conv_b", "ffn_w_down", "final_norm", "norm_g_2",
        "ffn1_w_in_2", "ffn1_w_out_2", "ffn2_w_in_2", "ffn2_w_out_2", "hyb_w_in_2", "hyb_w_out_2", "conv_dw_w_2",
        "conv_dw_b_2", "conv_ln_g_2", "conv_ln_b_2", "gla_w_in_2", "gla_w_gate_2", "gla_b_gate_2", "gla_norm_g_2",
        "gla_w_out_2"]


def kernel(**inputs):
    import concourse.bacc as bacc
    from concourse.bass_utils import run_bass_kernel_spmd as run

    nc = bacc.Bacc("TRN2", target_bir_lowering=False, num_devices=1)
    shape_const, level_masks = shape_constants()
    arrays = {name: np.ascontiguousarray(inputs[name]) for name in _INS}
    arrays["shape_const"] = shape_const
    arrays["level_masks"] = level_masks
    A = {name: nc.dram_tensor("in_" + name, a.shape, mybir.dt.from_np(a.dtype), kind="ExternalInput").ap()
         for name, a in arrays.items()}
    out = nc.dram_tensor("out_0", (1, SEQ, D), F32, kind="ExternalOutput").ap()
    build(nc, A, out)
    r = run(nc, [{"in_" + name: a for name, a in arrays.items()}], core_ids=[0])
    return r.results[0]["out_0"]
```
